# Optimizing a Trainium2 kernel written in Bass

```python
import jax, jax.numpy as jnp
from jax import lax
import numpy as np

D_MODEL = 2048
BATCH = 1
SEQ = 1024
DEPTH = 1
DEC_BATCH = 1
DEC_SEQ = 32
PAST_LEN = 256

CHUNK = 64
GDN_HEADS = 8
GDN_DK = 128
GDN_DV = 128
GDN_KEY_DIM = GDN_HEADS * GDN_DK
GDN_VAL_DIM = GDN_HEADS * GDN_DV
GDN_QKV_DIM = 2 * GDN_KEY_DIM + GDN_VAL_DIM
CONV_W = 4
GDN_CHUNK = 64
MLA_HEADS = 8
Q_LORA = 512
KV_LORA = 512
NOPE_DIM = 128
ROPE_DIM = 64
V_DIM = 128
MLA_WIDTH = MLA_HEADS * V_DIM
ROPE_THETA = 10000.0
Q_BLOCK = 128
MIX_WIDTH = GDN_VAL_DIM + MLA_WIDTH
IN_SIZES = (GDN_QKV_DIM, GDN_VAL_DIM, GDN_HEADS, GDN_HEADS, Q_LORA, KV_LORA, ROPE_DIM, MLA_WIDTH)
IN_DIM = GDN_QKV_DIM + GDN_VAL_DIM + 2 * GDN_HEADS + Q_LORA + KV_LORA + ROPE_DIM + MLA_WIDTH
EPS = 1e-6

kernel_name = 'hymba_gdn_mla_streaming_step'

def rmsnorm(x, w):
    xf = x.astype(jnp.float32)
    y = xf * lax.rsqrt(jnp.mean(xf * xf, axis=-1, keepdims=True) + EPS)
    return (y * w.astype(jnp.float32)).astype(x.dtype)

def l2norm(x):
    xf = x.astype(jnp.float32)
    return xf * lax.rsqrt(jnp.sum(xf * xf, axis=-1, keepdims=True) + EPS)

def rope_tables(pos):
    inv = ROPE_THETA ** (-jnp.arange(0, ROPE_DIM, 2, dtype=jnp.float32) / ROPE_DIM)
    ang = pos.astype(jnp.float32)[:, None] * inv[None, :]
    return jnp.cos(ang), jnp.sin(ang)

def apply_rope(x, cos, sin):
    xf = x.astype(jnp.float32)
    extra = x.ndim - 3
    c = cos.reshape((cos.shape[0],) + (1,) * extra + (cos.shape[1],))
    s = sin.reshape((sin.shape[0],) + (1,) * extra + (sin.shape[1],))
    half = ROPE_DIM // 2
    x1, x2 = xf[..., :half], xf[..., half:]
    return jnp.concatenate([x1 * c - x2 * s, x2 * c + x1 * s], axis=-1).astype(x.dtype)

def causal_short_conv(x, buf, w):
    t = x.shape[1]
    xp = jnp.concatenate([buf.astype(x.dtype), x], axis=1)
    y = xp[:, 0:t] * w[0]
    for i in range(1, CONV_W):
        y = y + xp[:, i:i + t] * w[i]
    return jax.nn.silu(y), xp[:, -(CONV_W - 1):]

def gated_delta_rule(q, k, v, g, beta, s0):
    b, h, t, _ = q.shape
    c = GDN_CHUNK
    pad = (-t) % c
    n = (t + pad) // c

    def blocks(a):
        a = jnp.pad(a, [(0, 0), (0, 0), (0, pad)] + [(0, 0)] * (a.ndim - 3))
        return a.reshape(b, h, n, c, *a.shape[3:])

    q = blocks(q * (GDN_DK ** -0.5))
    k = blocks(k)
    v = blocks(v)
    beta = blocks(beta)
    g = jnp.cumsum(blocks(g), axis=-1)
    incl = jnp.tril(jnp.ones((c, c), dtype=bool))
    strict = jnp.tril(jnp.ones((c, c), dtype=bool), -1)
    decay = jnp.exp(jnp.where(incl, g[..., :, None] - g[..., None, :], -jnp.inf))
    k_beta = k * beta[..., None]
    lmat = jnp.where(strict, jnp.einsum('bhnid,bhnjd->bhnij', k_beta, k) * decay, 0.0)
    eye = jnp.eye(c, dtype=q.dtype)
    tmat = lax.linalg.triangular_solve(lmat + eye, jnp.broadcast_to(eye, lmat.shape),
                                       left_side=True, lower=True)
    u = jnp.einsum('bhnij,bhnjv->bhniv', tmat, v * beta[..., None])
    w = jnp.einsum('bhnij,bhnjd->bhnid', tmat, k_beta * jnp.exp(g)[..., None])
    attn = jnp.einsum('bhnid,bhnjd->bhnij', q, k) * decay

    def step(s, xs):
        q_c, k_c, u_c, w_c, g_c, a_c = xs
        v_new = u_c - jnp.einsum('bhid,bhdv->bhiv', w_c, s)
        o_c = (jnp.einsum('bhid,bhdv->bhiv', q_c * jnp.exp(g_c)[..., None], s)
               + jnp.einsum('bhij,bhjv->bhiv', a_c, v_new))
        g_last = g_c[..., -1]
        k_dec = k_c * jnp.exp(g_last[..., None] - g_c)[..., None]
        s = s * jnp.exp(g_last)[..., None, None] + jnp.einsum('bhid,bhiv->bhdv', k_dec, v_new)
        return s, o_c

    xs = tuple(jnp.moveaxis(a, 2, 0) for a in (q, k, u, w, g, attn))
    s, o = lax.scan(step, s0, xs)
    o = jnp.moveaxis(o, 0, 2).reshape(b, h, n * c, GDN_DV)[:, :, :t]
    return o, s

def mla_attend(q_lat, q_rope, q_pos, c_kv, k_rope, k_pos):
    b, t, h, r = q_lat.shape
    qb = min(Q_BLOCK, t)
    nb = t // qb
    scale = (NOPE_DIM + ROPE_DIM) ** -0.5

    def block(args):
        ql, qr, qp = args
        s = (jnp.einsum('bqhr,bkr->bhqk', ql, c_kv)
             + jnp.einsum('bqhd,bkd->bhqk', qr, k_rope)).astype(jnp.float32) * scale
        visible = k_pos[None, :] < ((qp // CHUNK) + 1)[:, None] * CHUNK
        s = jnp.where(visible[None, None], s, -jnp.inf)
        p = jax.nn.softmax(s, axis=-1).astype(c_kv.dtype)
        return jnp.einsum('bhqk,bkr->bqhr', p, c_kv)

    ql = jnp.moveaxis(q_lat.reshape(b, nb, qb, h, r), 1, 0)
    qr = jnp.moveaxis(q_rope.reshape(b, nb, qb, h, ROPE_DIM), 1, 0)
    qp = q_pos.reshape(nb, qb)
    out = lax.map(block, (ql, qr, qp))
    return jnp.moveaxis(out, 0, 1).reshape(b, t, h, r)

def mixer_layer(x, conv_buf, ssm0, past_lat, past_krope,
                ln_in_w, w_in, w_conv, a_log, dt_bias, gdn_norm_w,
                q_norm_w, w_q_up, kv_norm_w, w_uk, w_uv, w_out):
    b, t, _ = x.shape
    hproj = rmsnorm(x, ln_in_w) @ w_in
    points, acc = [], 0
    for size in IN_SIZES[:-1]:
        acc += size
        points.append(acc)
    qkv, z_g, b_g, a_g, cq, ckv, kr, z_m = jnp.split(hproj, points, axis=-1)

    qkv, new_conv = causal_short_conv(qkv, conv_buf, w_conv)
    q, k, v = jnp.split(qkv, [GDN_KEY_DIM, 2 * GDN_KEY_DIM], axis=-1)
    q = l2norm(q.reshape(b, t, GDN_HEADS, GDN_DK))
    k = l2norm(k.reshape(b, t, GDN_HEADS, GDN_DK))
    v = v.reshape(b, t, GDN_HEADS, GDN_DV).astype(jnp.float32)
    beta = jax.nn.sigmoid(b_g.astype(jnp.float32))
    g = -jnp.exp(a_log.astype(jnp.float32)) * jax.nn.softplus(
        a_g.astype(jnp.float32) + dt_bias.astype(jnp.float32))
    o_g, new_ssm = gated_delta_rule(q.transpose(0, 2, 1, 3), k.transpose(0, 2, 1, 3),
                                    v.transpose(0, 2, 1, 3), g.transpose(0, 2, 1),
                                    beta.transpose(0, 2, 1), ssm0.astype(jnp.float32))
    o_g = rmsnorm(o_g.transpose(0, 2, 1, 3), gdn_norm_w).reshape(b, t, GDN_VAL_DIM).astype(x.dtype)
    o_g = o_g * jax.nn.silu(z_g)

    p_len = past_lat.shape[1]
    q_pos = jnp.arange(p_len, p_len + t, dtype=jnp.int32)
    k_pos = jnp.arange(p_len + t, dtype=jnp.int32)
    cos, sin = rope_tables(q_pos)
    qm = jnp.einsum('btr,rhd->bthd', rmsnorm(cq, q_norm_w), w_q_up)
    q_nope, q_rope = qm[..., :NOPE_DIM], apply_rope(qm[..., NOPE_DIM:], cos, sin)
    c_kv = rmsnorm(ckv, kv_norm_w)
    k_rope = apply_rope(kr, cos, sin)
    q_lat = jnp.einsum('bthd,rhd->bthr', q_nope, w_uk)
    o_lat = mla_attend(q_lat, q_rope, q_pos,
                       jnp.concatenate([past_lat.astype(c_kv.dtype), c_kv], axis=1),
                       jnp.concatenate([past_krope.astype(k_rope.dtype), k_rope], axis=1), k_pos)
    o_m = jnp.einsum('bthr,rhv->bthv', o_lat, w_uv).reshape(b, t, MLA_WIDTH) * jax.nn.silu(z_m)

    y = x + jnp.concatenate([o_g, o_m], axis=-1) @ w_out
    return y, new_conv, new_ssm.astype(ssm0.dtype), c_kv, k_rope

def setup_inputs(seed: int = 0) -> dict:
    key = jax.random.key(seed)
    ks = jax.random.split(key, 24)
    f32 = jnp.float32
    nrm = lambda k, shape, s: jax.random.normal(k, shape, f32) * s
    gain = lambda k, shape: 1.0 + 0.01 * jax.random.normal(k, shape, f32)
    dt = jnp.exp(jax.random.uniform(ks[6], (DEPTH, GDN_HEADS), f32, np.log(1e-3), np.log(1e-1)))
    return {
        'x_prompt': nrm(ks[0], (BATCH, SEQ, D_MODEL), 1.0),
        'x_sample': nrm(ks[1], (DEC_BATCH, DEC_SEQ, D_MODEL), 1.0),
        'cache_mla_latent': nrm(ks[2], (DEPTH, DEC_BATCH, PAST_LEN, KV_LORA), 1.0),
        'cache_mla_krope': nrm(ks[3], (DEPTH, DEC_BATCH, PAST_LEN, ROPE_DIM), 1.0),
        'state_gdn_conv': nrm(ks[4], (DEPTH, DEC_BATCH, CONV_W - 1, GDN_QKV_DIM), 1.0),
        'state_gdn_ssm': nrm(ks[5], (DEPTH, DEC_BATCH, GDN_HEADS, GDN_DK, GDN_DV), 0.1),
        'ln_in_w': gain(ks[7], (DEPTH, D_MODEL)),
        'w_in': nrm(ks[8], (DEPTH, D_MODEL, IN_DIM), D_MODEL ** -0.5),
        'w_conv': nrm(ks[9], (DEPTH, CONV_W, GDN_QKV_DIM), CONV_W ** -0.5),
        'a_log': jnp.log(jax.random.uniform(ks[10], (DEPTH, GDN_HEADS), f32, 1.0, 16.0)),
        'dt_bias': dt + jnp.log(-jnp.expm1(-dt)),
        'gdn_norm_w': gain(ks[11], (DEPTH, GDN_DV)),
        'q_norm_w': gain(ks[12], (DEPTH, Q_LORA)),
        'w_q_up': nrm(ks[13], (DEPTH, Q_LORA, MLA_HEADS, NOPE_DIM + ROPE_DIM), Q_LORA ** -0.5),
        'kv_norm_w': gain(ks[14], (DEPTH, KV_LORA)),
        'w_uk': nrm(ks[15], (DEPTH, KV_LORA, MLA_HEADS, NOPE_DIM), KV_LORA ** -0.5),
        'w_uv': nrm(ks[16], (DEPTH, KV_LORA, MLA_HEADS, V_DIM), KV_LORA ** -0.5),
        'w_out': nrm(ks[17], (DEPTH, MIX_WIDTH, D_MODEL), MIX_WIDTH ** -0.5),
        'ln_final_w': gain(ks[18], (D_MODEL,)),
    }

def reference(x_prompt, x_sample, cache_mla_latent, cache_mla_krope, state_gdn_conv, state_gdn_ssm,
              ln_in_w, w_in, w_conv, a_log, dt_bias, gdn_norm_w, q_norm_w, w_q_up, kv_norm_w,
              w_uk, w_uv, w_out, ln_final_w):
    hp, hs = x_prompt, x_sample
    bp = x_prompt.shape[0]
    conv_p, ssm_p, lat_p, kr_p = [], [], [], []
    conv_s, ssm_s, lat_s, kr_s = [], [], [], []
    for l in range(DEPTH):
        lw = (ln_in_w[l], w_in[l], w_conv[l], a_log[l], dt_bias[l], gdn_norm_w[l],
              q_norm_w[l], w_q_up[l], kv_norm_w[l], w_uk[l], w_uv[l], w_out[l])
        hp, c1, s1, l1, r1 = mixer_layer(
            hp, jnp.zeros((bp, CONV_W - 1, GDN_QKV_DIM), hp.dtype),
            jnp.zeros((bp, GDN_HEADS, GDN_DK, GDN_DV), hp.dtype),
            jnp.zeros((bp, 0, KV_LORA), hp.dtype), jnp.zeros((bp, 0, ROPE_DIM), hp.dtype), *lw)
        hs, c2, s2, l2, r2 = mixer_layer(
            hs, state_gdn_conv[l], state_gdn_ssm[l], cache_mla_latent[l], cache_mla_krope[l], *lw)
        conv_p.append(c1); ssm_p.append(s1); lat_p.append(l1); kr_p.append(r1)
        conv_s.append(c2); ssm_s.append(s2); lat_s.append(l2); kr_s.append(r2)
    y_prompt = rmsnorm(hp, ln_final_w)
    y_sample = rmsnorm(hs, ln_final_w)
    return (y_prompt, y_sample,
            jnp.stack(conv_p), jnp.stack(ssm_p), jnp.stack(lat_p), jnp.stack(kr_p),
            jnp.stack(conv_s), jnp.stack(ssm_s), jnp.stack(lat_s), jnp.stack(kr_s))


_drawn_inputs = setup_inputs


def setup_inputs(seed=0):
    import zlib

    import numpy as np

    out = dict(_drawn_inputs(seed))
    spreads = {}
    factors = {'cache_mla_krope': 2.972,
     'ln_in_w': 10.653,
     'gdn_norm_w': 200.0,
     'q_norm_w': 63.009,
     'kv_norm_w': 35.843,
     'ln_final_w': 183.529,
     'cache_mla_latent': 8.0}
    for name, (base, spread) in spreads.items():
        noise = np.random.default_rng([zlib.crc32(name.encode()), seed]).standard_normal(out[name].shape)
        drawn = base * np.exp(spread * noise) if base else spread * noise
        out[name] = __import__('jax').numpy.asarray(drawn.astype(out[name].dtype))
    for name, factor in factors.items():
        out[name] = (out[name] * factor).astype(out[name].dtype)
    return out
```

```python
import concourse.bass as bass
from concourse import mybir
from concourse.alu_op_type import AluOpType as ALU
from contextlib import ExitStack

F32 = mybir.dt.float32
F32R = mybir.dt.float32r
ACT = mybir.ActivationFunctionType
AX = mybir.AxisListType

P = 128
D_MODEL = 2048
SEQ = 1024
DEC = 32
PAST = 256
T = SEQ + DEC
EPS = 1e-6
HEADS = 8
CONV_W = 4
QKV = 3 * HEADS * P
LORA = 512
ROPE = 64
KT = D_MODEL // P
PROMPT_TILES = SEQ // P
TOKEN_TILES = PROMPT_TILES + 1
NCHUNK = 3
NW = T // NCHUNK
QKV_TILES = QKV // P
Z_G0 = QKV
BA0 = Z_G0 + HEADS * P
CQ0 = BA0 + 2 * HEADS
CKV0 = CQ0 + LORA
KR0 = CKV0 + LORA
Z_M0 = KR0 + ROPE
BAKR = ROPE + 2 * HEADS
C_TILES = LORA // P
PRE = CONV_W - 1
ROW = PRE + SEQ + PRE + DEC
CONV = ROW - PRE
SAMPLE_AT = SEQ + PRE
R_CONV, R_LN, R_QN, R_KVN, R_GN = 0, 96, 112, 116, 120
PARAMS = 121


class Space:

    def __init__(self, nc, ctx, tag):
        self.nc, self.ctx, self.tag = nc, ctx, tag

    def sb(self, name, shape, dt=F32):
        return self.ctx.enter_context(self.nc.sbuf_tensor(f"{self.tag}_{name}", shape, dt))

    def ps(self, name, shape):
        return self.ctx.enter_context(self.nc.psum_tensor(f"{self.tag}_{name}", shape, F32))

    def sem(self, name):
        return self.ctx.enter_context(self.nc.semaphore(f"{self.tag}_{name}"))


def normalise_inputs(nc, a, hn_hi, hn_lo, cols, ident):
    with ExitStack() as ctx:
        s = Space(nc, ctx, "norm")
        x = s.sb("x", [P, 2, D_MODEL])
        xs = s.sb("xs", [P, 2, D_MODEL])
        sq = s.sb("sq", [P, D_MODEL])
        ss = s.sb("ss", [P, 2])
        var = s.sb("var", [P, 2])
        rstd = s.sb("rstd", [P, 2])
        mhalf = s.sb("mhalf", [P, 1])
        hn = s.sb("hn", [P, 4, 4 * P])
        rows = s.sb("rows", [P, 2, P])
        pt = [s.ps(f"pt{i}", [P, 512]) for i in range(8)]
        rows_in, x_free, squared, var_ready, rstd_ready, scaled = (
            s.sem(n) for n in ("rows_in", "x_free", "squared", "var_ready", "rstd_ready", "scaled"))
        x_in = [s.sem(f"x_in{u}") for u in range(2)]
        quarter_T, weighted, hi_ready, lo_ready, params_T, params_in, consts = (
            s.sem(n) for n in ("quarter_T", "weighted", "hi_ready", "lo_ready", "params_T", "params_in", "consts"))
        block = ctx.enter_context(nc.Block())

        @block.sync
        def _(sp):
            loads = [(ident[:], a["ident"]),
                     (rows[R_CONV:R_LN, 0], a["w_conv"].rearrange("d i (j p) -> (d i j) p", p=P)),
                     (rows[R_LN:R_QN, 0], a["ln_in_w"].rearrange("d (j p) -> (d j) p", p=P)),
                     (rows[R_QN:R_KVN, 0], a["q_norm_w"].rearrange("d (j p) -> (d j) p", p=P)),
                     (rows[R_KVN:R_GN, 0], a["kv_norm_w"].rearrange("d (j p) -> (d j) p", p=P)),
                     (rows[R_GN:PARAMS, 0], a["gdn_norm_w"]),
                     (rows[0:PRE * QKV_TILES, 1], a["state_gdn_conv"].rearrange("d b i (j p) -> (d b i j) p", p=P))]
            for dst, src in loads:
                sp.dma_start(dst, src).then_inc(rows_in, 16)
            with sp.Fori(0, PROMPT_TILES // 2) as i:
                for u in range(2):
                    t = sp.snap(2 * i + u)
                    sp.wait_ge(x_free, t + 1)
                    sp.dma_start(x[:, u], a["x_prompt"][0, bass.ts(t, P), :]).then_inc(x_in[u], 16)
            sp.wait_ge(x_free, PROMPT_TILES + 1)
            sp.dma_start(x[0:DEC, 0], a["x_sample"][0]).then_inc(x_in[0], 16)

        @block.gpsimd
        def _(pool):
            pool.memset(mhalf[:], -0.5).then_inc(consts, 1)
            pool.wait_ge(consts, 1)

            def tile(t, u, n):
                pool.wait_ge(var_ready, t + 1)
                pool.tensor_tensor(rstd[0:n, u:u + 1], var[0:n, u:u + 1], mhalf[0:n], ALU.pow).then_inc(rstd_ready, 1)

            with pool.Fori(0, PROMPT_TILES // 2) as i:
                for u in range(2):
                    tile(2 * i + u, u, P)
            tile(PROMPT_TILES, 0, DEC)

        @block.scalar
        def _(act):
            act.sem_inc(x_free, 2)
            act.wait_ge(params_T, 1)
            act.copy(cols[:, 0, 0:PARAMS], pt[0][:, 0:PARAMS])
            act.copy(cols[:, 1, 0:PRE * QKV_TILES], pt[1][:, 0:PRE * QKV_TILES]).then_inc(params_in, 1)

            def tile(t, u, x_arrived, n):
                act.wait_ge(x_in[u], x_arrived)
                act.wait_ge(scaled, t + 1)
                act.activation(sq[0:n], x[0:n, u], ACT.Square, accum_out=ss[0:n, u:u + 1]).then_inc(squared, 1)
                act.wait_ge(rstd_ready, t + 1)
                act.wait_ge(quarter_T, 4 * t + 4)
                act.activation(xs[0:n, u], x[0:n, u], ACT.Copy, scale=rstd[0:n, u:u + 1]).then_inc(scaled, 1)
                act.wait_ge(scaled, t + 2)
                act.sem_inc(x_free, 1)
                for q in range(4):
                    act.wait_ge(weighted, 4 * t + q + 9)
                    act.copy(hn_hi[:, 4 * q:4 * q + 4, bass.ds(P * t, n)],
                             hn[:, q, :].rearrange("p (k n) -> p k n", k=4)[:, :, 0:n]).then_inc(hi_ready, 1)

            act.sem_inc(scaled, 1)
            with act.Fori(0, PROMPT_TILES // 2) as i:
                for u in range(2):
                    tile(2 * i + u, u, 16 * i + 16, P)
            tile(PROMPT_TILES, 0, 16 * (PROMPT_TILES // 2 + 1), DEC)

        @block.vector
        def _(dve):
            dve.wait_ge(params_in, 1)

            def tile(t, u, n):
                dve.wait_ge(squared, t + 1)
                dve.tensor_scalar(var[0:n, u:u + 1], ss[0:n, u:u + 1], 1.0 / D_MODEL, EPS, ALU.mult, ALU.add).then_inc(var_ready, 1)
                for q in range(4):
                    dve.wait_ge(quarter_T, 4 * t + q + 9)
                    dve.wait_ge(lo_ready, 4 * t + q + 1)
                    view = hn[:, q, :].rearrange("p (k n) -> p k n", k=4)[:, :, 0:n]
                    w = cols[:, 0, R_LN + 4 * q:R_LN + 4 * q + 4]
                    dve.tensor_tensor(view, pt[4 * u + q][:, :].rearrange("p (k n) -> p k n", k=4)[:, :, 0:n],
                                      w[:, :, None].to_broadcast([P, 4, n]), ALU.mult).then_inc(weighted, 1)
                for q in range(4):
                    dve.wait_ge(hi_ready, 4 * t + q + 1)
                    view = hn[:, q, :].rearrange("p (k n) -> p k n", k=4)[:, :, 0:n]
                    cut = (slice(None), slice(4 * q, 4 * q + 4), bass.ds(P * t, n))
                    dve.tensor_tensor(hn_lo[cut], view, hn_hi[cut].bitcast(F32), ALU.subtract).then_inc(lo_ready, 1)

            dve.sem_inc(lo_ready, 4)
            dve.sem_inc(weighted, 8)
            with dve.Fori(0, PROMPT_TILES // 2) as i:
                for u in range(2):
                    tile(2 * i + u, u, P)
            tile(PROMPT_TILES, 0, DEC)

        @block.tensor
        def _(pe):
            pe.wait_ge(rows_in, 16 * 7)
            pe.transpose(pt[0][:, 0:PARAMS], rows[0:PARAMS, 0], ident[0:PARAMS, 0:PARAMS])
            pe.transpose(pt[1][:, 0:PRE * QKV_TILES], rows[0:PRE * QKV_TILES, 1],
                         ident[0:PRE * QKV_TILES, 0:PRE * QKV_TILES]).then_inc(params_T, 1)
            pe.wait_ge(params_in, 1)
            pe.sem_inc(quarter_T, 8)

            def tile(t, u, n):
                pe.wait_ge(scaled, t + 2)
                for q in range(4):
                    for k in range(4):
                        if k == 0:
                            pe.wait_ge(weighted, 4 * t + q + 1)
                        last = pe.transpose(pt[4 * u + q][:, P * k:P * k + n], xs[0:n, u, P * (4 * q + k):P * (4 * q + k + 1)],
                                            ident[0:n, 0:n])
                    last.then_inc(quarter_T, 1)

            with pe.Fori(0, PROMPT_TILES // 2) as i:
                for u in range(2):
                    tile(2 * i + u, u, P)
            tile(PROMPT_TILES, 0, DEC)


def project(nc, a, d, hn_hi, hn_lo, cols, ident, out):
    PAIRS = [(QKV_TILES // 2, "qkv"), (HEADS, "gate"), (C_TILES, "latent")]
    TILES = 2 * sum(n for n, _ in PAIRS) + 1

    def each_tile(eng, body):
        first = 1
        for g, (pairs, kind) in enumerate(PAIRS):
            peeled = g == len(PAIRS) - 1
            with eng.Fori(0, pairs - peeled) as i:
                for u in range(2):
                    body(kind, i, u, eng.snap(2 * i + (first + u)), (first + u) % 2)
            if peeled:
                for u in range(2):
                    body(kind, pairs - 1, u, 2 * (pairs - 1) + first + u, (first + u) % 2)
            first += 2 * pairs

    def stores(kind, i, u):
        first = {"qkv": 0, "gate": QKV_TILES, "latent": QKV_TILES + 2 * HEADS}[kind]
        return 16 * i + (16 + 16 * ((first + 1 + u) // 2))

    def column(kind, i, u):
        return {"qkv": (2 * i + u) * P,
                "gate": (Z_M0 if u else Z_G0) + i * P,
                "latent": (CKV0 if u else CQ0) + i * P}[kind]

    with ExitStack() as ctx:
        s = Space(nc, ctx, "proj")
        w_raw = s.sb("w_raw", [P, KT, P])
        w_hi = s.sb("w_hi", [P, 2, KT, P], F32R)
        w_lo = s.sb("w_lo", [P, 2, KT, P], F32R)
        pre = s.sb("pre", [P, 2, ROW])
        act_out = s.sb("act_out", [P, 2, CONV])
        tails = s.sb("tails", [P, 2, PRE, QKV_TILES])
        tail_rows = s.sb("tail_rows", [PRE * QKV_TILES, 2, P])
        acc = [[s.ps(f"acc{u}{c}", [P, 512]) for c in range(NCHUNK)] for u in range(2)]
        tailT = s.ps("tailT", [P, 512])
        w_loaded, ba_loaded, hi_ready, lo_ready, chunk_done, evacuated = (
            s.sem(n) for n in ("w_loaded", "ba_loaded", "hi_ready", "lo_ready", "chunk_done", "evacuated"))
        state_in, tail_out, conv_step, conv_done, silu_done, tails_T, tails_in, zeroed = (
            s.sem(n) for n in ("state_in", "tail_out", "conv_step", "conv_done", "silu_done", "tails_T", "tails_in", "zeroed"))
        tails_stored = [s.sem(f"tails_stored{g}") for g in range(2)]
        stored = [s.sem(f"stored{u}") for u in range(2)]
        block = ctx.enter_context(nc.Block())
        w_v = a["w_in"][0].rearrange("(k p) n -> p k n", p=P)

        @block.sync
        def _(sp):
            sp.wait_ge(lo_ready, 1)
            sp.dma_start(w_raw[:, :, 0:ROPE], w_v[:, :, KR0:KR0 + ROPE]).then_inc(w_loaded, 16)
            sp.dma_start(w_raw[:, :, ROPE:BAKR], w_v[:, :, BA0:BA0 + 2 * HEADS]).then_inc(ba_loaded, 16)

            def load(kind, i, u, t, b):
                col = sp.snap(column(kind, i, u)) if not isinstance(i, int) else column(kind, i, u)
                sp.wait_ge(lo_ready, t + 1)
                sp.dma_start(w_raw[:], w_v[:, :, bass.ds(col, P)]).then_inc(w_loaded, 16)

            each_tile(sp, load)
            sp.wait_ge(tails_in, 1)
            for g, name in enumerate(("new_conv_prompt", "new_conv_sample")):
                sp.dma_start(out[name].rearrange("d b i (j p) -> (d b i j) p", p=P), tail_rows[:, g]).then_inc(tails_stored[g], 16)
            for g in range(2):
                sp.wait_ge(tails_stored[g], 16)

        @block.scalar
        def _(act):
            act.sem_inc(evacuated, 2)
            for b in range(2):
                act.sem_inc(stored[b], 16)

            def split(t, b, n=P):
                act.wait_ge(w_loaded, 16 * t + 16)
                act.wait_ge(chunk_done, NCHUNK * t + NCHUNK)
                act.copy(w_hi[:, b, :, 0:n], w_raw[:, :, 0:n]).then_inc(hi_ready, 1)

            def product(t, c):
                act.wait_ge(chunk_done, NCHUNK * t + (2 * NCHUNK + c + 1))

            act.wait_ge(ba_loaded, 16)
            split(0, 0, BAKR)
            split(1, 1)
            for c in range(NCHUNK):
                product(0, c)
                last = act.copy(act_out[0:BAKR, 0, NW * c:NW * c + NW], acc[0][c][0:BAKR, 0:NW])
            last.then_inc(evacuated, 1)
            act.wait_ge(evacuated, 3)
            act.dma_start(d["bakr"], act_out[0:BAKR, 0, 0:T]).then_inc(stored[0], 16)

            def tile(kind, i, u, t, b):
                row = act.snap(2 * i + u) if not isinstance(i, int) else 2 * i + u
                if not (isinstance(t, int) and t == TILES - 1):
                    split(t + 1, 1 - b)
                if kind == "qkv":
                    act.wait_ge(tail_out, t)
                    product(t, 0)
                    act.copy(pre[:, b, PRE:PRE + NW], acc[b][0][:, 0:NW])
                    product(t, 1)
                    act.copy(pre[:, b, PRE + NW:PRE + 2 * NW], acc[b][1][:, 0:NW])
                    product(t, 2)
                    act.copy(pre[:, b, PRE + 2 * NW:PRE + SEQ], acc[b][2][:, 0:SEQ - 2 * NW])
                    act.copy(pre[:, b, PRE + SAMPLE_AT:ROW], acc[b][2][:, SEQ - 2 * NW:NW]).then_inc(evacuated, 1)
                    act.wait_ge(conv_done, t + 2)
                    act.activation(act_out[:, b], act_out[:, b], ACT.Silu).then_inc(silu_done, 1)
                    act.wait_ge(silu_done, t)
                else:
                    act.wait_ge(stored[b], stores(kind, i, u))
                    for c in range(NCHUNK):
                        product(t, c)
                        last = act.activation(act_out[:, b, NW * c:NW * c + NW], acc[b][c][:, 0:NW],
                                              ACT.Silu if kind == "gate" else ACT.Copy)
                    last.then_inc(evacuated, 1)
                    act.wait_ge(evacuated, t + 3)
                n = CONV if kind == "qkv" else T
                act.dma_start(d[kind][bass.ds(row, 1)].rearrange("j p n -> p (j n)"), act_out[:, b, 0:n]).then_inc(stored[b], 16)

            each_tile(act, tile)
            act.wait_ge(stored[0], 16 + 16 * ((TILES + 1) // 2))
            act.wait_ge(stored[1], 16 + 16 * (TILES // 2))
            act.wait_ge(tails_T, 1)
            act.copy(tail_rows[:], tailT[0:PRE * QKV_TILES, 0:2 * P].rearrange("r (g p) -> r g p", g=2)).then_inc(tails_in, 1)

        @block.vector
        def _(dve):
            for u in range(2):
                dve.memset(pre[:, u, 0:PRE], 0.0).then_inc(zeroed, 1)
            dve.sem_inc(lo_ready, 1)
            dve.sem_inc(conv_done, 2)
            dve.wait_ge(zeroed, 2)

            def split(t, b, n=P):
                dve.wait_ge(hi_ready, t + 1)
                dve.tensor_tensor(w_lo[:, b, :, 0:n], w_raw[:, :, 0:n], w_hi[:, b, :, 0:n].bitcast(F32), ALU.subtract).then_inc(lo_ready, 1)

            split(0, 0, BAKR)
            split(1, 1)

            def tile(kind, i, u, t, b):
                if not (isinstance(t, int) and t == TILES - 1):
                    split(t + 1, 1 - b)
                if kind == "qkv":
                    y = act_out[:, b]
                    j = dve.snap(t - 1)
                    w = [cols[:, 0, bass.ds(dve.snap(j + QKV_TILES * n), 1)] for n in range(CONV_W)]
                    dve.wait_ge(evacuated, t + 3)
                    dve.wait_ge(state_in, t)
                    dve.wait_ge(stored[b], stores(kind, i, u))
                    dve.tensor_scalar(y, pre[:, b, 0:CONV], w[0], None, ALU.mult).then_inc(conv_step, 1)
                    for n in range(1, CONV_W):
                        dve.wait_ge(conv_step, (CONV_W - 1) * j + n)
                        ins = dve.scalar_tensor_tensor(y, pre[:, b, n:n + CONV], w[n], y, ALU.mult, ALU.add)
                        ins.then_inc(conv_step if n < CONV_W - 1 else conv_done, 1)

            each_tile(dve, tile)

        @block.gpsimd
        def _(pool):
            pool.sem_inc(tail_out, 2)

            with pool.Fori(0, QKV_TILES // 2) as i:
                for u in range(2):
                    row = pool.snap(2 * i + u)
                    t, b = row + 1, 1 - u
                    pool.wait_ge(conv_done, t)
                    pool.tensor_copy(pre[:, b, PRE + SEQ:PRE + SAMPLE_AT],
                                     cols[:, 1, bass.ds(row, PRE, step=QKV_TILES)]).then_inc(state_in, 1)
                    pool.wait_ge(evacuated, t + 3)
                    for g, at in enumerate((SEQ, ROW - PRE)):
                        last = pool.tensor_copy(tails[:, g, :, bass.ds(row, 1)].rearrange("p i j -> p (i j)"), pre[:, b, at:at + PRE])
                    last.then_inc(tail_out, 1)

        @block.tensor
        def _(pe):
            pe.sem_inc(chunk_done, 2 * NCHUNK)

            def tile(t, b, n=P):
                pe.wait_ge(lo_ready, t + 2)
                pe.wait_ge(evacuated, t + 1)
                for c in range(NCHUNK):
                    cut = slice(NW * c, NW * c + NW)
                    for k in range(KT):
                        for x, (w, h) in enumerate(((w_hi, hn_hi), (w_hi, hn_lo), (w_lo, hn_hi))):
                            last = pe.matmul(acc[b][c][0:n, 0:NW], w[:, b, k, 0:n], h[:, k, cut],
                                             start=(k == 0 and x == 0), stop=(k == KT - 1 and x == 2))
                    last.then_inc(chunk_done, 1)

            tile(0, 0, BAKR)
            each_tile(pe, lambda kind, i, u, t, b: tile(t, b))
            pe.wait_ge(tail_out, QKV_TILES + 2)
            for g in range(2):
                last = pe.transpose(tailT[0:PRE * QKV_TILES, P * g:P * g + P], tails[:, g].rearrange("p i j -> p (i j)"), ident[:])
            last.then_inc(tails_T, 1)


LEVELS = 7


class Steps:

    def __init__(self, sem, names):
        self.sem, self.names, self.next = sem, names, 0

    def begin(self, eng):
        eng.sem_inc(self.sem, 2 * len(self.names))

    def done(self, instruction, name):
        assert self.names[self.next] == name, (name, self.names[self.next])
        self.next = (self.next + 1) % len(self.names)
        instruction.then_inc(self.sem, 1)

    def at(self, c, name, before=0):
        return len(self.names) * c + (len(self.names) * (2 - before) + self.names.index(name) + 1)


def decays(nc, a, d, ident, g_all, beta, eg, egl, edl):
    with ExitStack() as ctx:
        s = Space(nc, ctx, "dec")
        W = TOKEN_TILES * HEADS
        ba = s.sb("ba", [2 * HEADS, TOKEN_TILES * P])
        upper = s.sb("upper", [P, P])
        ones = s.sb("ones", [P, P])
        strict = s.sb("strict", [P, P])
        alog = s.sb("alog", [P, HEADS])
        dt = s.sb("dt", [P, HEADS])
        v, neg, e, ln = (s.sb(n, [P, TOKEN_TILES, HEADS]) for n in ("v", "neg", "e", "ln"))
        tok = s.ps("tok", [P, 512])
        cum = s.ps("cum", [P, 512])
        loaded, padded, tok_T, step, act_step, g_ready, cum_done = (
            s.sem(n) for n in ("loaded", "padded", "tok_T", "step", "act_step", "g_ready", "cum_done"))
        block = ctx.enter_context(nc.Block())
        tok_v = tok[:, 0:2 * W].rearrange("p (c x) -> p c x", x=2 * HEADS)

        @block.sync
        def _(sp):
            sp.dma_start(ba[:, 0:T], d["bakr"][ROPE:BAKR]).then_inc(loaded, 16)
            sp.dma_start(upper[:], a["upper"]).then_inc(loaded, 16)
            sp.dma_start(strict[:], a["lower"]).then_inc(loaded, 16)
            sp.dma_start(alog[:], a["a_log"].to_broadcast([P, HEADS])).then_inc(loaded, 16)
            sp.dma_start(dt[:], a["dt_bias"].to_broadcast([P, HEADS])).then_inc(loaded, 16)

        @block.gpsimd
        def _(pool):
            pool.memset(ba[:, T:], 0.0).then_inc(padded, 1)
            pool.memset(ones[:], 1.0).then_inc(padded, 1)

        @block.scalar
        def _(act):
            act.wait_ge(loaded, 80)
            act.activation(alog[:], alog[:], ACT.Exp).then_inc(act_step, 1)
            act.wait_ge(tok_T, 1)
            act.activation(beta[:], tok_v[:, :, 0:HEADS], ACT.Exp, scale=-1.0).then_inc(act_step, 1)
            act.wait_ge(step, 3)
            act.activation(e[:], neg[:], ACT.Exp).then_inc(act_step, 1)
            act.wait_ge(act_step, 3)
            act.activation(ln[:], e[:], ACT.Ln, bias=1.0).then_inc(act_step, 1)
            act.wait_ge(cum_done, 1)
            for k, e_out in enumerate((eg, egl, edl)):
                act.activation(e_out[:], cum[:, W * k:W * k + W].rearrange("p (c h) -> p c h", h=HEADS), ACT.Exp)

        @block.vector
        def _(dve):
            n = [0]

            def chain(ins):
                n[0] += 1
                ins.then_inc(step, 1)
                dve.wait_ge(step, n[0])

            dve.wait_ge(act_step, 2)
            av = tok_v[:, :, HEADS:]
            shape = [P, TOKEN_TILES, HEADS]
            chain(dve.tensor_tensor(v[:], av, dt[:, None, :].to_broadcast(shape), ALU.add))
            chain(dve.tensor_scalar(neg[:], v[:], -1.0, None, ALU.mult))
            chain(dve.tensor_tensor(neg[:], v[:], neg[:], ALU.min))
            chain(dve.tensor_scalar(v[:], v[:], 0.0, None, ALU.max))
            chain(dve.tensor_scalar(beta[:], beta[:], 1.0, None, ALU.add))
            chain(dve.reciprocal(beta[:], beta[:]))
            dve.wait_ge(act_step, 4)
            chain(dve.tensor_tensor(v[:], v[:], ln[:], ALU.add))
            chain(dve.tensor_tensor(v[:], v[:], alog[:, None, :].to_broadcast(shape), ALU.mult))
            chain(dve.tensor_scalar(g_all[:], v[:], -1.0, None, ALU.mult))
            dve.memset(g_all[DEC:2 * DEC, TOKEN_TILES - 1, :], 0.0).then_inc(g_ready, 1)
            dve.memset(g_all[2 * DEC:, TOKEN_TILES - 1, :], 0.0).then_inc(g_ready, 1)

        @block.tensor
        def _(pe):
            pe.wait_ge(loaded, 80)
            pe.wait_ge(padded, 2)
            for c in range(TOKEN_TILES):
                last = pe.transpose(tok[:, 16 * c:16 * c + 16], ba[:, P * c:P * c + P], ident[0:16, 0:16])
            last.then_inc(tok_T, 1)
            pe.wait_ge(g_ready, 2)
            flat = g_all[:].rearrange("p c h -> p (c h)")
            pe.matmul(cum[:, 0:W], upper[:], flat, start=True, stop=True)
            pe.matmul(cum[:, W:2 * W], ones[:], flat, start=True, stop=True)
            pe.matmul(cum[:, 2 * W:3 * W], strict[:], flat, start=True, stop=True).then_inc(cum_done, 1)


def delta_rule(nc, a, d, cols, ident, out):
    with ExitStack() as ctx:
        s = Space(nc, ctx, "gdn")
        CH = [P, TOKEN_TILES, HEADS]
        g_all, beta, eg, egl, edl = (s.sb(n, CH) for n in ("g_all", "beta", "eg", "egl", "edl"))
        decays(nc, a, d, ident, g_all, beta, eg, egl, edl)
        HF = HEADS // 2
        full = [P, HEADS, P]
        qkv = s.sb("qkv", [P, 2, 3 * HEADS, P])
        gate = s.sb("gate", [P, 2, HEADS, P])
        squares = s.sb("squares", [P, 2 * HEADS, P])
        kd, vb, dT, dL, aT, lmat, pc, X, Y, R, y, o, osq = (
            s.sb(n, full) for n in ("kd", "vb", "dT", "dL", "aT", "lmat", "pc", "X", "Y", "R", "y", "o", "osq"))
        C = s.sb("C", [P, 2, HEADS, P])
        mix = s.sb("mix", full)
        mix_hi, mix_lo = (s.sb(n, [P, 2, HEADS, P], F32R) for n in ("mix_hi", "mix_lo"))
        S = s.sb("S", [P, 2, HEADS, P])
        upper, lower = (s.sb(n, [P, P]) for n in ("upper", "lower"))
        gm = s.sb("gm", full)
        level = s.sb("level", [P, LEVELS, P])
        ones = s.sb("ones", [P, 1])
        mhalf = s.sb("mhalf", [P, 2 * HEADS])
        gch, kb, lam, nle, sqc, sq2, oss, var, orr = (
            s.sb(n, [P, HEADS]) for n in ("gch", "kb", "lam", "nle", "sqc", "sq2", "oss", "var", "orr"))
        sse = s.sb("sse", [P, 2 * HEADS])
        rs = s.sb("rs", [P, 2 * HEADS])
        B = [s.ps(f"b{i}", [P, 512]) for i in range(8)]
        bank = lambda i: B[i][:, :].rearrange("p (h n) -> p h n", n=P)
        half = lambda g: slice(HF * g, HF * g + HF)
        G2 = ("0", "1")
        LV = range(1, LEVELS)
        pe_names = (["ssq", "kT0", "kT1", "rows0", "rows1", "cols0", "cols1", "vT0", "vT1"] + [f"gq{p}" for p in range(4)] + ["Y0_0", "Y0_1"]
                    + [f"{w}{l}_{g}" for l in LV for w in (("P", "YP", "XP") if l < LEVELS - 1 else ("P", "YP")) for g in G2]
                    + [f"{w}{g}" for w in ("kS", "qS", "y", "Ay", "dS", "oT") for g in G2])
        dve_names = (["gch", "sse", "kd0", "kd1", "kb", "lam", "nle0", "nle", "sqc", "sq2", "vb0", "vb1"]
                     + [f"{w}{p}" for p in range(4) for w in ("AT", "L")] + [f"{w}{g}" for g in G2 for w in ("c0_", "X0_")]
                     + [f"{w}{l}_{g}" for l in LV for w in (("Y", "X") if l < LEVELS - 1 else ("Y",)) for g in G2]
                     + [f"{w}{g}" for w in ("R", "qe", "o", "S") for g in G2]
                     + ["oss", "var0", "var", "orr", "on", "mix0", "mix1", "mix_lo"])
        act_names = (["squares"] + [f"{w}{g}" for w in ("dT", "dL") for g in G2] + ["Y0_0", "Y0_1"]
                     + [f"P{l}_{g}" for l in LV for g in G2] + ["y0", "y1", "osq", "mix_hi"])
        pool_names = ["gm", "rs"] + [f"C{l}_{g}" for l in LV for g in G2] + ["aT0", "aT1", "orms"]
        PE, DVE, ACTS, POOL = (Steps(s.sem(n), names) for n, names in (
            ("pe_step", pe_names), ("dve_step", dve_names), ("act_step", act_names), ("pool_step", pool_names)))
        consts_in, set_up, sample_padded, ssm_out = s.sem("consts_in"), s.sem("set_up"), s.sem("sample_padded"), s.sem("ssm_out")
        qkv_in, gate_in, mix_out = ([s.sem(f"{n}{u}") for u in range(2)] for n in ("qkv_in", "gate_in", "mix_out"))
        block = ctx.enter_context(nc.Block())
        qkv_d = d["qkv"].rearrange("f p n -> p f n")
        gate_d = d["gate"].rearrange("(j z) p n -> z p j n", z=2)[0]
        mix_d = d["mix"][:, 0:HEADS].rearrange("w j p n -> w p j n")
        LAST = PROMPT_TILES

        def each_chunk(eng, body):
            with eng.Fori(0, PROMPT_TILES // 2) as i:
                for u in range(2):
                    body(eng.snap(2 * i + u), u, i, P, 0)
            body(LAST, 0, PROMPT_TILES // 2, DEC, 1)

        @block.sync
        def _(sp):
            for dst, src in ((upper, "upper"), (lower, "lower"), (level, "level")):
                sp.dma_start(dst[:], a[src]).then_inc(consts_in, 16)
            sp.dma_start(S[:, 1], a["state_gdn_ssm"][0, 0].rearrange("h k v -> k h v")).then_inc(consts_in, 16)

            def chunk(c, u, i, n, stream):
                sp.wait_ge(PE.sem, PE.at(c, "qS1", before=2) if not isinstance(c, int) else PE.at(c, "qS1", before=2))
                if stream:
                    sp.wait_ge(sample_padded, 1)
                at = c * P if not stream else SAMPLE_AT
                at = sp.snap(at) if not isinstance(at, int) else at
                sp.dma_start(qkv[:, u, :, 0:n], qkv_d[:, :, bass.ds(at, n)]).then_inc(qkv_in[u], 16)
                sp.wait_ge(DVE.sem, DVE.at(c, "mix1", before=2))
                ag = c * P
                ag = sp.snap(ag) if not isinstance(ag, int) else ag
                sp.dma_start(gate[:, u, :, 0:n], gate_d[:, :, bass.ds(ag, n)]).then_inc(gate_in[u], 16)

            each_chunk(sp, chunk)

        @block.gpsimd
        def _(pool):
            POOL.begin(pool)
            pool.memset(ones[:], 1.0).then_inc(set_up, 1)
            pool.memset(mhalf[:], -0.5).then_inc(set_up, 1)
            pool.memset(S[:, 0], 0.0).then_inc(set_up, 1)
            pool.wait_ge(set_up, 3)
            pool.wait_ge(consts_in, 64)

            def chunk(c, u, i, n, stream):
                if stream:
                    pool.wait_ge(PE.sem, PE.at(c, "qS1", before=2))
                    pool.memset(qkv[:, u, :, n:], 0.0).then_inc(sample_padded, 1)
                pool.wait_ge(DVE.sem, DVE.at(c, "gch"))
                POOL.done(pool.tensor_tensor(gm[:], lower[:, None, :].to_broadcast(full), gch[:, :, None].to_broadcast(full), ALU.mult), "gm")
                pool.wait_ge(DVE.sem, DVE.at(c, "sse"))
                POOL.done(pool.tensor_tensor(rs[:], sse[:], mhalf[:], ALU.pow), "rs")
                for l in LV:
                    for g in range(2):
                        if l == 1:
                            pool.wait_ge(DVE.sem, DVE.at(c, f"L{2 * g + 1}"))
                        if l >= 3:
                            pool.wait_ge(PE.sem, PE.at(c, f"P{l - 2}_{g}"))
                        POOL.done(pool.tensor_tensor(C[:, l % 2, half(g)], lmat[:, half(g)],
                                                     level[:, l:l + 1, :].to_broadcast([P, HF, P]), ALU.mult), f"C{l}_{g}")
                for g in range(2):
                    POOL.done(pool.tensor_tensor(aT[:, half(g)], aT[:, half(g)], upper[:, None, :].to_broadcast([P, HF, P]), ALU.mult), f"aT{g}")
                pool.wait_ge(DVE.sem, DVE.at(c, "var"))
                POOL.done(pool.tensor_tensor(orr[:], var[:], mhalf[:, 0:HEADS], ALU.pow), "orms")

            each_chunk(pool, chunk)

        @block.scalar
        def _(act):
            ACTS.begin(act)

            def chunk(c, u, i, n, stream):
                pe = lambda name, before=0: act.wait_ge(PE.sem, PE.at(c, name, before))
                dve = lambda name, before=0: act.wait_ge(DVE.sem, DVE.at(c, name, before))
                act.wait_ge(qkv_in[u], 16 * i + 16)
                ACTS.done(act.activation(squares[:], qkv[:, u, 0:2 * HEADS], ACT.Square), "squares")
                for g in range(2):
                    pe(f"rows{g}")
                    ACTS.done(act.activation(dT[:, half(g)], bank(2 + g), ACT.Exp), f"dT{g}")
                for g in range(2):
                    pe(f"cols{g}")
                    ACTS.done(act.activation(dL[:, half(g)], bank(6 + g), ACT.Exp), f"dL{g}")
                for g in range(2):
                    pe(f"Y0_{g}")
                    ACTS.done(act.copy(Y[:, half(g)], bank(2 + g)), f"Y0_{g}")
                for l in LV:
                    for g in range(2):
                        pe(f"P{l}_{g}")
                        ACTS.done(act.copy(pc[:, half(g)], bank(6 + g)), f"P{l}_{g}")
                for g in range(2):
                    pe(f"y{g}")
                    ACTS.done(act.copy(y[:, half(g)], bank(6 + g)), f"y{g}")
                dve("o1")
                ACTS.done(act.activation(osq[:], o[:], ACT.Square), "osq")
                at = act.snap(c * P) if not isinstance(c, int) else c * P
                dve("mix1")
                act.wait_ge(mix_out[u], 32 * i + 32)
                ACTS.done(act.copy(mix_hi[:, u], mix[:]), "mix_hi")
                dve("mix_lo")
                for w, part in enumerate((mix_hi, mix_lo)):
                    act.dma_start(mix_d[w, :, :, bass.ds(at, n)], part[:, u, :, 0:n].bitcast(F32)).then_inc(mix_out[u], 16)
                if not isinstance(c, int):
                    return
                act.wait_ge(mix_out[0], 32 * (PROMPT_TILES // 2 + 1) + 32)
                act.wait_ge(mix_out[1], 32 * (PROMPT_TILES // 2) + 32)
                act.wait_ge(DVE.sem, DVE.at(c, "S1"))
                for k, name in enumerate(("new_ssm_prompt", "new_ssm_sample")):
                    act.dma_start(out[name][0, 0].rearrange("h k v -> k h v"), S[:, k]).then_inc(ssm_out, 16)
                act.wait_ge(ssm_out, 32)

            for u in range(2):
                act.sem_inc(mix_out[u], 32)
            each_chunk(act, chunk)

        @block.vector
        def _(dve):
            DVE.begin(dve)
            dve.wait_ge(consts_in, 64)
            dve.wait_ge(set_up, 3)

            def chunk(c, u, i, n, stream):
                pe = lambda name, before=0: dve.wait_ge(PE.sem, PE.at(c, name, before))
                own = lambda name, before=0: dve.wait_ge(DVE.sem, DVE.at(c, name, before))
                act = lambda name, before=0: dve.wait_ge(ACTS.sem, ACTS.at(c, name, before))
                pool = lambda name, before=0: dve.wait_ge(POOL.sem, POOL.at(c, name, before))
                row = lambda t: t[:, bass.ds(c, 1), :]
                wide = lambda t, g: t[:, half(g), None].to_broadcast([P, HF, P])
                per = lambda t, g: row(t)[:, 0, half(g)][:, :, None].to_broadcast([P, HF, P])
                DVE.done(dve.tensor_copy(gch[:], row(g_all)[:, 0]), "gch")
                pe("ssq")
                DVE.done(dve.tensor_scalar(sse[:], B[7][:, 0:2 * HEADS], EPS, None, ALU.add), "sse")
                for g in range(2):
                    pe(f"kT{g}")
                    DVE.done(dve.tensor_tensor(kd[:, half(g)], bank(g), per(edl, g), ALU.mult), f"kd{g}")
                pool("rs")
                DVE.done(dve.tensor_tensor(kb[:], rs[:, HEADS:], row(beta)[:, 0], ALU.mult), "kb")
                own("kb")
                DVE.done(dve.tensor_tensor(lam[:], rs[:, HEADS:], kb[:], ALU.mult), "lam")
                own("lam")
                DVE.done(dve.tensor_tensor(nle[:], lam[:], row(eg)[:, 0], ALU.mult), "nle0")
                own("nle0")
                DVE.done(dve.tensor_scalar(nle[:], nle[:], -1.0, None, ALU.mult), "nle")
                DVE.done(dve.tensor_scalar(sqc[:], rs[:, 0:HEADS], float(P) ** -0.5, None, ALU.mult), "sqc")
                own("sqc")
                DVE.done(dve.scalar_tensor_tensor(sq2[:], sqc[:], 1.0 / P, sqc[:], ALU.mult, ALU.mult), "sq2")
                for g in range(2):
                    pe(f"vT{g}")
                    DVE.done(dve.tensor_tensor(vb[:, half(g)], bank(4 + g), wide(kb, g), ALU.mult), f"vb{g}")
                for p in range(4):
                    b = B[(0, 1, 4, 5)[p]][:, :].rearrange("p (h w n) -> p h w n", h=2, w=2)
                    pe(f"gq{p}")
                    act(f"dT{p // 2}")
                    DVE.done(dve.tensor_tensor(aT[:, 2 * p:2 * p + 2], b[:, :, 0], dT[:, 2 * p:2 * p + 2], ALU.mult), f"AT{p}")
                    act(f"dL{p // 2}")
                    for h in range(2):
                        k = 2 * p + h
                        last = dve.scalar_tensor_tensor(lmat[:, k], b[:, h, 1], lam[:, k:k + 1], dL[:, k], ALU.mult, ALU.mult)
                    DVE.done(last, f"L{p}")
                for g in range(2):
                    own(f"L{2 * g + 1}")
                    DVE.done(dve.tensor_tensor(X[:, half(g)], lmat[:, half(g)], level[:, 0:1, :].to_broadcast([P, HF, P]), ALU.mult), f"c0_{g}")
                    own(f"c0_{g}")
                    DVE.done(dve.tensor_tensor(X[:, half(g)], ident[:, None, :].to_broadcast([P, HF, P]), X[:, half(g)], ALU.subtract), f"X0_{g}")
                for l in LV:
                    for g in range(2):
                        pe(f"YP{l}_{g}")
                        if l == 1:
                            act(f"Y0_{g}")
                        else:
                            own(f"Y{l - 1}_{g}")
                        DVE.done(dve.tensor_tensor(Y[:, half(g)], Y[:, half(g)], bank(2 + g), ALU.subtract), f"Y{l}_{g}")
                    if l == LEVELS - 1:
                        continue
                    for g in range(2):
                        pe(f"XP{l}_{g}")
                        own(f"X{l - 1}_{g}")
                        DVE.done(dve.tensor_tensor(X[:, half(g)], X[:, half(g)], bank(4 + g), ALU.subtract), f"X{l}_{g}")
                own("vb1")
                for g in range(2):
                    pe(f"kS{g}")
                    for h in range(HF):
                        k = HF * g + h
                        last = dve.scalar_tensor_tensor(R[:, k], bank(g)[:, h], nle[:, k:k + 1], vb[:, k], ALU.mult, ALU.add)
                    DVE.done(last, f"R{g}")
                for g in range(2):
                    pe(f"qS{g}")
                    DVE.done(dve.tensor_tensor(o[:, half(g)], bank(2 + g), per(eg, g), ALU.mult), f"qe{g}")
                for g in range(2):
                    pe(f"Ay{g}")
                    own(f"qe{g}")
                    DVE.done(dve.tensor_tensor(o[:, half(g)], o[:, half(g)], bank(4 + g), ALU.add), f"o{g}")
                for g in range(2):
                    pe(f"dS{g}")
                    for h in range(HF):
                        k = HF * g + h
                        last = dve.scalar_tensor_tensor(S[:, stream, k], S[:, stream, k], row(egl)[:, 0, k:k + 1], bank(g)[:, h],
                                                        ALU.mult, ALU.add)
                    DVE.done(last, f"S{g}")
                act("osq")
                DVE.done(dve.tensor_reduce(oss[:], osq[:], AX.X, ALU.add), "oss")
                own("oss")
                DVE.done(dve.tensor_tensor(var[:], oss[:], sq2[:], ALU.mult), "var0")
                own("var0")
                DVE.done(dve.tensor_scalar(var[:], var[:], EPS, None, ALU.add), "var")
                pool("orms")
                DVE.done(dve.tensor_tensor(orr[:], orr[:], sqc[:], ALU.mult), "orr")
                own("orr")
                DVE.done(dve.tensor_tensor(o[:], o[:], orr[:, :, None].to_broadcast(full), ALU.mult), "on")
                dve.wait_ge(gate_in[u], 16 * i + 16)
                for g in range(2):
                    pe(f"oT{g}")
                    DVE.done(dve.scalar_tensor_tensor(mix[:, half(g)], bank(6 + g), cols[:, 0, R_GN:R_GN + 1],
                                                      gate[:, u, half(g)], ALU.mult, ALU.mult), f"mix{g}")
                act("mix_hi")
                DVE.done(dve.tensor_tensor(mix_lo[:, u], mix[:], mix_hi[:, u].bitcast(F32), ALU.subtract), "mix_lo")

            each_chunk(dve, chunk)

        @block.tensor
        def _(pe):
            PE.begin(pe)
            pe.wait_ge(consts_in, 64)
            pe.wait_ge(set_up, 3)

            def chunk(c, u, i, n, stream):
                dve = lambda name, before=0: pe.wait_ge(DVE.sem, DVE.at(c, name, before))
                act = lambda name, before=0: pe.wait_ge(ACTS.sem, ACTS.at(c, name, before))
                pool = lambda name, before=0: pe.wait_ge(POOL.sem, POOL.at(c, name, before))
                q, k, v = (qkv[:, u, HEADS * w:HEADS * w + HEADS] for w in range(3))

                def heads(name, b, lhsT, rhs):
                    for g in range(2):
                        name_g = f"{name}{g}"
                        for h in range(HF):
                            x = HF * g + h
                            last = pe.matmul(bank(b + g)[:, h], lhsT(x), rhs(x), start=True, stop=True)
                        PE.done(last, name_g)
                        yield g

                pe.wait_ge(qkv_in[u], 16 * i + 16)
                dve("gch")
                act("squares")
                dve("mix1", before=1)
                for f in range(2 * HEADS):
                    last = pe.matmul(B[7][:, f:f + 1], squares[:, f], ones[:], start=True, stop=True)
                PE.done(last, "ssq")
                for g in range(2):
                    for h in range(HF):
                        last = pe.transpose(bank(g)[:, h], k[:, HF * g + h], ident[:])
                    PE.done(last, f"kT{g}")
                pool("gm")
                for g in range(2):
                    for h in range(HF):
                        last = pe.matmul(bank(2 + g)[:, h], gm[:, HF * g + h], upper[:], start=True, stop=True)
                    PE.done(last, f"rows{g}")
                for g in range(2):
                    if g == 1:
                        dve("sse")
                    PE.done(pe.matmul(B[6 + g][:], upper[:], gm[:, half(g)].rearrange("p h n -> p (h n)"), start=True, stop=True), f"cols{g}")
                for g in range(2):
                    for h in range(HF):
                        last = pe.transpose(bank(4 + g)[:, h], v[:, HF * g + h], ident[:])
                    PE.done(last, f"vT{g}")
                for p in range(4):
                    dve(("kd0", "kd1", "vb0", "vb1")[p])
                    b = B[(0, 1, 4, 5)[p]]
                    for h in range(2):
                        x = 2 * p + h
                        last = pe.matmul(b[:, 2 * P * h:2 * P * h + 2 * P], k[:, x], qkv[:, u, x:x + HEADS + 1:HEADS], start=True, stop=True)
                    PE.done(last, f"gq{p}")
                for g in range(2):
                    dve(f"X0_{g}")
                    for h in range(HF):
                        last = pe.transpose(bank(2 + g)[:, h], X[:, HF * g + h], ident[:])
                    PE.done(last, f"Y0_{g}")
                for l in LV:
                    for g in range(2):
                        pool(f"C{l}_{g}")
                        if l == 1:
                            act(f"Y0_{g}")
                            act(f"dL{g}")
                        else:
                            dve(f"Y{l - 1}_{g}")
                            act(f"P{l - 1}_{g}")
                        for h in range(HF):
                            x = HF * g + h
                            last = pe.matmul(bank(6 + g)[:, h], C[:, l % 2, x], Y[:, x], start=True, stop=True)
                        PE.done(last, f"P{l}_{g}")
                    for g in range(2):
                        act(f"P{l}_{g}")
                        dve(f"X{l - 1}_{g}")
                        for h in range(HF):
                            x = HF * g + h
                            last = pe.matmul(bank(2 + g)[:, h], X[:, x], pc[:, x], start=True, stop=True)
                        PE.done(last, f"YP{l}_{g}")
                    if l == LEVELS - 1:
                        continue
                    for g in range(2):
                        if l == 1:
                            dve(f"L{2 + g}")
                        for h in range(HF):
                            x = HF * g + h
                            last = pe.matmul(bank(4 + g)[:, h], pc[:, x], X[:, x], start=True, stop=True)
                        PE.done(last, f"XP{l}_{g}")
                for g in range(2):
                    dve(f"S{g}", before=1)
                    for h in range(HF):
                        x = HF * g + h
                        last = pe.matmul(bank(g)[:, h], k[:, x], S[:, stream, x], start=True, stop=True)
                    PE.done(last, f"kS{g}")
                for g in range(2):
                    dve(f"Y{LEVELS - 1}_{g}")
                    for h in range(HF):
                        x = HF * g + h
                        last = pe.matmul(bank(2 + g)[:, h], q[:, x], S[:, stream, x], start=True, stop=True)
                    PE.done(last, f"qS{g}")
                for g in range(2):
                    dve(f"R{g}")
                    act(f"P{LEVELS - 1}_{g}")
                    for h in range(HF):
                        x = HF * g + h
                        last = pe.matmul(bank(6 + g)[:, h], Y[:, x], R[:, x], start=True, stop=True)
                    PE.done(last, f"y{g}")
                for g in range(2):
                    act(f"y{g}")
                    pool(f"aT{g}")
                    for h in range(HF):
                        x = HF * g + h
                        last = pe.matmul(bank(4 + g)[:, h], aT[:, x], y[:, x], start=True, stop=True)
                    PE.done(last, f"Ay{g}")
                for g in range(2):
                    for h in range(HF):
                        x = HF * g + h
                        last = pe.matmul(bank(g)[:, h], kd[:, x], y[:, x], start=True, stop=True)
                    PE.done(last, f"dS{g}")
                dve("on")
                for g in range(2):
                    for h in range(HF):
                        last = pe.transpose(bank(6 + g)[:, h], o[:, HF * g + h], ident[:])
                    PE.done(last, f"oT{g}")

            each_chunk(pe, chunk)


def masks():
    import numpy as np
    i = np.arange(P)
    lower = i[:, None] > i[None, :]
    level = np.zeros((P, LEVELS, P), np.float32)
    for l in range(LEVELS):
        s = 1 << l
        joined = (i[:, None] // (2 * s) == i[None, :] // (2 * s)) & ((i[:, None] // s) % 2 == 1) & ((i[None, :] // s) % 2 == 0)
        level[:, l] = joined
    return {"ident": np.eye(P, dtype=np.float32),
            "upper": (i[:, None] <= i[None, :]).astype(np.float32),
            "lower": lower.astype(np.float32),
            "level": level}


KEYS = T + PAST
PAST_TILES = PAST // P
KCH = 4
KW = KEYS // KCH
KEY_TILES = [(P * b, P) for b in range(PROMPT_TILES)] + [(SEQ, DEC)] + [(T + P * b, P) for b in range(PAST_TILES)]
SCALE = float(P + ROPE) ** -0.5
HIDDEN = -1e30
CHUNK = 64


def latents(nc, a, d, cols, ident, out, cq_hi, cq_lo, kv_hi, kv_lo, kr_hi, kr_lo, cos, sin, turn):
    with ExitStack() as ctx:
        s = Space(nc, ctx, "lat")
        raw = s.sb("raw", [P, C_TILES, T])
        sq = s.sb("sq", [P, C_TILES, T])
        rstd = s.sb("rstd", [P, T])
        ones = s.sb("ones", [P, P])
        past = s.sb("past", [P, PAST_TILES, LORA])
        past_kr = s.sb("past_kr", [P, PAST_TILES, ROPE])
        rows = s.sb("rows", [P, 2, LORA])
        kr = s.sb("kr", [P, T])
        swapped = s.sb("swapped", [P, T])
        kr_rows = s.sb("kr_rows", [P, TOKEN_TILES, ROPE])
        B = [s.ps(f"b{i}", [P, 512]) for i in range(8)]
        ld, ldk, raw_in = s.sem("ld"), s.sem("ldk"), [s.sem(f"raw_in{w}") for w in range(2)]
        pe_s, act_s, dve_s, ones_s = s.sem("pe"), s.sem("act"), s.sem("dve"), s.sem("ones_s")
        rows_out, kr_out = [s.sem(f"rows_out{u}") for u in range(2)], s.sem("kr_out")
        block = ctx.enter_context(nc.Block())
        latent = d["latent"].rearrange("(j w) p n -> w p j n", w=2)
        tiles = [(P * t, P) for t in range(PROMPT_TILES)] + [(SEQ, DEC)]
        PE_AT = {n: i + 1 for i, n in enumerate(
            ["var0", "var1"] + [f"rows{t}" for t in range(TOKEN_TILES)] + [f"past{x}" for x in range(2)]
            + ["turn", "kr_past"] + [f"kr_rows{g}" for g in range(2)])}
        ACT_AT = {n: i + 1 for i, n in enumerate(
            ["sq0", "rms0", "hi0", "sq1", "rms1", "hi1"] + [f"rows{t}" for t in range(TOKEN_TILES)]
            + ["past0", "past1", "krhi", "kr_past", "krdup", "kr_rows0", "kr_rows1"])}
        DVE_AT = {n: i + 1 for i, n in enumerate(
            ["mean0", "rstd0", "norm0", "lo0", "mean1", "rstd1", "norm1", "lo1", "past0", "past1",
             "sin", "cos", "kr", "krlo", "kr_pastlo"])}

        @block.sync
        def _(sp):
            sp.dma_start(raw[:], latent[0]).then_inc(raw_in[0], 16)
            for dst, src in ((past[:], a["cache_mla_latent"][0, 0].rearrange("(t p) n -> p t n", p=P)),
                             (past_kr[:], a["cache_mla_krope"][0, 0].rearrange("(t p) n -> p t n", p=P)),
                             (cos[:], a["cos"]), (sin[:], a["sin"]), (turn[:], a["turn"])):
                sp.dma_start(dst, src).then_inc(ld, 16)
            for h in range(2):
                sp.dma_start(kr[ROPE * h:ROPE * h + ROPE], d["bakr"][0:ROPE]).then_inc(ldk, 16)
            sp.wait_ge(dve_s, DVE_AT["lo0"])
            sp.dma_start(raw[:], latent[1]).then_inc(raw_in[1], 16)
            for t, (at, n) in enumerate(tiles):
                sp.wait_ge(act_s, ACT_AT[f"rows{t}"])
                dst = out["new_latent_prompt"][0, 0, at:at + n] if t < PROMPT_TILES else out["new_latent_sample"][0, 0]
                sp.dma_start(dst, rows[0:n, t % 2]).then_inc(rows_out[t % 2], 16)
            sp.wait_ge(act_s, ACT_AT["kr_rows1"])
            sp.dma_start(out["new_krope_prompt"][0, 0].rearrange("(t p) n -> p t n", p=P), kr_rows[:, 0:PROMPT_TILES]).then_inc(kr_out, 16)
            sp.dma_start(out["new_krope_sample"][0, 0], kr_rows[0:DEC, PROMPT_TILES]).then_inc(kr_out, 16)
            sp.wait_ge(kr_out, 32)
            sp.wait_ge(rows_out[0], 16 * 5)
            sp.wait_ge(rows_out[1], 16 * 4)

        @block.scalar
        def _(act):
            at = [0]

            def done(ins, name):
                at[0] += 1
                assert ACT_AT[name] == at[0], name
                ins.then_inc(act_s, 1)

            pe = lambda name: act.wait_ge(pe_s, PE_AT[name])
            dve = lambda name: act.wait_ge(dve_s, DVE_AT[name])
            for w, hi in ((0, cq_hi), (1, kv_hi)):
                act.wait_ge(raw_in[w], 16)
                if w:
                    pe("var0")
                done(act.activation(sq[:], raw[:], ACT.Square), f"sq{w}")
                dve(f"mean{w}")
                done(act.activation(rstd[:], rstd[:], ACT.Sqrt), f"rms{w}")
                dve(f"norm{w}")
                done(act.copy(hi[:, :, 0:T], raw[:]), f"hi{w}")
            for t, (_, n) in enumerate(tiles):
                pe(f"rows{t}")
                if t >= 2:
                    act.wait_ge(rows_out[t % 2], 16 * (t // 2))
                done(act.copy(rows[0:n, t % 2], B[t % 2][0:n]), f"rows{t}")
            for x in range(PAST_TILES):
                pe(f"past{x}")
                done(act.copy(kv_hi[:, :, T + P * x:T + P * x + P], B[2 + x][:, :].rearrange("p (k n) -> p k n", k=4)), f"past{x}")
            dve("kr")
            done(act.copy(kr_hi[:, 0:T], kr[:]), "krhi")
            pe("kr_past")
            done(act.copy(kr_hi[0:ROPE, T:], B[7][0:ROPE, 0:PAST]), "kr_past")
            done(act.copy(kr_hi[ROPE:, T:], B[7][0:ROPE, 0:PAST]), "krdup")
            for g in range(2):
                pe(f"kr_rows{g}")
                if g == 0:
                    done(act.copy(kr_rows[:, 0:PROMPT_TILES], B[0][:, :].rearrange("p (t n) -> p t n", n=ROPE)), "kr_rows0")
                else:
                    done(act.copy(kr_rows[0:DEC, PROMPT_TILES], B[1][0:DEC, 0:ROPE]), "kr_rows1")

        @block.gpsimd
        def _(pool):
            pool.memset(ones[:], 1.0).then_inc(ones_s, 1)

        @block.vector
        def _(dve):
            at = [0]

            def done(ins, name):
                at[0] += 1
                assert DVE_AT[name] == at[0], name
                ins.then_inc(dve_s, 1)

            pe = lambda name: dve.wait_ge(pe_s, PE_AT[name])
            act = lambda name: dve.wait_ge(act_s, ACT_AT[name])
            own = lambda name: dve.wait_ge(dve_s, DVE_AT[name])
            for w, hi, lo, norm in ((0, cq_hi, cq_lo, R_QN), (1, kv_hi, kv_lo, R_KVN)):
                pe(f"var{w}")
                if w:
                    own("norm0")
                for c in range(NCHUNK):
                    last = dve.tensor_scalar(rstd[:, NW * c:NW * c + NW], B[c + 4 * w][:, 0:NW], 1.0 / LORA, EPS, ALU.mult, ALU.add)
                done(last, f"mean{w}")
                act(f"rms{w}")
                done(dve.reciprocal(rstd[:], rstd[:]), f"rstd{w}")
                own(f"rstd{w}")
                for k in range(C_TILES):
                    last = dve.scalar_tensor_tensor(raw[:, k], raw[:, k], cols[:, 0, norm + k:norm + k + 1], rstd[:], ALU.mult, ALU.mult)
                done(last, f"norm{w}")
                act(f"hi{w}")
                done(dve.tensor_tensor(lo[:, :, 0:T], raw[:], hi[:, :, 0:T].bitcast(F32), ALU.subtract), f"lo{w}")
            for x in range(PAST_TILES):
                act(f"past{x}")
                cut = slice(T + P * x, T + P * x + P)
                done(dve.tensor_tensor(kv_lo[:, :, cut], B[2 + x][:, :].rearrange("p (k n) -> p k n", k=4),
                                       kv_hi[:, :, cut].bitcast(F32), ALU.subtract), f"past{x}")
            pe("turn")
            for c in range(NCHUNK):
                cut = slice(NW * c, NW * c + NW)
                last = dve.tensor_tensor(swapped[:, cut], B[4 + c][:, 0:NW], sin[:, cut], ALU.mult)
            done(last, "sin")
            done(dve.tensor_tensor(kr[:], kr[:], cos[:], ALU.mult), "cos")
            own("cos")
            done(dve.tensor_tensor(kr[:], kr[:], swapped[:], ALU.add), "kr")
            act("krhi")
            done(dve.tensor_tensor(kr_lo[:, 0:T], kr[:], kr_hi[:, 0:T].bitcast(F32), ALU.subtract), "krlo")
            act("krdup")
            dve.tensor_tensor(kr_lo[0:ROPE, T:], B[7][0:ROPE, 0:PAST], kr_hi[0:ROPE, T:].bitcast(F32), ALU.subtract)
            done(dve.tensor_tensor(kr_lo[ROPE:, T:], B[7][0:ROPE, 0:PAST], kr_hi[ROPE:, T:].bitcast(F32), ALU.subtract), "kr_pastlo")

        @block.tensor
        def _(pe):
            at = [0]

            def done(ins, name):
                at[0] += 1
                assert PE_AT[name] == at[0], name
                ins.then_inc(pe_s, 1)

            act = lambda name: pe.wait_ge(act_s, ACT_AT[name])
            dve = lambda name: pe.wait_ge(dve_s, DVE_AT[name])
            pe.wait_ge(ones_s, 1)
            for w in range(2):
                act(f"sq{w}")
                for c in range(NCHUNK):
                    for k in range(C_TILES):
                        last = pe.matmul(B[c + 4 * w][:, 0:NW], ones[:], sq[:, k, NW * c:NW * c + NW], start=(k == 0), stop=(k == C_TILES - 1))
                done(last, f"var{w}")
            dve("norm1")
            for t, (first, n) in enumerate(tiles):
                if t >= 2:
                    act(f"rows{t - 2}")
                else:
                    dve("mean1")
                for k in range(C_TILES):
                    last = pe.transpose(B[t % 2][0:n, P * k:P * k + P], raw[:, k, first:first + n], ident[:])
                done(last, f"rows{t}")
            pe.wait_ge(ld, 80)
            pe.wait_ge(ldk, 32)
            for x in range(PAST_TILES):
                for k in range(C_TILES):
                    last = pe.transpose(B[2 + x][:, P * k:P * k + P], past[:, x, P * k:P * k + P], ident[:])
                done(last, f"past{x}")
            for c in range(NCHUNK):
                last = pe.matmul(B[4 + c][:, 0:NW], turn[:], kr[:, NW * c:NW * c + NW], start=True, stop=True)
            done(last, "turn")
            for x in range(PAST_TILES):
                last = pe.transpose(B[7][0:ROPE, P * x:P * x + P], past_kr[:, x], ident[:])
            done(last, "kr_past")
            dve("kr")
            act(f"rows{TOKEN_TILES - 1}")
            for t in range(PROMPT_TILES):
                last = pe.transpose(B[0][:, ROPE * t:ROPE * t + ROPE], kr[0:ROPE, P * t:P * t + P], ident[0:ROPE, 0:ROPE])
            done(last, "kr_rows0")
            done(pe.transpose(B[1][0:DEC, 0:ROPE], kr[0:ROPE, SEQ:T], ident[0:ROPE, 0:ROPE]), "kr_rows1")


def attend(nc, a, d, cols, ident, out):
    with ExitStack() as ctx:
        s = Space(nc, ctx, "mla")
        cq_hi, cq_lo = (s.sb(n, [P, C_TILES, T], F32R) for n in ("cq_hi", "cq_lo"))
        kv_hi, kv_lo = (s.sb(n, [P, C_TILES, KEYS], F32R) for n in ("kv_hi", "kv_lo"))
        kr_hi, kr_lo = (s.sb(n, [P, KEYS], F32R) for n in ("kr_hi", "kr_lo"))
        cos, sin = (s.sb(n, [P, T]) for n in ("cos", "sin"))
        turn = s.sb("turn", [P, P])
        latents(nc, a, d, cols, ident, out, cq_hi, cq_lo, kv_hi, kv_lo, kr_hi, kr_lo, cos, sin, turn)
        UNITS = [("qr", None)] + [(x, e) for e in range(2) for x in ("q", "k", "v")]
        U = len(UNITS)
        w_raw = s.sb("w_raw", [P, U, C_TILES, P])
        w_hi, w_lo = (s.sb(n, [P, 2, C_TILES, P], F32R) for n in ("w_hi", "w_lo"))
        q_hi, q_lo, qr_hi, qr_lo = (s.sb(n, [P, T], F32R) for n in ("q_hi", "q_lo", "qr_hi", "qr_lo"))
        k_hi, k_lo = (s.sb(n, [P, KEYS], F32R) for n in ("k_hi", "k_lo"))
        qr = s.sb("qr", [P, T])
        vT = s.sb("vT", [P, KEYS])
        v_tok = s.sb("v_tok", [P, len(KEY_TILES), P])
        probs, pT = (s.sb(n, [P, 2, SEQ]) for n in ("probs", "pT"))
        o_tok = s.sb("o_tok", [P, 2, P])
        gate = s.sb("gate", [P, 2, T])
        mix = s.sb("mix", [P, T])
        mix_hi, mix_lo = (s.sb(n, [P, T], F32R) for n in ("mix_hi", "mix_lo"))
        mx, nm, total, inv = (s.sb(n, [P, 2]) for n in ("mx", "nm", "total", "inv"))
        scores = [s.ps(f"scores{u}", [P, 1024]) for u in range(2)]
        ptp = [s.ps(f"ptp{g}", [P, 512]) for g in range(2)]
        o_ps, oT_ps = s.ps("o", [P, 512]), s.ps("oT", [P, 512])
        chunk_bank = lambda c: scores[c // 2][:, 512 * (c % 2):512 * (c % 2) + 512]
        NT = TOKEN_TILES
        TILE = [(P * t, P, list(range(t + 1))) for t in range(PROMPT_TILES)] + [(SEQ, DEC, list(range(PROMPT_TILES, len(KEY_TILES))))]

        def groups(t):
            at, parts = 0, []
            for b in TILE[t][2]:
                parts.append((b, at, KEY_TILES[b][1]))
                at += KEY_TILES[b][1]
            return [parts[i:i + 4] for i in range(0, len(parts), 4)], at

        def nchunks(x):
            return NCHUNK if x in ("qr", "q") else KCH

        names = {"pe": [], "act": [], "dve": []}

        def unit_names(w):
            x, e = UNITS[w]
            names["act"].append(f"w{w}")
            names["dve"].append(f"w{w}")
            names["pe"] += [f"u{w}_{c}" for c in range(nchunks(x))]
            if x == "qr":
                names["act"] += [f"raw{w}_{c}" for c in range(NCHUNK)] + ["qr_hi"]
                names["pe"].append("turn")
                names["dve"] += ["sin", "cos", "qr", "qr_lo"]
            elif x == "v":
                names["act"] += [f"raw{w}_{c}" for c in range(KCH)]
                names["pe"] += [f"vt{w}_{g}" for g in range(3)]
                names["dve"] += [f"vt{w}_{g}" for g in range(3)]
            else:
                names["act"] += [f"hi{w}_{c}" for c in range(nchunks(x))]
                names["dve"] += [f"lo{w}_{c}" for c in range(nchunks(x))]

        def attention_names(e):
            for st in range(NT + 3):
                if st < NT:
                    names["pe"].append(f"S{e}_{st}")
                    names["dve"] += ([f"mask{e}_{st}"] if st < PROMPT_TILES else []) + [f"mx{e}_{st}", f"nm{e}_{st}"]
                    names["act"].append(f"E{e}_{st}")
                if 0 <= st - 1 < NT:
                    gs = range(len(groups(st - 1)[0]))
                    names["pe"] += [f"T{e}_{st - 1}_{g}" for g in gs]
                    names["dve"] += [f"T{e}_{st - 1}_0", f"inv{e}_{st - 1}"]
                    if len(gs) > 1:
                        names["act"].append(f"T{e}_{st - 1}_1")
                if 0 <= st - 2 < NT:
                    names["pe"].append(f"O{e}_{st - 2}")
                    names["act"].append(f"O{e}_{st - 2}")
                if 0 <= st - 3 < NT:
                    names["pe"].append(f"OT{e}_{st - 3}")
                    names["dve"].append(f"mix{e}_{st - 3}")
            names["act"].append(f"mix_hi{e}")
            names["dve"].append(f"mix_lo{e}")

        def each_step(unit, attention):
            unit(0)
            for e in range(2):
                for w in range(3 * e + 1, 3 * e + 4):
                    unit(w)
                attention(e)

        each_step(unit_names, attention_names)
        PE, ACTS, DVE = (Steps(s.sem(f"{n}_step"), names[n]) for n in ("pe", "act", "dve"))
        w_loaded = [s.sem(f"w_loaded{w}") for w in range(U)]
        gate_in, mix_out = [s.sem(f"gate_in{e}") for e in range(2)], s.sem("mix_out")
        passed, free_seen = s.sem("passed"), s.sem("free_seen")
        block = ctx.enter_context(nc.Block())
        q_up = a["w_q_up"][0].rearrange("(k p) h n -> p k h n", p=P)
        uk, uv = (a[n][0].rearrange("(k p) h n -> p k h n", p=P) for n in ("w_uk", "w_uv"))
        TURNS = HEADS // 2

        @block.sync
        def _(sp):
            with sp.Fori(0, TURNS) as i:
                for w, (x, e) in enumerate(UNITS):
                    head = sp.snap(2 * i + (e or 0))
                    both = [sp.snap(2 * i + h) for h in range(2)]
                    sp.wait_ge(DVE.sem, DVE.at(i, f"w{w}", before=1))
                    sp.sem_inc(free_seen, 1)
                    if x == "qr":
                        for h in range(2):
                            sp.dma_start(w_raw[:, w, :, ROPE * h:ROPE * h + ROPE],
                                         q_up[:, :, bass.ds(both[h], 1), P:].rearrange("p k h n -> p k (h n)")).then_inc(w_loaded[w], 16)
                        continue
                    src = {"q": q_up, "k": uk, "v": uv}[x]
                    sp.dma_start(w_raw[:, w], src[:, :, bass.ds(head, 1), 0:P].rearrange("p k h n -> p k (h n)")).then_inc(w_loaded[w], 16)
                for e in range(2):
                    row = sp.snap(4 * i + (2 * e + 1))
                    sp.wait_ge(DVE.sem, DVE.at(i, f"mix{e}_{NT - 1}", before=1))
                    sp.sem_inc(free_seen, 1)
                    sp.dma_start(gate[:, e], d["gate"][bass.ds(row, 1)].rearrange("j p n -> p (j n)")).then_inc(gate_in[e], 16)

        @block.scalar
        def _(act):
            ACTS.begin(act)
            act.sem_inc(mix_out, 32)
            with act.Fori(0, TURNS) as i:
                pe = lambda name, before=0: act.wait_ge(PE.sem, PE.at(i, name, before))
                dve = lambda name, before=0: act.wait_ge(DVE.sem, DVE.at(i, name, before))

                def unit(w):
                    x, e = UNITS[w]
                    act.wait_ge(w_loaded[w], 32 * i + 32 if x == "qr" else 16 * i + 16)
                    before = w - 2 if w >= 2 else U - 1 - w
                    pe(f"u{before}_{nchunks(UNITS[before][0]) - 1}", 0 if w >= 2 else 1)
                    ACTS.done(act.copy(w_hi[:, w % 2], w_raw[:, w]), f"w{w}")
                    for c in range(nchunks(x)):
                        pe(f"u{w}_{c}")
                        n = NW if x in ("qr", "q") else KW
                        cut = slice(n * c, n * c + n)
                        dst = {"qr": qr, "q": q_hi, "k": k_hi, "v": vT}[x]
                        ACTS.done(act.copy(dst[:, cut], chunk_bank(c)[:, 0:n]), f"{'raw' if x in ('qr', 'v') else 'hi'}{w}_{c}")
                    if x == "qr":
                        dve("qr")
                        ACTS.done(act.copy(qr_hi[:], qr[:]), "qr_hi")

                def attention(e):
                    for st in range(NT + 3):
                        if st < NT:
                            t, n = st, TILE[st][1]
                            width = groups(t)[1]
                            dve(f"nm{e}_{t}")
                            ACTS.done(act.activation(probs[0:n, t % 2, 0:width], scores[t % 2][0:n, 0:width], ACT.Exp,
                                                     bias=nm[0:n, t % 2:t % 2 + 1], scale=SCALE,
                                                     accum_out=total[0:n, t % 2:t % 2 + 1]), f"E{e}_{t}")
                        t = st - 1
                        if 0 <= t < NT and len(groups(t)[0]) > 1:
                            pe(f"T{e}_{t}_1")
                            k = sum(x[2] for x in groups(t)[0][1])
                            ACTS.done(act.copy(pT[:, t % 2, 512:512 + k], ptp[1][:, 0:k]), f"T{e}_{t}_1")
                        t = st - 2
                        if 0 <= t < NT:
                            n = TILE[t][1]
                            pe(f"O{e}_{t}")
                            dve(f"inv{e}_{t}")
                            ACTS.done(act.activation(o_tok[0:n, t % 2], o_ps[0:n, 0:P], ACT.Copy, scale=inv[0:n, t % 2:t % 2 + 1]), f"O{e}_{t}")
                    row = act.snap(2 * i + (HEADS + e))
                    dve(f"mix{e}_{NT - 1}")
                    act.wait_ge(mix_out, 64 * i + (32 * e + 32))
                    ACTS.done(act.copy(mix_hi[:], mix[:]), f"mix_hi{e}")
                    dve(f"mix_lo{e}")
                    for w, part in enumerate((mix_hi, mix_lo)):
                        act.dma_start(d["mix"][w, bass.ds(row, 1)].rearrange("j p n -> p (j n)"), part[:].bitcast(F32)).then_inc(mix_out, 16)

                each_step(unit, attention)
            act.wait_ge(mix_out, 64 * TURNS + 32)

        @block.vector
        def _(dve):
            DVE.begin(dve)
            with dve.Fori(0, TURNS) as i:
                pe = lambda name, before=0: dve.wait_ge(PE.sem, PE.at(i, name, before))
                act = lambda name, before=0: dve.wait_ge(ACTS.sem, ACTS.at(i, name, before))
                own = lambda name, before=0: dve.wait_ge(DVE.sem, DVE.at(i, name, before))

                def unit(w):
                    x, e = UNITS[w]
                    act(f"w{w}")
                    DVE.done(dve.tensor_tensor(w_lo[:, w % 2], w_raw[:, w], w_hi[:, w % 2].bitcast(F32), ALU.subtract), f"w{w}")
                    if x == "qr":
                        pe("turn")
                        for c in range(NCHUNK):
                            cut = slice(NW * c, NW * c + NW)
                            bank = (ptp[0], ptp[1], o_ps)[c]
                            last = dve.tensor_tensor(vT[:, cut], bank[:, 0:NW], sin[:, cut], ALU.mult)
                        DVE.done(last, "sin")
                        DVE.done(dve.tensor_tensor(qr[:], qr[:], cos[:], ALU.mult), "cos")
                        own("cos")
                        DVE.done(dve.tensor_tensor(qr[:], qr[:], vT[:, 0:T], ALU.add), "qr")
                        act("qr_hi")
                        DVE.done(dve.tensor_tensor(qr_lo[:], qr[:], qr_hi[:].bitcast(F32), ALU.subtract), "qr_lo")
                    elif x == "v":
                        for g in range(3):
                            pe(f"vt{w}_{g}")
                            tiles = list(range(len(KEY_TILES)))[4 * g:4 * g + 4]
                            b = ptp[g % 2][:, 0:P * len(tiles)].rearrange("p (t n) -> p t n", n=P)
                            if PROMPT_TILES in tiles:
                                dve.tensor_copy(v_tok[0:DEC, tiles[0]], b[0:DEC, 0])
                                DVE.done(dve.tensor_copy(v_tok[:, tiles[1]:tiles[-1] + 1], b[:, 1:]), f"vt{w}_{g}")
                            else:
                                DVE.done(dve.tensor_copy(v_tok[:, tiles[0]:tiles[-1] + 1], b), f"vt{w}_{g}")
                    else:
                        n = NW if x == "q" else KW
                        for c in range(nchunks(x)):
                            cut = slice(n * c, n * c + n)
                            hi, lo = (q_hi, q_lo) if x == "q" else (k_hi, k_lo)
                            act(f"hi{w}_{c}")
                            DVE.done(dve.tensor_tensor(lo[:, cut], chunk_bank(c)[:, 0:n], hi[:, cut].bitcast(F32), ALU.subtract), f"lo{w}_{c}")

                def attention(e):
                    for st in range(NT + 3):
                        if st < NT:
                            t, n = st, TILE[st][1]
                            width = groups(t)[1]
                            pe(f"S{e}_{t}")
                            if t < PROMPT_TILES:
                                DVE.done(dve.memset(scores[t % 2][0:CHUNK, width - CHUNK:width], HIDDEN), f"mask{e}_{t}")
                                own(f"mask{e}_{t}")
                            DVE.done(dve.tensor_reduce(mx[0:n, t % 2:t % 2 + 1], scores[t % 2][0:n, 0:width], AX.X, ALU.max), f"mx{e}_{t}")
                            own(f"mx{e}_{t}")
                            DVE.done(dve.tensor_scalar(nm[0:n, t % 2:t % 2 + 1], mx[0:n, t % 2:t % 2 + 1], -SCALE, None, ALU.mult), f"nm{e}_{t}")
                        t = st - 1
                        if 0 <= t < NT:
                            n = TILE[t][1]
                            pe(f"T{e}_{t}_0")
                            if t < PROMPT_TILES:
                                k = P * len(groups(t)[0][0])
                                last = dve.tensor_copy(pT[:, t % 2, 0:k], ptp[0][:, 0:k])
                            else:
                                dve.tensor_copy(pT[0:DEC, t % 2, 0:DEC], ptp[0][0:DEC, 0:DEC])
                                last = dve.tensor_copy(pT[:, t % 2, P:3 * P].rearrange("p (b n) -> p b n", n=P)[:, :, 0:DEC],
                                                       ptp[0][:, P:3 * P].rearrange("p (b n) -> p b n", n=P)[:, :, 0:DEC])
                            DVE.done(last, f"T{e}_{t}_0")
                            act(f"E{e}_{t}")
                            if t >= 2:
                                act(f"O{e}_{t - 2}")
                            DVE.done(dve.reciprocal(inv[0:n, t % 2:t % 2 + 1], total[0:n, t % 2:t % 2 + 1]), f"inv{e}_{t}")
                        t = st - 3
                        if 0 <= t < NT:
                            first, n, _ = TILE[t]
                            pe(f"OT{e}_{t}")
                            if t == 0:
                                dve.wait_ge(gate_in[e], 16 * i + 16)
                            DVE.done(dve.tensor_tensor(mix[:, first:first + n], oT_ps[:, 0:n], gate[:, e, first:first + n], ALU.mult), f"mix{e}_{t}")

                    act(f"mix_hi{e}")
                    DVE.done(dve.tensor_tensor(mix_lo[:], mix[:], mix_hi[:].bitcast(F32), ALU.subtract), f"mix_lo{e}")

                each_step(unit, attention)

        @block.tensor
        def _(pe):
            PE.begin(pe)
            with pe.Fori(0, TURNS) as i:
                dve = lambda name, before=0: pe.wait_ge(DVE.sem, DVE.at(i, name, before))
                act = lambda name, before=0: pe.wait_ge(ACTS.sem, ACTS.at(i, name, before))
                THREE = ((0, 0), (0, 1), (1, 0))

                def chunk_free(w, c):
                    if w == 0:
                        act(f"E1_{NT - 1}", 1)
                        return
                    if w == 4:
                        act(f"E0_{NT - 1}")
                        return
                    x = UNITS[w - 1][0]
                    if c < nchunks(x):
                        if x in ("qr", "v"):
                            act(f"raw{w - 1}_{c}")
                        else:
                            dve(f"lo{w - 1}_{c}")

                def hold(t):
                    if t == PROMPT_TILES:
                        pe.sem_inc(passed, 1)

                def unit(w):
                    x, e = UNITS[w]
                    dve(f"w{w}")
                    n = NW if x in ("qr", "q") else KW
                    hi, lo = (cq_hi, cq_lo) if x in ("qr", "q") else (kv_hi, kv_lo)
                    for c in range(nchunks(x)):
                        chunk_free(w, c)
                        for k in range(C_TILES):
                            for j, (ww, xx) in enumerate(THREE):
                                last = pe.matmul(chunk_bank(c)[:, 0:n], (w_hi, w_lo)[ww][:, w % 2, k], (hi, lo)[xx][:, k, n * c:n * c + n],
                                                 start=(k == 0 and j == 0), stop=(k == C_TILES - 1 and j == 2))
                        PE.done(last, f"u{w}_{c}")
                    if x == "qr":
                        act(f"raw{w}_{NCHUNK - 1}")
                        for c in range(NCHUNK):
                            bank = (ptp[0], ptp[1], o_ps)[c]
                            last = pe.matmul(bank[:, 0:NW], turn[:], qr[:, NW * c:NW * c + NW], start=True, stop=True)
                        PE.done(last, "turn")
                    elif x == "v":
                        act(f"raw{w}_{KCH - 1}")
                        for g in range(3):
                            if g == 2:
                                dve(f"vt{w}_0")
                            if g == 0 and w < 4:
                                dve("sin")
                            if g == 2:
                                hold(PROMPT_TILES)
                            for j, b in enumerate(range(len(KEY_TILES))[4 * g:4 * g + 4]):
                                at, m = KEY_TILES[b]
                                last = pe.transpose(ptp[g % 2][0:m, P * j:P * j + P], vT[:, at:at + m], ident[:])
                            PE.done(last, f"vt{w}_{g}")

                def attention(e):
                    for st in range(NT + 3):
                        if st < NT:
                            t = st
                            first, n, tiles = TILE[t]
                            key0, width = KEY_TILES[tiles[0]][0], groups(t)[1]
                            if t < 2:
                                act(f"raw{3 * e + 3}_{KCH - 1}")
                                if t == 0:
                                    dve(f"vt{3 * e + 3}_2")
                            else:
                                act(f"E{e}_{t - 2}")
                            rope = slice(ROPE * e, ROPE * e + ROPE)
                            hold(t)
                            for c0 in range(0, width, 512):
                                c1 = min(c0 + 512, width)
                                for j, (ww, xx) in enumerate(THREE):
                                    pe.matmul(scores[t % 2][0:n, c0:c1], (q_hi, q_lo)[ww][:, first:first + n],
                                              (k_hi, k_lo)[xx][:, key0 + c0:key0 + c1], start=(j == 0), stop=False)
                                for j, (ww, xx) in enumerate(THREE):
                                    last = pe.matmul(scores[t % 2][0:n, c0:c1], (qr_hi, qr_lo)[ww][rope, first:first + n],
                                                     (kr_hi, kr_lo)[xx][rope, key0 + c0:key0 + c1], start=False, stop=(j == 2))
                            PE.done(last, f"S{e}_{t}")
                        t = st - 1
                        if 0 <= t < NT:
                            n = TILE[t][1]
                            act(f"E{e}_{t}")
                            for g, parts in enumerate(groups(t)[0]):
                                if t > 0:
                                    if g == 0:
                                        dve(f"T{e}_{t - 1}_0")
                                    elif len(groups(t - 1)[0]) > 1:
                                        act(f"T{e}_{t - 1}_1")
                                hold(t)
                                for j, (b, at, m) in enumerate(parts):
                                    last = pe.transpose(ptp[g][0:m, P * j:P * j + n], probs[0:n, t % 2, at:at + m], ident[0:n, 0:n])
                                PE.done(last, f"T{e}_{t}_{g}")
                        t = st - 2
                        if 0 <= t < NT:
                            n = TILE[t][1]
                            dve(f"T{e}_{t}_0")
                            if t > 0:
                                act(f"O{e}_{t - 1}")
                            hold(t)
                            parts = [x for g in groups(t)[0] for x in g]
                            for j, (b, at, m) in enumerate(parts):
                                last = pe.matmul(o_ps[0:n, 0:P], pT[0:m, t % 2, P * j:P * j + n], v_tok[0:m, b], start=(j == 0), stop=(j == len(parts) - 1))
                            PE.done(last, f"O{e}_{t}")
                        t = st - 3
                        if 0 <= t < NT:
                            n = TILE[t][1]
                            act(f"O{e}_{t}")
                            if t > 0:
                                dve(f"mix{e}_{t - 1}")
                            hold(t)
                            PE.done(pe.transpose(oT_ps[:, 0:n], o_tok[0:n, t % 2], ident[0:n, 0:n]), f"OT{e}_{t}")

                each_step(unit, attention)


def rotation():
    import numpy as np
    inv = (10000.0 ** (-np.arange(0, ROPE, 2) / ROPE)).astype(np.float32)
    pos = np.concatenate([np.arange(SEQ), PAST + np.arange(DEC)]).astype(np.float32)
    ang = (pos[:, None] * inv[None, :]).astype(np.float32)
    rows = np.tile(ang.T, (4, 1))
    turn = np.zeros((P, P), np.float32)
    for h in range(2):
        for r in range(ROPE // 2):
            turn[ROPE * h + r + ROPE // 2, ROPE * h + r] = -1.0
            turn[ROPE * h + r, ROPE * h + r + ROPE // 2] = 1.0
    return {"cos": np.cos(rows).astype(np.float32), "sin": np.sin(rows).astype(np.float32), "turn": turn}


def project_out(nc, a, d, ident, ssq, w_hi, w_lo, w_raw):
    MT = D_MODEL // P
    with ExitStack() as ctx:
        s = Space(nc, ctx, "mixo")
        m_hi, m_lo = (s.sb(n, [P, KT, T], F32R) for n in ("m_hi", "m_lo"))
        yT = s.sb("yT", [P, T])
        xb, yb = (s.sb(n, [P, 2, TOKEN_TILES, P]) for n in ("xb", "yb"))
        sq = s.sb("sq", [P, TOKEN_TILES, P])
        acc = [[s.ps(f"acc{u}{c}", [P, 512]) for c in range(NCHUNK)] for u in range(2)]
        back = [s.ps(f"back{u}", [P, 512]) for u in range(2)]
        w_loaded, hi_ready, lo_ready, chunk_done, yT_ready, turned, added, squared, summed, sq_zero = (
            s.sem(n) for n in ("w_loaded", "hi_ready", "lo_ready", "chunk_done", "yT_ready", "turned", "added", "squared", "summed", "sq_zero"))
        free_seen = s.sem("free_seen")
        mix_in = [s.sem(f"mix_in{k}") for k in range(4)]
        x_in, y_out = ([s.sem(f"{n}{u}") for u in range(2)] for n in ("x_in", "y_out"))
        xs_in, ys_out = ([s.sem(f"{n}{u}") for u in range(2)] for n in ("xs_in", "ys_out"))
        block = ctx.enter_context(nc.Block())
        w_v = a["w_out"][0].rearrange("(k p) n -> p k n", p=P)
        x_v = a["x_prompt"][0].rearrange("(t p) n -> p t n", p=P)
        y_v = d["y"][0:SEQ].rearrange("(t p) n -> p t n", p=P)
        GROUPS = [(0, 4), (4, 8), (8, 9)]
        LASTT = TOKEN_TILES - 1

        @block.sync
        def _(sp):
            sp.wait_ge(lo_ready, 1)
            sp.dma_start(w_raw[:], w_v[:, :, 0:P]).then_inc(w_loaded, 16)
            for k in range(4):
                cut = slice(4 * k, 4 * k + 4)
                for w, part in enumerate((m_hi, m_lo)):
                    sp.dma_start(part[:, cut].bitcast(F32), d["mix"][w, cut].rearrange("k p n -> p k n")).then_inc(mix_in[k], 16)

            def tile(m, u, i):
                col = sp.snap(m * P) if not isinstance(m, int) else m * P
                if not (isinstance(m, int) and m == MT - 1):
                    after = sp.snap(m * P + P) if not isinstance(m, int) else m * P + P
                    sp.wait_ge(lo_ready, m + 2)
                    sp.sem_inc(free_seen, 1)
                    sp.dma_start(w_raw[:], w_v[:, :, bass.ds(after, P)]).then_inc(w_loaded, 16)
                sp.wait_ge(added, 3 * m + 3)
                sp.sem_inc(free_seen, 1)
                sp.dma_start(xb[:, u, 0:PROMPT_TILES], x_v[:, :, bass.ds(col, P)]).then_inc(x_in[u], 16)
                sp.dma_start(xb[0:DEC, u, LASTT], a["x_sample"][0, :, bass.ds(col, P)]).then_inc(xs_in[u], 16)

            with sp.Fori(0, MT // 2 - 1) as i:
                for u in range(2):
                    tile(sp.snap(2 * i + u), u, i)
            for u in range(2):
                tile(MT - 2 + u, u, MT // 2 - 1)

        @block.scalar
        def _(act):
            act.sem_inc(squared, 1)
            for u in range(2):
                act.sem_inc(y_out[u], 16)
                act.sem_inc(ys_out[u], 16)
            act.sem_inc(yT_ready, 6)

            def split(m, u):
                act.wait_ge(w_loaded, 16 * m + 16)
                act.wait_ge(chunk_done, NCHUNK * m + NCHUNK)
                act.copy(w_hi[:, u], w_raw[:]).then_inc(hi_ready, 1)

            split(0, 0)

            def tile(m, u, i):
                if not (isinstance(m, int) and m == MT - 1):
                    split(m + 1, 1 - u)
                for c in range(NCHUNK):
                    act.wait_ge(chunk_done, NCHUNK * m + (2 * NCHUNK + c + 1))
                    if c == 0:
                        act.wait_ge(turned, 3 * m + 3)
                    act.copy(yT[:, NW * c:NW * c + NW], acc[u][c][:, 0:NW]).then_inc(yT_ready, 1)
                col = act.snap(m * P) if not isinstance(m, int) else m * P
                act.wait_ge(added, 3 * m + 9)
                act.wait_ge(summed, 2 * m + 2)
                act.activation(sq[:, 0:PROMPT_TILES], yb[:, u, 0:PROMPT_TILES], ACT.Square)
                act.activation(sq[0:DEC, LASTT], yb[0:DEC, u, LASTT], ACT.Square).then_inc(squared, 1)
                act.dma_start(y_v[:, :, bass.ds(col, P)], yb[:, u, 0:PROMPT_TILES]).then_inc(y_out[u], 16)
                act.dma_start(d["y"][SEQ:T, bass.ds(col, P)], yb[0:DEC, u, LASTT]).then_inc(ys_out[u], 16)

            with act.Fori(0, MT // 2 - 1) as i:
                for u in range(2):
                    tile(act.snap(2 * i + u), u, i)
            for u in range(2):
                tile(MT - 2 + u, u, MT // 2 - 1)
            for u in range(2):
                act.wait_ge(y_out[u], 16 + 8 * MT)
                act.wait_ge(ys_out[u], 16 + 8 * MT)

        @block.vector
        def _(dve):
            dve.sem_inc(lo_ready, 1)
            dve.sem_inc(added, 6)
            dve.sem_inc(summed, 2)

            def split(m, u):
                dve.wait_ge(hi_ready, m + 1)
                dve.tensor_tensor(w_lo[:, u], w_raw[:], w_hi[:, u].bitcast(F32), ALU.subtract).then_inc(lo_ready, 1)

            split(0, 0)

            def tile(m, u, i):
                if not (isinstance(m, int) and m == MT - 1):
                    split(m + 1, 1 - u)
                dve.wait_ge(x_in[u], 16 * i + 16)
                dve.wait_ge(xs_in[u], 16 * i + 16)
                dve.wait_ge(y_out[u], 16 * i + 16)
                dve.wait_ge(ys_out[u], 16 * i + 16)
                for g, (t0, t1) in enumerate(GROUPS):
                    dve.wait_ge(turned, 3 * m + (g + 4))
                    rows = DEC if g == 2 else P
                    dve.tensor_tensor(yb[0:rows, u, t0:t1], back[g % 2][0:rows, 0:P * (t1 - t0)].rearrange("p (t n) -> p t n", n=P),
                                      xb[0:rows, u, t0:t1], ALU.add).then_inc(added, 1)
                dve.wait_ge(squared, m + 2)
                mm = bass.ds(m, 1)
                dve.tensor_reduce(ssq[:, 0:PROMPT_TILES, mm].rearrange("p t m -> p (t m)"), sq[:, 0:PROMPT_TILES], AX.X, ALU.add).then_inc(summed, 1)
                dve.tensor_reduce(ssq[0:DEC, LASTT, mm], sq[0:DEC, LASTT], AX.X, ALU.add).then_inc(summed, 1)

            with dve.Fori(0, MT // 2 - 1) as i:
                for u in range(2):
                    tile(dve.snap(2 * i + u), u, i)
            for u in range(2):
                tile(MT - 2 + u, u, MT // 2 - 1)

        @block.tensor
        def _(pe):
            pe.sem_inc(chunk_done, 2 * NCHUNK)
            pe.sem_inc(turned, 3)

            def turn_back(m):
                for g, (t0, t1) in enumerate(GROUPS):
                    if g == 0:
                        pe.wait_ge(yT_ready, NCHUNK * m + (6 + NCHUNK))
                    pe.wait_ge(added, 3 * m + (6 if g < 2 else 7))
                    for j, t in enumerate(range(t0, t1)):
                        n = DEC if t == LASTT else P
                        last = pe.transpose(back[g % 2][0:n, P * j:P * j + P], yT[:, P * t:P * t + n], ident[:])
                    last.then_inc(turned, 1)

            def products(m, u, i):
                pe.wait_ge(lo_ready, m + 2)
                pe.wait_ge(yT_ready, NCHUNK * m + NCHUNK)
                for c in range(NCHUNK):
                    cut = slice(NW * c, NW * c + NW)
                    for k in range(KT):
                        if isinstance(m, int) and m == 0 and c == 0 and k % 4 == 0:
                            pe.wait_ge(mix_in[k // 4], 32)
                        for x, (w, h) in enumerate(((w_hi, m_hi), (w_hi, m_lo), (w_lo, m_hi))):
                            last = pe.matmul(acc[u][c][:, 0:NW], w[:, u, k], h[:, k, cut],
                                             start=(k == 0 and x == 0), stop=(k == KT - 1 and x == 2))
                    last.then_inc(chunk_done, 1)

            products(0, 0, 0)
            with pe.Fori(0, MT // 2 - 1) as i:
                for u in range(2):
                    products(2 * i + (u + 1), 1 - u, i)
                    turn_back(2 * i + u)
            products(MT - 1, 1, 0)
            turn_back(MT - 2)
            turn_back(MT - 1)


def finish(nc, a, d, ssq, out):
    with ExitStack() as ctx:
        s = Space(nc, ctx, "fin")
        y = s.sb("y", [P, TOKEN_TILES, D_MODEL])
        gain = s.sb("gain", [P, D_MODEL])
        mean, rstd, mhalf = (s.sb(n, [P, TOKEN_TILES]) for n in ("mean", "rstd", "mhalf"))
        y_in = [s.sem(f"y_in{t}") for t in range(TOKEN_TILES)]
        gain_in, ready, pooled, normed, stored = (s.sem(n) for n in ("gain_in", "ready", "pooled", "normed", "stored"))
        block = ctx.enter_context(nc.Block())
        rows = [P] * PROMPT_TILES + [DEC]

        @block.sync
        def _(sp):
            for t, n in enumerate(rows):
                sp.dma_start(y[0:n, t], d["y"][P * t:P * t + n]).then_inc(y_in[t], 16)

        @block.scalar
        def _(act):
            act.dma_start(gain[:], a["ln_final_w"].rearrange("(o n) -> o n", o=1).to_broadcast([P, D_MODEL])).then_inc(gain_in, 16)
            for t, n in enumerate(rows):
                act.wait_ge(normed, t + 1)
                dst = out["y_prompt"][0, P * t:P * t + P] if t < PROMPT_TILES else out["y_sample"][0]
                act.dma_start(dst, y[0:n, t]).then_inc(stored, 16)
            act.wait_ge(stored, 16 * TOKEN_TILES)

        @block.gpsimd
        def _(pool):
            pool.memset(mhalf[:], -0.5).then_inc(pooled, 1)
            pool.wait_ge(pooled, 1)
            pool.wait_ge(ready, 4)
            pool.tensor_tensor(rstd[:], mean[:], mhalf[:], ALU.pow).then_inc(pooled, 1)

        @block.vector
        def _(dve):
            dve.memset(mean[:], 1.0).then_inc(ready, 1)
            dve.wait_ge(ready, 1)
            dve.tensor_reduce(mean[:, 0:PROMPT_TILES], ssq[:, 0:PROMPT_TILES], AX.X, ALU.add).then_inc(ready, 1)
            dve.tensor_reduce(mean[0:DEC, PROMPT_TILES:], ssq[0:DEC, PROMPT_TILES:], AX.X, ALU.add).then_inc(ready, 1)
            dve.wait_ge(ready, 3)
            dve.tensor_scalar(mean[:], mean[:], 1.0 / D_MODEL, EPS, ALU.mult, ALU.add).then_inc(ready, 1)
            dve.wait_ge(pooled, 2)
            dve.wait_ge(gain_in, 16)
            for t, n in enumerate(rows):
                dve.wait_ge(y_in[t], 16)
                dve.scalar_tensor_tensor(y[0:n, t], y[0:n, t], rstd[0:n, t:t + 1], gain[0:n], ALU.mult, ALU.mult).then_inc(normed, 1)


def mix_and_finish(nc, a, d, ident, out):
    with ExitStack() as ctx:
        s = Space(nc, ctx, "outp")
        ssq = s.sb("ssq", [P, TOKEN_TILES, D_MODEL // P])
        with ExitStack() as inner:
            w = Space(nc, inner, "outw")
            w_raw = w.sb("w_raw", [P, KT, P])
            w_hi, w_lo = (w.sb(n, [P, 2, KT, P], F32R) for n in ("w_hi", "w_lo"))
            project_out(nc, a, d, ident, ssq, w_hi, w_lo, w_raw)
        finish(nc, a, d, ssq, out)


def streaming_step(nc, a, out):
    d = {"qkv": nc.dram_tensor("scratch_qkv", (QKV_TILES, P, CONV), F32).ap(),
         "gate": nc.dram_tensor("scratch_gate", (2 * HEADS, P, T), F32).ap(),
         "latent": nc.dram_tensor("scratch_latent", (2 * C_TILES, P, T), F32).ap(),
         "bakr": nc.dram_tensor("scratch_bakr", (BAKR, T), F32).ap(),
         "mix": nc.dram_tensor("scratch_mix", (2, 2 * HEADS, P, T), F32).ap(),
         "y": nc.dram_tensor("scratch_y", (T, D_MODEL), F32).ap()}
    with ExitStack() as ctx:
        s = Space(nc, ctx, "all")
        cols = s.sb("cols", [P, 2, P])
        ident = s.sb("ident", [P, P])
        with ExitStack() as inner:
            h = Space(nc, inner, "h")
            hn_hi, hn_lo = (h.sb(n, [P, KT, T], F32R) for n in ("hn_hi", "hn_lo"))
            normalise_inputs(nc, a, hn_hi, hn_lo, cols, ident)
            project(nc, a, d, hn_hi, hn_lo, cols, ident, out)
        delta_rule(nc, a, d, cols, ident, out)
        attend(nc, a, d, cols, ident, out)
        mix_and_finish(nc, a, d, ident, out)


INPUTS = ["x_prompt", "x_sample", "cache_mla_latent", "cache_mla_krope", "state_gdn_conv", "state_gdn_ssm", "ln_in_w", "w_in",
          "w_conv", "a_log", "dt_bias", "gdn_norm_w", "q_norm_w", "w_q_up", "kv_norm_w", "w_uk", "w_uv", "w_out", "ln_final_w"]
OUTPUTS = [("y_prompt", (1, SEQ, D_MODEL)), ("y_sample", (1, DEC, D_MODEL)),
           ("new_conv_prompt", (1, 1, PRE, QKV)), ("new_ssm_prompt", (1, 1, HEADS, P, P)),
           ("new_latent_prompt", (1, 1, SEQ, LORA)), ("new_krope_prompt", (1, 1, SEQ, ROPE)),
           ("new_conv_sample", (1, 1, PRE, QKV)), ("new_ssm_sample", (1, 1, HEADS, P, P)),
           ("new_latent_sample", (1, 1, DEC, LORA)), ("new_krope_sample", (1, 1, DEC, ROPE))]


def kernel(**inputs):
    import numpy as np
    import concourse.bacc as bacc
    from concourse.bass_utils import run_bass_kernel_spmd

    nc = bacc.Bacc("TRN2", target_bir_lowering=False, num_devices=1)
    arrays = {f"in_{n}": np.ascontiguousarray(inputs[n]) for n in INPUTS}
    arrays.update({f"in_{n}": v for n, v in (masks() | rotation()).items()})
    a = {n[3:]: nc.dram_tensor(n, v.shape, F32, kind="ExternalInput").ap() for n, v in arrays.items()}
    out = {n: nc.dram_tensor(f"out_{n}", shape, F32, kind="ExternalOutput").ap() for n, shape in OUTPUTS}
    streaming_step(nc, a, out)
    r = run_bass_kernel_spmd(nc, [arrays], core_ids=[0])
    return tuple(r.results[0][f"out_{n}"] for n, _ in OUTPUTS)
```

```python
import concourse.bass as bass
from concourse import mybir
from concourse.alu_op_type import AluOpType as ALU
from contextlib import ExitStack

F32 = mybir.dt.float32
F32R = mybir.dt.float32r
ACT = mybir.ActivationFunctionType
AX = mybir.AxisListType

P = 128
D_MODEL = 2048
SEQ = 1024
DEC = 32
PAST = 256
T = SEQ + DEC
EPS = 1e-6
HEADS = 8
CONV_W = 4
QKV = 3 * HEADS * P
LORA = 512
ROPE = 64
KT = D_MODEL // P
PROMPT_TILES = SEQ // P
TOKEN_TILES = PROMPT_TILES + 1
NCHUNK = 3
NW = T // NCHUNK
QKV_TILES = QKV // P
Z_G0 = QKV
BA0 = Z_G0 + HEADS * P
CQ0 = BA0 + 2 * HEADS
CKV0 = CQ0 + LORA
KR0 = CKV0 + LORA
Z_M0 = KR0 + ROPE
BAKR = ROPE + 2 * HEADS
C_TILES = LORA // P
PRE = CONV_W - 1
ROW = PRE + SEQ + PRE + DEC
CONV = ROW - PRE
SAMPLE_AT = SEQ + PRE
R_CONV, R_LN, R_QN, R_KVN, R_GN = 0, 96, 112, 116, 120
PARAMS = 121


class Space:

    def __init__(self, nc, ctx, tag):
        self.nc, self.ctx, self.tag = nc, ctx, tag

    def sb(self, name, shape, dt=F32):
        return self.ctx.enter_context(self.nc.sbuf_tensor(f"{self.tag}_{name}", shape, dt))

    def ps(self, name, shape):
        return self.ctx.enter_context(self.nc.psum_tensor(f"{self.tag}_{name}", shape, F32))

    def sem(self, name):
        return self.ctx.enter_context(self.nc.semaphore(f"{self.tag}_{name}"))


def normalise_inputs(nc, a, hn_hi, hn_lo, cols, ident):
    with ExitStack() as ctx:
        s = Space(nc, ctx, "norm")
        x = s.sb("x", [P, 2, D_MODEL])
        xs = s.sb("xs", [P, 2, D_MODEL])
        sq = s.sb("sq", [P, D_MODEL])
        ss = s.sb("ss", [P, 2])
        var = s.sb("var", [P, 2])
        rstd = s.sb("rstd", [P, 2])
        mhalf = s.sb("mhalf", [P, 1])
        hn = s.sb("hn", [P, 4, 4 * P])
        rows = s.sb("rows", [P, 2, P])
        pt = [s.ps(f"pt{i}", [P, 512]) for i in range(8)]
        rows_in, x_free, squared, var_ready, rstd_ready, scaled = (
            s.sem(n) for n in ("rows_in", "x_free", "squared", "var_ready", "rstd_ready", "scaled"))
        x_in = [s.sem(f"x_in{u}") for u in range(2)]
        quarter_T, weighted, hi_ready, lo_ready, params_T, params_in, consts = (
            s.sem(n) for n in ("quarter_T", "weighted", "hi_ready", "lo_ready", "params_T", "params_in", "consts"))
        block = ctx.enter_context(nc.Block())

        @block.sync
        def _(sp):
            loads = [(ident[:], a["ident"]),
                     (rows[R_CONV:R_LN, 0], a["w_conv"].rearrange("d i (j p) -> (d i j) p", p=P)),
                     (rows[R_LN:R_QN, 0], a["ln_in_w"].rearrange("d (j p) -> (d j) p", p=P)),
                     (rows[R_QN:R_KVN, 0], a["q_norm_w"].rearrange("d (j p) -> (d j) p", p=P)),
                     (rows[R_KVN:R_GN, 0], a["kv_norm_w"].rearrange("d (j p) -> (d j) p", p=P)),
                     (rows[R_GN:PARAMS, 0], a["gdn_norm_w"]),
                     (rows[0:PRE * QKV_TILES, 1], a["state_gdn_conv"].rearrange("d b i (j p) -> (d b i j) p", p=P))]
            for dst, src in loads:
                sp.dma_start(dst, src).then_inc(rows_in, 16)
            with sp.Fori(0, PROMPT_TILES // 2) as i:
                for u in range(2):
                    t = sp.snap(2 * i + u)
                    sp.wait_ge(x_free, t + 1)
                    sp.dma_start(x[:, u], a["x_prompt"][0, bass.ts(t, P), :]).then_inc(x_in[u], 16)
            sp.wait_ge(x_free, PROMPT_TILES + 1)
            sp.dma_start(x[0:DEC, 0], a["x_sample"][0]).then_inc(x_in[0], 16)

        @block.gpsimd
        def _(pool):
            pool.memset(mhalf[:], -0.5).then_inc(consts, 1)
            pool.wait_ge(consts, 1)

            def tile(t, u, n):
                pool.wait_ge(var_ready, t + 1)
                pool.tensor_tensor(rstd[0:n, u:u + 1], var[0:n, u:u + 1], mhalf[0:n], ALU.pow).then_inc(rstd_ready, 1)

            with pool.Fori(0, PROMPT_TILES // 2) as i:
                for u in range(2):
                    tile(2 * i + u, u, P)
            tile(PROMPT_TILES, 0, DEC)

        @block.scalar
        def _(act):
            act.sem_inc(x_free, 2)
            act.wait_ge(params_T, 1)
            act.copy(cols[:, 0, 0:PARAMS], pt[0][:, 0:PARAMS])
            act.copy(cols[:, 1, 0:PRE * QKV_TILES], pt[1][:, 0:PRE * QKV_TILES]).then_inc(params_in, 1)

            def rows_of(t, u, x_arrived, n):
                act.wait_ge(x_in[u], x_arrived)
                act.wait_ge(scaled, t + 1)
                act.activation(sq[0:n], x[0:n, u], ACT.Square, accum_out=ss[0:n, u:u + 1]).then_inc(squared, 1)
                act.wait_ge(rstd_ready, t + 1)
                act.wait_ge(quarter_T, 4 * t + 4)
                act.activation(xs[0:n, u], x[0:n, u], ACT.Copy, scale=rstd[0:n, u:u + 1]).then_inc(scaled, 1)
                act.wait_ge(scaled, t + 2)
                act.sem_inc(x_free, 1)

            def high(t, n):
                for q in range(4):
                    act.wait_ge(weighted, 4 * t + (q + 9))
                    act.copy(hn_hi[:, 4 * q:4 * q + 4, bass.ds(P * t, n)],
                             hn[:, q, :].rearrange("p (k n) -> p k n", k=4)[:, :, 0:n]).then_inc(hi_ready, 1)

            act.sem_inc(scaled, 1)
            rows_of(0, 0, 16, P)
            with act.Fori(0, PROMPT_TILES // 2 - 1) as i:
                for u in range(2):
                    rows_of(act.snap(2 * i + (u + 1)), 1 - u, 16 * i + (16 if u == 0 else 32), P)
                    high(act.snap(2 * i + u), P)
            rows_of(PROMPT_TILES - 1, 1, 16 * (PROMPT_TILES // 2), P)
            high(PROMPT_TILES - 2, P)
            rows_of(PROMPT_TILES, 0, 16 * (PROMPT_TILES // 2 + 1), DEC)
            high(PROMPT_TILES - 1, P)
            high(PROMPT_TILES, DEC)

        @block.vector
        def _(dve):
            dve.wait_ge(params_in, 1)

            def mean(t, u, n):
                dve.wait_ge(squared, t + 1)
                dve.tensor_scalar(var[0:n, u:u + 1], ss[0:n, u:u + 1], 1.0 / D_MODEL, EPS, ALU.mult, ALU.add).then_inc(var_ready, 1)

            def parts(t, u, n):
                def weigh(q):
                    dve.wait_ge(quarter_T, 4 * t + (q + 9))
                    dve.wait_ge(lo_ready, 4 * t + (q + 1))
                    view = hn[:, q, :].rearrange("p (k n) -> p k n", k=4)[:, :, 0:n]
                    w = cols[:, 0, R_LN + 4 * q:R_LN + 4 * q + 4]
                    dve.tensor_tensor(view, pt[4 * u + q][:, :].rearrange("p (k n) -> p k n", k=4)[:, :, 0:n],
                                      w[:, :, None].to_broadcast([P, 4, n]), ALU.mult).then_inc(weighted, 1)

                def low(q):
                    dve.wait_ge(hi_ready, 4 * t + (q + 1))
                    view = hn[:, q, :].rearrange("p (k n) -> p k n", k=4)[:, :, 0:n]
                    cut = (slice(None), slice(4 * q, 4 * q + 4), bass.ds(P * t, n))
                    dve.tensor_tensor(hn_lo[cut], view, hn_hi[cut].bitcast(F32), ALU.subtract).then_inc(lo_ready, 1)

                weigh(0)
                weigh(1)
                for q in range(4):
                    if q < 2:
                        weigh(q + 2)
                    low(q)

            dve.sem_inc(lo_ready, 4)
            dve.sem_inc(weighted, 8)
            mean(0, 0, P)
            with dve.Fori(0, PROMPT_TILES // 2 - 1) as i:
                for u in range(2):
                    mean(dve.snap(2 * i + (u + 1)), 1 - u, P)
                    parts(dve.snap(2 * i + u), u, P)
            mean(PROMPT_TILES - 1, 1, P)
            parts(PROMPT_TILES - 2, 0, P)
            mean(PROMPT_TILES, 0, DEC)
            parts(PROMPT_TILES - 1, 1, P)
            parts(PROMPT_TILES, 0, DEC)

        @block.tensor
        def _(pe):
            pe.wait_ge(rows_in, 16 * 7)
            pe.transpose(pt[0][:, 0:PARAMS], rows[0:PARAMS, 0], ident[0:PARAMS, 0:PARAMS])
            pe.transpose(pt[1][:, 0:PRE * QKV_TILES], rows[0:PRE * QKV_TILES, 1],
                         ident[0:PRE * QKV_TILES, 0:PRE * QKV_TILES]).then_inc(params_T, 1)
            pe.wait_ge(params_in, 1)
            pe.sem_inc(quarter_T, 8)

            def tile(t, u, n):
                pe.wait_ge(scaled, t + 2)
                for q in range(4):
                    for k in range(4):
                        if k == 0:
                            pe.wait_ge(weighted, 4 * t + q + 1)
                        last = pe.transpose(pt[4 * u + q][:, P * k:P * k + n], xs[0:n, u, P * (4 * q + k):P * (4 * q + k + 1)],
                                            ident[0:n, 0:n])
                    last.then_inc(quarter_T, 1)

            with pe.Fori(0, PROMPT_TILES // 2) as i:
                for u in range(2):
                    tile(2 * i + u, u, P)
            tile(PROMPT_TILES, 0, DEC)


def project(nc, a, d, hn_hi, hn_lo, cols, ident, out):
    PAIRS = [(QKV_TILES // 2, "qkv"), (HEADS, "gate"), (C_TILES, "latent")]
    TILES = 2 * sum(n for n, _ in PAIRS) + 1

    def each_tile(eng, body):
        first = 1
        for g, (pairs, kind) in enumerate(PAIRS):
            peeled = g == len(PAIRS) - 1
            with eng.Fori(0, pairs - peeled) as i:
                for u in range(2):
                    body(kind, i, u, eng.snap(2 * i + (first + u)), (first + u) % 2)
            if peeled:
                for u in range(2):
                    body(kind, pairs - 1, u, 2 * (pairs - 1) + first + u, (first + u) % 2)
            first += 2 * pairs

    def stores(kind, i, u):
        first = {"qkv": 0, "gate": QKV_TILES, "latent": QKV_TILES + 2 * HEADS}[kind]
        return 16 * i + (16 + 16 * ((first + 1 + u) // 2))

    def column(kind, i, u):
        return {"qkv": (2 * i + u) * P,
                "gate": (Z_M0 if u else Z_G0) + i * P,
                "latent": (CKV0 if u else CQ0) + i * P}[kind]

    with ExitStack() as ctx:
        s = Space(nc, ctx, "proj")
        w_raw = s.sb("w_raw", [P, KT, P])
        w_hi = s.sb("w_hi", [P, 2, KT, P], F32R)
        w_lo = s.sb("w_lo", [P, 2, KT, P], F32R)
        pre = s.sb("pre", [P, 2, ROW])
        act_out = s.sb("act_out", [P, 2, CONV])
        tails = s.sb("tails", [P, 2, PRE, QKV_TILES])
        tail_rows = s.sb("tail_rows", [PRE * QKV_TILES, 2, P])
        acc = [[s.ps(f"acc{u}{c}", [P, 512]) for c in range(NCHUNK)] for u in range(2)]
        tailT = s.ps("tailT", [P, 512])
        w_loaded, ba_loaded, hi_ready, lo_ready, chunk_done, evacuated = (
            s.sem(n) for n in ("w_loaded", "ba_loaded", "hi_ready", "lo_ready", "chunk_done", "evacuated"))
        state_in, tail_out, conv_step, conv_done, silu_done, tails_T, tails_in, zeroed = (
            s.sem(n) for n in ("state_in", "tail_out", "conv_step", "conv_done", "silu_done", "tails_T", "tails_in", "zeroed"))
        tails_stored = [s.sem(f"tails_stored{g}") for g in range(2)]
        stored = [s.sem(f"stored{u}") for u in range(2)]
        block = ctx.enter_context(nc.Block())
        w_v = a["w_in"][0].rearrange("(k p) n -> p k n", p=P)

        @block.sync
        def _(sp):
            sp.wait_ge(lo_ready, 1)
            sp.dma_start(w_raw[:, :, 0:ROPE], w_v[:, :, KR0:KR0 + ROPE]).then_inc(w_loaded, 16)
            sp.dma_start(w_raw[:, :, ROPE:BAKR], w_v[:, :, BA0:BA0 + 2 * HEADS]).then_inc(ba_loaded, 16)

            def load(kind, i, u, t, b):
                col = sp.snap(column(kind, i, u)) if not isinstance(i, int) else column(kind, i, u)
                sp.wait_ge(lo_ready, t + 1)
                sp.dma_start(w_raw[:], w_v[:, :, bass.ds(col, P)]).then_inc(w_loaded, 16)

            each_tile(sp, load)
            sp.wait_ge(tails_in, 1)
            for g, name in enumerate(("new_conv_prompt", "new_conv_sample")):
                sp.dma_start(out[name].rearrange("d b i (j p) -> (d b i j) p", p=P), tail_rows[:, g]).then_inc(tails_stored[g], 16)
            for g in range(2):
                sp.wait_ge(tails_stored[g], 16)

        @block.scalar
        def _(act):
            act.sem_inc(evacuated, 2)
            for b in range(2):
                act.sem_inc(stored[b], 16)

            def split(t, b, n=P):
                act.wait_ge(w_loaded, 16 * t + 16)
                act.wait_ge(chunk_done, NCHUNK * t + NCHUNK)
                act.copy(w_hi[:, b, :, 0:n], w_raw[:, :, 0:n]).then_inc(hi_ready, 1)

            def product(t, c):
                act.wait_ge(chunk_done, NCHUNK * t + (2 * NCHUNK + c + 1))

            act.wait_ge(ba_loaded, 16)
            split(0, 0, BAKR)
            split(1, 1)
            for c in range(NCHUNK):
                product(0, c)
                last = act.copy(act_out[0:BAKR, 0, NW * c:NW * c + NW], acc[0][c][0:BAKR, 0:NW])
            last.then_inc(evacuated, 1)
            act.wait_ge(evacuated, 3)
            act.dma_start(d["bakr"], act_out[0:BAKR, 0, 0:T]).then_inc(stored[0], 16)

            def tile(kind, i, u, t, b):
                row = act.snap(2 * i + u) if not isinstance(i, int) else 2 * i + u
                if not (isinstance(t, int) and t == TILES - 1):
                    split(t + 1, 1 - b)
                if kind == "qkv":
                    act.wait_ge(tail_out, t)
                    product(t, 0)
                    act.copy(pre[:, b, PRE:PRE + NW], acc[b][0][:, 0:NW])
                    product(t, 1)
                    act.copy(pre[:, b, PRE + NW:PRE + 2 * NW], acc[b][1][:, 0:NW])
                    product(t, 2)
                    act.copy(pre[:, b, PRE + 2 * NW:PRE + SEQ], acc[b][2][:, 0:SEQ - 2 * NW])
                    act.copy(pre[:, b, PRE + SAMPLE_AT:ROW], acc[b][2][:, SEQ - 2 * NW:NW]).then_inc(evacuated, 1)
                    act.wait_ge(conv_done, t + 2)
                    act.activation(act_out[:, b], act_out[:, b], ACT.Silu).then_inc(silu_done, 1)
                    act.wait_ge(silu_done, t)
                else:
                    act.wait_ge(stored[b], stores(kind, i, u))
                    for c in range(NCHUNK):
                        product(t, c)
                        last = act.activation(act_out[:, b, NW * c:NW * c + NW], acc[b][c][:, 0:NW],
                                              ACT.Silu if kind == "gate" else ACT.Copy)
                    last.then_inc(evacuated, 1)
                    act.wait_ge(evacuated, t + 3)
                n = CONV if kind == "qkv" else T
                act.dma_start(d[kind][bass.ds(row, 1)].rearrange("j p n -> p (j n)"), act_out[:, b, 0:n]).then_inc(stored[b], 16)

            each_tile(act, tile)
            act.wait_ge(stored[0], 16 + 16 * ((TILES + 1) // 2))
            act.wait_ge(stored[1], 16 + 16 * (TILES // 2))
            act.wait_ge(tails_T, 1)
            act.copy(tail_rows[:], tailT[0:PRE * QKV_TILES, 0:2 * P].rearrange("r (g p) -> r g p", g=2)).then_inc(tails_in, 1)

        @block.vector
        def _(dve):
            for u in range(2):
                dve.memset(pre[:, u, 0:PRE], 0.0).then_inc(zeroed, 1)
            dve.sem_inc(lo_ready, 1)
            dve.sem_inc(conv_done, 2)
            dve.wait_ge(zeroed, 2)

            def split(t, b, n=P):
                dve.wait_ge(hi_ready, t + 1)
                dve.tensor_tensor(w_lo[:, b, :, 0:n], w_raw[:, :, 0:n], w_hi[:, b, :, 0:n].bitcast(F32), ALU.subtract).then_inc(lo_ready, 1)

            split(0, 0, BAKR)
            split(1, 1)

            def tile(kind, i, u, t, b):
                if not (isinstance(t, int) and t == TILES - 1):
                    split(t + 1, 1 - b)
                if kind == "qkv":
                    y = act_out[:, b]
                    j = dve.snap(t - 1)
                    w = [cols[:, 0, bass.ds(dve.snap(j + QKV_TILES * n), 1)] for n in range(CONV_W)]
                    dve.wait_ge(evacuated, t + 3)
                    dve.wait_ge(state_in, t)
                    dve.wait_ge(stored[b], stores(kind, i, u))
                    dve.tensor_scalar(y, pre[:, b, 0:CONV], w[0], None, ALU.mult).then_inc(conv_step, 1)
                    for n in range(1, CONV_W):
                        dve.wait_ge(conv_step, (CONV_W - 1) * j + n)
                        ins = dve.scalar_tensor_tensor(y, pre[:, b, n:n + CONV], w[n], y, ALU.mult, ALU.add)
                        ins.then_inc(conv_step if n < CONV_W - 1 else conv_done, 1)

            each_tile(dve, tile)

        @block.gpsimd
        def _(pool):
            pool.sem_inc(tail_out, 2)

            with pool.Fori(0, QKV_TILES // 2) as i:
                for u in range(2):
                    row = pool.snap(2 * i + u)
                    t, b = row + 1, 1 - u
                    pool.wait_ge(conv_done, t)
                    pool.tensor_copy(pre[:, b, PRE + SEQ:PRE + SAMPLE_AT],
                                     cols[:, 1, bass.ds(row, PRE, step=QKV_TILES)]).then_inc(state_in, 1)
                    pool.wait_ge(evacuated, t + 3)
                    for g, at in enumerate((SEQ, ROW - PRE)):
                        last = pool.tensor_copy(tails[:, g, :, bass.ds(row, 1)].rearrange("p i j -> p (i j)"), pre[:, b, at:at + PRE])
                    last.then_inc(tail_out, 1)

        @block.tensor
        def _(pe):
            pe.sem_inc(chunk_done, 2 * NCHUNK)

            def tile(t, b, n=P):
                pe.wait_ge(lo_ready, t + 2)
                pe.wait_ge(evacuated, t + 1)
                for c in range(NCHUNK):
                    cut = slice(NW * c, NW * c + NW)
                    for k in range(KT):
                        for x, (w, h) in enumerate(((w_hi, hn_hi), (w_hi, hn_lo), (w_lo, hn_hi))):
                            last = pe.matmul(acc[b][c][0:n, 0:NW], w[:, b, k, 0:n], h[:, k, cut],
                                             start=(k == 0 and x == 0), stop=(k == KT - 1 and x == 2))
                    last.then_inc(chunk_done, 1)

            tile(0, 0, BAKR)
            each_tile(pe, lambda kind, i, u, t, b: tile(t, b))
            pe.wait_ge(tail_out, QKV_TILES + 2)
            for g in range(2):
                last = pe.transpose(tailT[0:PRE * QKV_TILES, P * g:P * g + P], tails[:, g].rearrange("p i j -> p (i j)"), ident[:])
            last.then_inc(tails_T, 1)


LEVELS = 7


class Steps:

    def __init__(self, sem, names):
        self.sem, self.names, self.next = sem, names, 0

    def begin(self, eng):
        eng.sem_inc(self.sem, 2 * len(self.names))

    def done(self, instruction, name):
        assert self.names[self.next] == name, (name, self.names[self.next])
        self.next = (self.next + 1) % len(self.names)
        instruction.then_inc(self.sem, 1)

    def at(self, c, name, before=0):
        return len(self.names) * c + (len(self.names) * (2 - before) + self.names.index(name) + 1)


class Stages:

    def __init__(self, space, engine, **stages):
        self.stages = {stage: Steps(space.sem(f"{engine}_{stage}"), names) for stage, names in stages.items()}
        self.of = {name: self.stages[stage] for stage, names in stages.items() for name in names}

    def begin(self, eng):
        for steps in self.stages.values():
            steps.begin(eng)

    def done(self, instruction, name):
        self.of[name].done(instruction, name)

    def wait(self, eng, c, name, before=0):
        eng.wait_ge(self.of[name].sem, self.of[name].at(c, name, before))


def decays(nc, a, d, ident, g_all, beta, eg, egl, edl):
    with ExitStack() as ctx:
        s = Space(nc, ctx, "dec")
        W = TOKEN_TILES * HEADS
        ba = s.sb("ba", [2 * HEADS, TOKEN_TILES * P])
        upper = s.sb("upper", [P, P])
        ones = s.sb("ones", [P, P])
        strict = s.sb("strict", [P, P])
        alog = s.sb("alog", [P, HEADS])
        dt = s.sb("dt", [P, HEADS])
        v, neg, e, ln = (s.sb(n, [P, TOKEN_TILES, HEADS]) for n in ("v", "neg", "e", "ln"))
        tok = s.ps("tok", [P, 512])
        cum = s.ps("cum", [P, 512])
        loaded, padded, tok_T, step, act_step, g_ready, cum_done = (
            s.sem(n) for n in ("loaded", "padded", "tok_T", "step", "act_step", "g_ready", "cum_done"))
        block = ctx.enter_context(nc.Block())
        tok_v = tok[:, 0:2 * W].rearrange("p (c x) -> p c x", x=2 * HEADS)

        @block.sync
        def _(sp):
            sp.dma_start(ba[:, 0:T], d["bakr"][ROPE:BAKR]).then_inc(loaded, 16)
            sp.dma_start(upper[:], a["upper"]).then_inc(loaded, 16)
            sp.dma_start(strict[:], a["lower"]).then_inc(loaded, 16)
            sp.dma_start(alog[:], a["a_log"].to_broadcast([P, HEADS])).then_inc(loaded, 16)
            sp.dma_start(dt[:], a["dt_bias"].to_broadcast([P, HEADS])).then_inc(loaded, 16)

        @block.gpsimd
        def _(pool):
            pool.memset(ba[:, T:], 0.0).then_inc(padded, 1)
            pool.memset(ones[:], 1.0).then_inc(padded, 1)

        @block.scalar
        def _(act):
            act.wait_ge(loaded, 80)
            act.activation(alog[:], alog[:], ACT.Exp).then_inc(act_step, 1)
            act.wait_ge(tok_T, 1)
            act.activation(beta[:], tok_v[:, :, 0:HEADS], ACT.Exp, scale=-1.0).then_inc(act_step, 1)
            act.wait_ge(step, 3)
            act.activation(e[:], neg[:], ACT.Exp).then_inc(act_step, 1)
            act.wait_ge(act_step, 3)
            act.activation(ln[:], e[:], ACT.Ln, bias=1.0).then_inc(act_step, 1)
            act.wait_ge(cum_done, 1)
            for k, e_out in enumerate((eg, egl, edl)):
                act.activation(e_out[:], cum[:, W * k:W * k + W].rearrange("p (c h) -> p c h", h=HEADS), ACT.Exp)

        @block.vector
        def _(dve):
            n = [0]

            def chain(ins):
                n[0] += 1
                ins.then_inc(step, 1)
                dve.wait_ge(step, n[0])

            dve.wait_ge(act_step, 2)
            av = tok_v[:, :, HEADS:]
            shape = [P, TOKEN_TILES, HEADS]
            chain(dve.tensor_tensor(v[:], av, dt[:, None, :].to_broadcast(shape), ALU.add))
            chain(dve.tensor_scalar(neg[:], v[:], -1.0, None, ALU.mult))
            chain(dve.tensor_tensor(neg[:], v[:], neg[:], ALU.min))
            chain(dve.tensor_scalar(v[:], v[:], 0.0, None, ALU.max))
            chain(dve.tensor_scalar(beta[:], beta[:], 1.0, None, ALU.add))
            chain(dve.reciprocal(beta[:], beta[:]))
            dve.wait_ge(act_step, 4)
            chain(dve.tensor_tensor(v[:], v[:], ln[:], ALU.add))
            chain(dve.tensor_tensor(v[:], v[:], alog[:, None, :].to_broadcast(shape), ALU.mult))
            chain(dve.tensor_scalar(g_all[:], v[:], -1.0, None, ALU.mult))
            dve.memset(g_all[DEC:2 * DEC, TOKEN_TILES - 1, :], 0.0).then_inc(g_ready, 1)
            dve.memset(g_all[2 * DEC:, TOKEN_TILES - 1, :], 0.0).then_inc(g_ready, 1)

        @block.tensor
        def _(pe):
            pe.wait_ge(loaded, 80)
            pe.wait_ge(padded, 2)
            for c in range(TOKEN_TILES):
                last = pe.transpose(tok[:, 16 * c:16 * c + 16], ba[:, P * c:P * c + P], ident[0:16, 0:16])
            last.then_inc(tok_T, 1)
            pe.wait_ge(g_ready, 2)
            flat = g_all[:].rearrange("p c h -> p (c h)")
            pe.matmul(cum[:, 0:W], upper[:], flat, start=True, stop=True)
            pe.matmul(cum[:, W:2 * W], ones[:], flat, start=True, stop=True)
            pe.matmul(cum[:, 2 * W:3 * W], strict[:], flat, start=True, stop=True).then_inc(cum_done, 1)


def delta_rule(nc, a, d, cols, ident, out):
    with ExitStack() as ctx:
        s = Space(nc, ctx, "gdn")
        CH = [P, TOKEN_TILES, HEADS]
        g_all, beta, eg, egl, edl = (s.sb(n, CH) for n in ("g_all", "beta", "eg", "egl", "edl"))
        decays(nc, a, d, ident, g_all, beta, eg, egl, edl)
        HF = HEADS // 2
        full = [P, HEADS, P]
        qkv = s.sb("qkv", [P, 2, 3 * HEADS, P])
        gate = s.sb("gate", [P, 2, HEADS, P])
        squares = s.sb("squares", [P, 2 * HEADS, P])
        kd, vb, dT, dL, aT, lmat, pc, X, Y, R, y, o, osq = (
            s.sb(n, full) for n in ("kd", "vb", "dT", "dL", "aT", "lmat", "pc", "X", "Y", "R", "y", "o", "osq"))
        C = s.sb("C", [P, 2, HEADS, P])
        mix = s.sb("mix", full)
        mix_hi, mix_lo = (s.sb(n, [P, 2, HEADS, P], F32R) for n in ("mix_hi", "mix_lo"))
        S = s.sb("S", [P, 2, HEADS, P])
        upper, lower = (s.sb(n, [P, P]) for n in ("upper", "lower"))
        gm = s.sb("gm", full)
        level = s.sb("level", [P, LEVELS, P])
        ones = s.sb("ones", [P, 1])
        mhalf = s.sb("mhalf", [P, 2 * HEADS])
        gch, kb, lam, nle, sqc, sq2, oss, var, orr = (
            s.sb(n, [P, HEADS]) for n in ("gch", "kb", "lam", "nle", "sqc", "sq2", "oss", "var", "orr"))
        sse = s.sb("sse", [P, 2 * HEADS])
        rs = s.sb("rs", [P, 2 * HEADS])
        B = [s.ps(f"b{i}", [P, 512]) for i in range(8)]
        bank = lambda i: B[i][:, :].rearrange("p (h n) -> p h n", n=P)
        half = lambda g: slice(HF * g, HF * g + HF)
        G2 = ("0", "1")
        LV = range(1, LEVELS)
        PE = Stages(s, "pe",
                    body=["ssq", "cols0", "rows0", "rows1", "gq2", "gq3", "gq0", "gq1", "cols1", "kT0", "kT1", "Y0_0", "Y0_1"]
                    + [f"{w}{l}_{g}" for l in LV for w in (("P", "YP", "XP") if l < LEVELS - 1 else ("P", "YP")) for g in G2]
                    + [f"{w}{g}" for w in ("kS", "qS", "y", "Ay", "dS") for g in G2],
                    values=["vT0", "vT1"], tail=["oT0", "oT1"])
        DVE = Stages(s, "dve",
                     ahead=["gch"],
                     body=["sse", "kb", "lam", "L0", "L1", "c0_0", "X0_0", "L2", "L3", "c0_1", "X0_1", "kd0", "kd1"]
                     + [f"AT{p}" for p in range(4)]
                     + [f"{w}{l}_{g}" for l in LV for w in (("Y", "X") if l < LEVELS - 1 else ("Y",)) for g in G2]
                     + [f"{w}{g}" for w in ("R", "qe", "o", "S") for g in G2],
                     coefs=["nle0", "nle", "sqc", "sq2"], values=["vb0", "vb1"],
                     tail=["oss", "var0", "var", "orr", "on", "mix0", "mix1", "mix_lo"])
        ACTS = Stages(s, "act",
                      ahead=["squares"],
                      body=["dL0", "dT0", "dT1", "dL1", "Y0_0", "Y0_1"] + [f"P{l}_{g}" for l in LV for g in G2] + ["y0", "y1"],
                      tail=["osq", "mix_hi"])
        POOL = Stages(s, "pool", ahead=["gm"], body=["rs"] + [f"C{l}_{g}" for l in LV for g in G2] + ["aT0", "aT1"], tail=["orms"])
        consts_in, set_up, sample_padded, ssm_out = s.sem("consts_in"), s.sem("set_up"), s.sem("sample_padded"), s.sem("ssm_out")
        qkv_in, gate_in, mix_out = ([s.sem(f"{n}{u}") for u in range(2)] for n in ("qkv_in", "gate_in", "mix_out"))
        block = ctx.enter_context(nc.Block())
        qkv_d = d["qkv"].rearrange("f p n -> p f n")
        gate_d = d["gate"].rearrange("(j z) p n -> z p j n", z=2)[0]
        mix_d = d["mix"][:, 0:HEADS].rearrange("w j p n -> w p j n")
        LAST = PROMPT_TILES

        def each_chunk(eng, chunk):
            prompt = lambda c, u, times: (c, u, times, P, 0)
            sample = (LAST, 0, LAST // 2, DEC, 1)
            chunk(prompt(0, 0, 0), None, prompt(1, 1, 0))
            with eng.Fori(0, LAST // 2 - 1) as i:
                c = [eng.snap(2 * i + k) for k in range(4)]
                times = eng.snap(i + 1)
                chunk(prompt(c[1], 1, i), prompt(c[0], 0, i), prompt(c[2], 0, times))
                chunk(prompt(c[2], 0, times), prompt(c[1], 1, i), prompt(c[3], 1, times))
            chunk(prompt(LAST - 1, 1, LAST // 2 - 1), prompt(LAST - 2, 0, LAST // 2 - 1), sample)
            chunk(sample, prompt(LAST - 1, 1, LAST // 2 - 1), None)

        @block.sync
        def _(sp):
            for dst, src in ((upper, "upper"), (lower, "lower"), (level, "level")):
                sp.dma_start(dst[:], a[src]).then_inc(consts_in, 16)
            sp.dma_start(S[:, 1], a["state_gdn_ssm"][0, 0].rearrange("h k v -> k h v")).then_inc(consts_in, 16)

            def chunk(x, before, after):
                c, u, times, n, stream = x
                ag = c * P
                ag = sp.snap(ag) if not isinstance(ag, int) else ag
                at = ag if not stream else SAMPLE_AT
                PE.wait(sp, c, "qS1", before=2)
                if stream:
                    sp.wait_ge(sample_padded, 1)
                sp.dma_start(qkv[:, u, :, 0:n], qkv_d[:, :, bass.ds(at, n)]).then_inc(qkv_in[u], 16)
                DVE.wait(sp, c, "mix1", before=2)
                sp.dma_start(gate[:, u, :, 0:n], gate_d[:, :, bass.ds(ag, n)]).then_inc(gate_in[u], 16)

            each_chunk(sp, chunk)

        @block.gpsimd
        def _(pool):
            POOL.begin(pool)
            pool.memset(ones[:], 1.0).then_inc(set_up, 1)
            pool.memset(mhalf[:], -0.5).then_inc(set_up, 1)
            pool.memset(S[:, 0], 0.0).then_inc(set_up, 1)
            pool.wait_ge(set_up, 3)
            pool.wait_ge(consts_in, 64)

            def ahead(x):
                DVE.wait(pool, x[0], "gch")
                POOL.done(pool.tensor_tensor(gm[:], lower[:, None, :].to_broadcast(full), gch[:, :, None].to_broadcast(full), ALU.mult), "gm")

            def tail(x):
                DVE.wait(pool, x[0], "var")
                POOL.done(pool.tensor_tensor(orr[:], var[:], mhalf[:, 0:HEADS], ALU.pow), "orms")

            def chunk(x, before, after):
                c, u, times, n, stream = x
                if after and after[4]:
                    PE.wait(pool, after[0], "qS1", before=2)
                    pool.memset(qkv[:, after[1], :, DEC:], 0.0).then_inc(sample_padded, 1)
                DVE.wait(pool, c, "sse")
                POOL.done(pool.tensor_tensor(rs[:], sse[:], mhalf[:], ALU.pow), "rs")
                for l in LV:
                    for g in range(2):
                        if l == 1:
                            DVE.wait(pool, c, f"L{2 * g + 1}")
                        if l >= 3:
                            PE.wait(pool, c, f"P{l - 2}_{g}")
                        POOL.done(pool.tensor_tensor(C[:, l % 2, half(g)], lmat[:, half(g)],
                                                     level[:, l:l + 1, :].to_broadcast([P, HF, P]), ALU.mult), f"C{l}_{g}")
                    if l == 2 and before:
                        tail(before)
                for g in range(2):
                    DVE.wait(pool, c, f"AT{2 * g + 1}")
                    POOL.done(pool.tensor_tensor(aT[:, half(g)], aT[:, half(g)], upper[:, None, :].to_broadcast([P, HF, P]), ALU.mult), f"aT{g}")
                if after:
                    ahead(after)

            ahead((0,))
            each_chunk(pool, chunk)
            tail((LAST,))

        @block.scalar
        def _(act):
            ACTS.begin(act)

            def ahead(x):
                c, u, times, n, stream = x
                act.wait_ge(qkv_in[u], 16 * times + 16)
                ACTS.done(act.activation(squares[:], qkv[:, u, 0:2 * HEADS], ACT.Square), "squares")

            def square_out(x):
                DVE.wait(act, x[0], "o1")
                ACTS.done(act.activation(osq[:], o[:], ACT.Square), "osq")

            def round_mix(x):
                act.wait_ge(mix_out[x[1]], 32 * x[2] + 32)
                DVE.wait(act, x[0], "mix1")
                ACTS.done(act.copy(mix_hi[:, x[1]], mix[:]), "mix_hi")

            def send_mix(x):
                c, u, times, n, stream = x
                at = act.snap(c * P) if not isinstance(c, int) else c * P
                DVE.wait(act, c, "mix_lo")
                for w, part in enumerate((mix_hi, mix_lo)):
                    act.dma_start(mix_d[w, :, :, bass.ds(at, n)], part[:, u, :, 0:n].bitcast(F32)).then_inc(mix_out[u], 16)

            def chunk(x, before, after):
                c, u, times, n, stream = x
                pe = lambda name: PE.wait(act, c, name)
                for kind, bank_at, g in (("cols", 6, 0), ("rows", 2, 0), ("rows", 3, 1), ("cols", 7, 1)):
                    to, name = (dL, f"dL{g}") if kind == "cols" else (dT, f"dT{g}")
                    pe(f"{kind}{g}")
                    ACTS.done(act.activation(to[:, half(g)], bank(bank_at), ACT.Exp), name)
                if before:
                    square_out(before)
                for g in range(2):
                    pe(f"Y0_{g}")
                    ACTS.done(act.copy(Y[:, half(g)], bank(2 + g)), f"Y0_{g}")
                for l in LV:
                    for g in range(2):
                        pe(f"P{l}_{g}")
                        ACTS.done(act.copy(pc[:, half(g)], bank(6 + g)), f"P{l}_{g}")
                    if l == 4 and before:
                        round_mix(before)
                    if l == 5 and before:
                        send_mix(before)
                if after:
                    ahead(after)
                for g in range(2):
                    pe(f"y{g}")
                    ACTS.done(act.copy(y[:, half(g)], bank(6 + g)), f"y{g}")

            for u in range(2):
                act.sem_inc(mix_out[u], 32)
            ahead((0, 0, 0, P, 0))
            each_chunk(act, chunk)
            sample = (LAST, 0, LAST // 2, DEC, 1)
            square_out(sample)
            DVE.wait(act, LAST, "S1")
            for k, name in enumerate(("new_ssm_prompt", "new_ssm_sample")):
                act.dma_start(out[name][0, 0].rearrange("h k v -> k h v"), S[:, k]).then_inc(ssm_out, 16)
            round_mix(sample)
            send_mix(sample)
            act.wait_ge(mix_out[0], 32 * (LAST // 2 + 1) + 32)
            act.wait_ge(mix_out[1], 32 * (LAST // 2) + 32)
            act.wait_ge(ssm_out, 32)

        @block.vector
        def _(dve):
            DVE.begin(dve)
            dve.wait_ge(consts_in, 64)
            dve.wait_ge(set_up, 3)
            row = lambda t, c: t[:, bass.ds(c, 1), :]
            own = lambda c, name: DVE.wait(dve, c, name)

            def ahead(x):
                DVE.done(dve.tensor_copy(gch[:], row(g_all, x[0])[:, 0]), "gch")

            def mean_square(x):
                c = x[0]
                ACTS.wait(dve, c, "osq")
                DVE.done(dve.tensor_reduce(oss[:], osq[:], AX.X, ALU.add), "oss")
                own(c, "oss")
                DVE.done(dve.tensor_tensor(var[:], oss[:], sq2[:], ALU.mult), "var0")
                own(c, "var0")
                DVE.done(dve.tensor_scalar(var[:], var[:], EPS, None, ALU.add), "var")

            def normalise(x):
                c = x[0]
                POOL.wait(dve, c, "orms")
                DVE.done(dve.tensor_tensor(orr[:], orr[:], sqc[:], ALU.mult), "orr")
                own(c, "orr")
                DVE.done(dve.tensor_tensor(o[:], o[:], orr[:, :, None].to_broadcast(full), ALU.mult), "on")

            def gated(x):
                c, u, times, n, stream = x
                dve.wait_ge(gate_in[u], 16 * times + 16)
                for g in range(2):
                    PE.wait(dve, c, f"oT{g}")
                    DVE.done(dve.scalar_tensor_tensor(mix[:, half(g)], bank(g), cols[:, 0, R_GN:R_GN + 1],
                                                      gate[:, u, half(g)], ALU.mult, ALU.mult), f"mix{g}")

            def rest_of_mix(x):
                ACTS.wait(dve, x[0], "mix_hi")
                DVE.done(dve.tensor_tensor(mix_lo[:, x[1]], mix[:], mix_hi[:, x[1]].bitcast(F32), ALU.subtract), "mix_lo")

            def chunk(x, before, after):
                c, u, times, n, stream = x
                pe = lambda name: PE.wait(dve, c, name)
                act = lambda name: ACTS.wait(dve, c, name)
                wide = lambda t, g: t[:, half(g), None].to_broadcast([P, HF, P])
                per = lambda t, g: row(t, c)[:, 0, half(g)][:, :, None].to_broadcast([P, HF, P])
                pair = lambda p: B[(0, 1, 4, 5)[p]][:, :].rearrange("p (h w n) -> p h w n", h=2, w=2)
                pe("ssq")
                DVE.done(dve.tensor_scalar(sse[:], B[7][:, 0:2 * HEADS], EPS, None, ALU.add), "sse")
                POOL.wait(dve, c, "rs")
                DVE.done(dve.tensor_tensor(kb[:], rs[:, HEADS:], row(beta, c)[:, 0], ALU.mult), "kb")
                own(c, "kb")
                DVE.done(dve.tensor_tensor(lam[:], rs[:, HEADS:], kb[:], ALU.mult), "lam")
                own(c, "lam")
                for g in range(2):
                    act(f"dL{g}")
                    for p in (2 * g, 2 * g + 1):
                        pe(f"gq{p}")
                        for h in range(2):
                            k = 2 * p + h
                            last = dve.scalar_tensor_tensor(lmat[:, k], pair(p)[:, h, 1], lam[:, k:k + 1], dL[:, k], ALU.mult, ALU.mult)
                        DVE.done(last, f"L{p}")
                    own(c, f"L{2 * g + 1}")
                    DVE.done(dve.tensor_tensor(X[:, half(g)], lmat[:, half(g)], level[:, 0:1, :].to_broadcast([P, HF, P]), ALU.mult), f"c0_{g}")
                    own(c, f"c0_{g}")
                    DVE.done(dve.tensor_tensor(X[:, half(g)], ident[:, None, :].to_broadcast([P, HF, P]), X[:, half(g)], ALU.subtract), f"X0_{g}")
                for g in range(2):
                    pe(f"kT{g}")
                    DVE.done(dve.tensor_tensor(kd[:, half(g)], bank(6 + g), per(edl, g), ALU.mult), f"kd{g}")
                for p in range(4):
                    act(f"dT{p // 2}")
                    DVE.done(dve.tensor_tensor(aT[:, 2 * p:2 * p + 2], pair(p)[:, :, 0], dT[:, 2 * p:2 * p + 2], ALU.mult), f"AT{p}")
                for l in LV:
                    for g in range(2):
                        pe(f"YP{l}_{g}")
                        if l == 1:
                            act(f"Y0_{g}")
                        else:
                            own(c, f"Y{l - 1}_{g}")
                        DVE.done(dve.tensor_tensor(Y[:, half(g)], Y[:, half(g)], bank(2 + g), ALU.subtract), f"Y{l}_{g}")
                    if l == LEVELS - 1:
                        continue
                    for g in range(2):
                        pe(f"XP{l}_{g}")
                        own(c, f"X{l - 1}_{g}")
                        DVE.done(dve.tensor_tensor(X[:, half(g)], X[:, half(g)], bank(4 + g), ALU.subtract), f"X{l}_{g}")
                    if l == 1:
                        DVE.done(dve.tensor_tensor(nle[:], lam[:], row(eg, c)[:, 0], ALU.mult), "nle0")
                        if before:
                            mean_square(before)
                        own(c, "nle0")
                        DVE.done(dve.tensor_scalar(nle[:], nle[:], -1.0, None, ALU.mult), "nle")
                    if l == 2:
                        if before:
                            normalise(before)
                        DVE.done(dve.tensor_scalar(sqc[:], rs[:, 0:HEADS], float(P) ** -0.5, None, ALU.mult), "sqc")
                        own(c, "sqc")
                        DVE.done(dve.scalar_tensor_tensor(sq2[:], sqc[:], 1.0 / P, sqc[:], ALU.mult, ALU.mult), "sq2")
                    if l == 3 and before:
                        gated(before)
                    if l == 4 and before:
                        rest_of_mix(before)
                    if l == 5:
                        for g in range(2):
                            pe(f"vT{g}")
                            DVE.done(dve.tensor_tensor(vb[:, half(g)], bank(g), wide(kb, g), ALU.mult), f"vb{g}")
                own(c, "nle")
                for g in range(2):
                    own(c, f"vb{g}")
                    pe(f"kS{g}")
                    for h in range(HF):
                        k = HF * g + h
                        last = dve.scalar_tensor_tensor(R[:, k], bank(g)[:, h], nle[:, k:k + 1], vb[:, k], ALU.mult, ALU.add)
                    DVE.done(last, f"R{g}")
                if after:
                    ahead(after)
                for g in range(2):
                    pe(f"qS{g}")
                    DVE.done(dve.tensor_tensor(o[:, half(g)], bank(2 + g), per(eg, g), ALU.mult), f"qe{g}")
                for g in range(2):
                    pe(f"Ay{g}")
                    own(c, f"qe{g}")
                    DVE.done(dve.tensor_tensor(o[:, half(g)], o[:, half(g)], bank(4 + g), ALU.add), f"o{g}")
                for g in range(2):
                    pe(f"dS{g}")
                    for h in range(HF):
                        k = HF * g + h
                        last = dve.scalar_tensor_tensor(S[:, stream, k], S[:, stream, k], row(egl, c)[:, 0, k:k + 1], bank(g)[:, h],
                                                        ALU.mult, ALU.add)
                    DVE.done(last, f"S{g}")

            ahead((0,))
            each_chunk(dve, chunk)
            sample = (LAST, 0, LAST // 2, DEC, 1)
            for step in (mean_square, normalise, gated, rest_of_mix):
                step(sample)

        @block.tensor
        def _(pe):
            PE.begin(pe)
            pe.wait_ge(consts_in, 64)
            pe.wait_ge(set_up, 3)

            def turn_out(x):
                DVE.wait(pe, x[0], "on")
                for g in range(2):
                    for h in range(HF):
                        last = pe.transpose(bank(g)[:, h], o[:, HF * g + h], ident[:])
                    PE.done(last, f"oT{g}")

            def chunk(x, before, after):
                c, u, times, n, stream = x
                dve = lambda name, before=0: DVE.wait(pe, c, name, before)
                act = lambda name, before=0: ACTS.wait(pe, c, name, before)
                pool = lambda name, before=0: POOL.wait(pe, c, name, before)
                q, k, v = (qkv[:, u, HEADS * w:HEADS * w + HEADS] for w in range(3))

                def heads(b, g, lhsT, rhs, name):
                    for h in range(HF):
                        f = HF * g + h
                        last = pe.matmul(bank(b + g)[:, h], lhsT[:, f], rhs[:, f], start=True, stop=True)
                    PE.done(last, f"{name}{g}")

                def turn(b, g, src, name):
                    for h in range(HF):
                        last = pe.transpose(bank(b + g)[:, h], src[:, HF * g + h], ident[:])
                    PE.done(last, f"{name}{g}")

                def columns(g):
                    PE.done(pe.matmul(B[6 + g][:], upper[:], gm[:, half(g)].rearrange("p h n -> p (h n)"), start=True, stop=True), f"cols{g}")

                def scores(p):
                    b = B[(0, 1, 4, 5)[p]]
                    for h in range(2):
                        f = 2 * p + h
                        last = pe.matmul(b[:, 2 * P * h:2 * P * h + 2 * P], k[:, f], qkv[:, u, f:f + HEADS + 1:HEADS], start=True, stop=True)
                    PE.done(last, f"gq{p}")

                pe.wait_ge(qkv_in[u], 16 * times + 16)
                act("squares")
                act("y1", before=1)
                for f in range(2 * HEADS):
                    last = pe.matmul(B[7][:, f:f + 1], squares[:, f], ones[:], start=True, stop=True)
                PE.done(last, "ssq")
                pool("gm")
                columns(0)
                dve("o1", before=1)
                for g in range(2):
                    for h in range(HF):
                        last = pe.matmul(bank(2 + g)[:, h], gm[:, HF * g + h], upper[:], start=True, stop=True)
                    PE.done(last, f"rows{g}")
                scores(2)
                scores(3)
                dve("S1", before=1)
                scores(0)
                scores(1)
                dve("sse")
                columns(1)
                for g in range(2):
                    act(f"dL{g}")
                    turn(6, g, k, "kT")
                for g in range(2):
                    dve(f"X0_{g}")
                    turn(2, g, X, "Y0_")
                for l in LV:
                    for g in range(2):
                        pool(f"C{l}_{g}")
                        if l == 1:
                            act(f"Y0_{g}")
                            dve(f"kd{g}")
                        else:
                            dve(f"Y{l - 1}_{g}")
                            act(f"P{l - 1}_{g}")
                        heads(6, g, C[:, l % 2], Y, f"P{l}_")
                    for g in range(2):
                        act(f"P{l}_{g}")
                        dve(f"X{l - 1}_{g}")
                        heads(2, g, X, pc, f"YP{l}_")
                    if l == LEVELS - 1:
                        continue
                    for g in range(2):
                        if l == 1:
                            dve(f"AT{2 + g}")
                        heads(4, g, pc, X, f"XP{l}_")
                    if l == 3 and before:
                        turn_out(before)
                    if l == 4:
                        for g in range(2):
                            if before:
                                DVE.wait(pe, before[0], f"mix{g}")
                            else:
                                dve(f"AT{g}")
                            turn(0, g, v, "vT")
                for g in range(2):
                    dve(f"vb{g}")
                    dve(f"S{g}", before=1)
                    heads(0, g, k, S[:, stream], "kS")
                for g in range(2):
                    dve(f"Y{LEVELS - 1}_{g}")
                    heads(2, g, q, S[:, stream], "qS")
                for g in range(2):
                    dve(f"R{g}")
                    act(f"P{LEVELS - 1}_{g}")
                    heads(6, g, Y, R, "y")
                for g in range(2):
                    act(f"y{g}")
                    pool(f"aT{g}")
                    heads(4, g, aT, y, "Ay")
                for g in range(2):
                    heads(0, g, kd, y, "dS")

            each_chunk(pe, chunk)
            turn_out((LAST,))


def masks():
    import numpy as np
    i = np.arange(P)
    lower = i[:, None] > i[None, :]
    level = np.zeros((P, LEVELS, P), np.float32)
    for l in range(LEVELS):
        s = 1 << l
        joined = (i[:, None] // (2 * s) == i[None, :] // (2 * s)) & ((i[:, None] // s) % 2 == 1) & ((i[None, :] // s) % 2 == 0)
        level[:, l] = joined
    return {"ident": np.eye(P, dtype=np.float32),
            "upper": (i[:, None] <= i[None, :]).astype(np.float32),
            "lower": lower.astype(np.float32),
            "level": level}


KEYS = T + PAST
PAST_TILES = PAST // P
KCH = 4
KW = KEYS // KCH
KEY_TILES = [(P * b, P) for b in range(PROMPT_TILES)] + [(SEQ, DEC)] + [(T + P * b, P) for b in range(PAST_TILES)]
SCALE = float(P + ROPE) ** -0.5
HIDDEN = -1e30
CHUNK = 64


def latents(nc, a, d, cols, ident, out, cq_hi, cq_lo, kv_hi, kv_lo, kr_hi, kr_lo, cos, sin, turn):
    with ExitStack() as ctx:
        s = Space(nc, ctx, "lat")
        raws = s.sb("raw", [P, 2, C_TILES, T])
        sqs = s.sb("sq", [P, 2, C_TILES, T])
        rstds = s.sb("rstd", [P, 2, T])
        ones = s.sb("ones", [P, P])
        past = s.sb("past", [P, PAST_TILES, LORA])
        past_kr = s.sb("past_kr", [P, PAST_TILES, ROPE])
        rows = s.sb("rows", [P, 2, LORA])
        kr = s.sb("kr", [P, T])
        swapped = s.sb("swapped", [P, T])
        kr_rows = s.sb("kr_rows", [P, TOKEN_TILES, ROPE])
        B = [s.ps(f"b{i}", [P, 512]) for i in range(8)]
        ld, ldk, raw_in = s.sem("ld"), s.sem("ldk"), [s.sem(f"raw_in{w}") for w in range(2)]
        pe_s, act_s, dve_s, ones_s = s.sem("pe"), s.sem("act"), s.sem("dve"), s.sem("ones_s")
        rows_out, kr_out = [s.sem(f"rows_out{u}") for u in range(2)], s.sem("kr_out")
        block = ctx.enter_context(nc.Block())
        latent = d["latent"].rearrange("(j w) p n -> w p j n", w=2)
        tiles = [(P * t, P) for t in range(PROMPT_TILES)] + [(SEQ, DEC)]
        PE_AT = {n: i + 1 for i, n in enumerate(
            ["var0", "var1", "past0", "past1", "turn", "kr_past"] + [f"rows{t}" for t in range(TOKEN_TILES)] + [f"kr_rows{g}" for g in range(2)])}
        ACT_AT = {n: i + 1 for i, n in enumerate(
            ["sq0", "sq1", "rms0", "rms1", "past0", "past1", "kr_past", "krdup", "hi0", "hi1", "krhi"] + [f"rows{t}" for t in range(TOKEN_TILES)]
            + ["kr_rows0", "kr_rows1"])}
        DVE_AT = {n: i + 1 for i, n in enumerate(
            ["mean0", "mean1", "rstd0", "norm0", "rstd1", "norm1", "sin", "cos", "kr", "past0", "past1", "kr_pastlo", "lo0", "lo1", "krlo"])}

        @block.sync
        def _(sp):
            for w in range(2):
                sp.dma_start(raws[:, w], latent[w]).then_inc(raw_in[w], 16)
            for dst, src in ((past[:], a["cache_mla_latent"][0, 0].rearrange("(t p) n -> p t n", p=P)),
                             (past_kr[:], a["cache_mla_krope"][0, 0].rearrange("(t p) n -> p t n", p=P)),
                             (cos[:], a["cos"]), (sin[:], a["sin"]), (turn[:], a["turn"])):
                sp.dma_start(dst, src).then_inc(ld, 16)
            for h in range(2):
                sp.dma_start(kr[ROPE * h:ROPE * h + ROPE], d["bakr"][0:ROPE]).then_inc(ldk, 16)
            for t, (at, n) in enumerate(tiles):
                sp.wait_ge(act_s, ACT_AT[f"rows{t}"])
                dst = out["new_latent_prompt"][0, 0, at:at + n] if t < PROMPT_TILES else out["new_latent_sample"][0, 0]
                sp.dma_start(dst, rows[0:n, t % 2]).then_inc(rows_out[t % 2], 16)
            sp.wait_ge(act_s, ACT_AT["kr_rows1"])
            sp.dma_start(out["new_krope_prompt"][0, 0].rearrange("(t p) n -> p t n", p=P), kr_rows[:, 0:PROMPT_TILES]).then_inc(kr_out, 16)
            sp.dma_start(out["new_krope_sample"][0, 0], kr_rows[0:DEC, PROMPT_TILES]).then_inc(kr_out, 16)
            sp.wait_ge(kr_out, 32)
            sp.wait_ge(rows_out[0], 16 * 5)
            sp.wait_ge(rows_out[1], 16 * 4)

        @block.scalar
        def _(act):
            at = [0]

            def done(ins, name):
                at[0] += 1
                assert ACT_AT[name] == at[0], name
                ins.then_inc(act_s, 1)

            pe = lambda name: act.wait_ge(pe_s, PE_AT[name])
            dve = lambda name: act.wait_ge(dve_s, DVE_AT[name])
            for w in range(2):
                act.wait_ge(raw_in[w], 16)
                done(act.activation(sqs[:, w], raws[:, w], ACT.Square), f"sq{w}")
            for w in range(2):
                dve(f"mean{w}")
                done(act.activation(rstds[:, w], rstds[:, w], ACT.Sqrt), f"rms{w}")
            for x in range(PAST_TILES):
                pe(f"past{x}")
                done(act.copy(kv_hi[:, :, T + P * x:T + P * x + P], B[2 + x][:, :].rearrange("p (k n) -> p k n", k=4)), f"past{x}")
            pe("kr_past")
            done(act.copy(kr_hi[0:ROPE, T:], B[7][0:ROPE, 0:PAST]), "kr_past")
            done(act.copy(kr_hi[ROPE:, T:], B[7][0:ROPE, 0:PAST]), "krdup")
            for w, hi in enumerate((cq_hi, kv_hi)):
                dve(f"norm{w}")
                done(act.copy(hi[:, :, 0:T], raws[:, w]), f"hi{w}")
            dve("kr")
            done(act.copy(kr_hi[:, 0:T], kr[:]), "krhi")
            for t, (_, n) in enumerate(tiles):
                pe(f"rows{t}")
                if t >= 2:
                    act.wait_ge(rows_out[t % 2], 16 * (t // 2))
                done(act.copy(rows[0:n, t % 2], B[t % 2][0:n]), f"rows{t}")
            for g in range(2):
                pe(f"kr_rows{g}")
                if g == 0:
                    done(act.copy(kr_rows[:, 0:PROMPT_TILES], B[0][:, :].rearrange("p (t n) -> p t n", n=ROPE)), "kr_rows0")
                else:
                    done(act.copy(kr_rows[0:DEC, PROMPT_TILES], B[1][0:DEC, 0:ROPE]), "kr_rows1")

        @block.gpsimd
        def _(pool):
            pool.memset(ones[:], 1.0).then_inc(ones_s, 1)

        @block.vector
        def _(dve):
            at = [0]

            def done(ins, name):
                at[0] += 1
                assert DVE_AT[name] == at[0], name
                ins.then_inc(dve_s, 1)

            pe = lambda name: dve.wait_ge(pe_s, PE_AT[name])
            act = lambda name: dve.wait_ge(act_s, ACT_AT[name])
            own = lambda name: dve.wait_ge(dve_s, DVE_AT[name])
            for w in range(2):
                pe(f"var{w}")
                for c in range(NCHUNK):
                    last = dve.tensor_scalar(rstds[:, w, NW * c:NW * c + NW], B[c + 4 * w][:, 0:NW], 1.0 / LORA, EPS, ALU.mult, ALU.add)
                done(last, f"mean{w}")
            for w, norm in enumerate((R_QN, R_KVN)):
                act(f"rms{w}")
                done(dve.reciprocal(rstds[:, w], rstds[:, w]), f"rstd{w}")
                own(f"rstd{w}")
                for k in range(C_TILES):
                    last = dve.scalar_tensor_tensor(raws[:, w, k], raws[:, w, k], cols[:, 0, norm + k:norm + k + 1], rstds[:, w], ALU.mult, ALU.mult)
                done(last, f"norm{w}")
            pe("turn")
            for c in range(NCHUNK):
                cut = slice(NW * c, NW * c + NW)
                last = dve.tensor_tensor(swapped[:, cut], B[4 + c][:, 0:NW], sin[:, cut], ALU.mult)
            done(last, "sin")
            done(dve.tensor_tensor(kr[:], kr[:], cos[:], ALU.mult), "cos")
            own("cos")
            done(dve.tensor_tensor(kr[:], kr[:], swapped[:], ALU.add), "kr")
            for x in range(PAST_TILES):
                act(f"past{x}")
                cut = slice(T + P * x, T + P * x + P)
                done(dve.tensor_tensor(kv_lo[:, :, cut], B[2 + x][:, :].rearrange("p (k n) -> p k n", k=4),
                                       kv_hi[:, :, cut].bitcast(F32), ALU.subtract), f"past{x}")
            act("krdup")
            dve.tensor_tensor(kr_lo[0:ROPE, T:], B[7][0:ROPE, 0:PAST], kr_hi[0:ROPE, T:].bitcast(F32), ALU.subtract)
            done(dve.tensor_tensor(kr_lo[ROPE:, T:], B[7][0:ROPE, 0:PAST], kr_hi[ROPE:, T:].bitcast(F32), ALU.subtract), "kr_pastlo")
            for w, (hi, lo) in enumerate(((cq_hi, cq_lo), (kv_hi, kv_lo))):
                act(f"hi{w}")
                done(dve.tensor_tensor(lo[:, :, 0:T], raws[:, w], hi[:, :, 0:T].bitcast(F32), ALU.subtract), f"lo{w}")
            act("krhi")
            done(dve.tensor_tensor(kr_lo[:, 0:T], kr[:], kr_hi[:, 0:T].bitcast(F32), ALU.subtract), "krlo")

        @block.tensor
        def _(pe):
            at = [0]

            def done(ins, name):
                at[0] += 1
                assert PE_AT[name] == at[0], name
                ins.then_inc(pe_s, 1)

            act = lambda name: pe.wait_ge(act_s, ACT_AT[name])
            dve = lambda name: pe.wait_ge(dve_s, DVE_AT[name])
            pe.wait_ge(ones_s, 1)
            for w in range(2):
                act(f"sq{w}")
                for c in range(NCHUNK):
                    for k in range(C_TILES):
                        last = pe.matmul(B[c + 4 * w][:, 0:NW], ones[:], sqs[:, w, k, NW * c:NW * c + NW], start=(k == 0), stop=(k == C_TILES - 1))
                done(last, f"var{w}")
            dve("mean1")
            pe.wait_ge(ld, 80)
            pe.wait_ge(ldk, 32)
            for x in range(PAST_TILES):
                for k in range(C_TILES):
                    last = pe.transpose(B[2 + x][:, P * k:P * k + P], past[:, x, P * k:P * k + P], ident[:])
                done(last, f"past{x}")
            for c in range(NCHUNK):
                last = pe.matmul(B[4 + c][:, 0:NW], turn[:], kr[:, NW * c:NW * c + NW], start=True, stop=True)
            done(last, "turn")
            for x in range(PAST_TILES):
                last = pe.transpose(B[7][0:ROPE, P * x:P * x + P], past_kr[:, x], ident[:])
            done(last, "kr_past")
            dve("norm1")
            for t, (first, n) in enumerate(tiles):
                if t >= 2:
                    act(f"rows{t - 2}")
                for k in range(C_TILES):
                    last = pe.transpose(B[t % 2][0:n, P * k:P * k + P], raws[:, 1, k, first:first + n], ident[:])
                done(last, f"rows{t}")
            dve("kr")
            act(f"rows{TOKEN_TILES - 1}")
            for t in range(PROMPT_TILES):
                last = pe.transpose(B[0][:, ROPE * t:ROPE * t + ROPE], kr[0:ROPE, P * t:P * t + P], ident[0:ROPE, 0:ROPE])
            done(last, "kr_rows0")
            done(pe.transpose(B[1][0:DEC, 0:ROPE], kr[0:ROPE, SEQ:T], ident[0:ROPE, 0:ROPE]), "kr_rows1")


def attend(nc, a, d, cols, ident, out):
    with ExitStack() as ctx:
        s = Space(nc, ctx, "mla")
        cq_hi, cq_lo = (s.sb(n, [P, C_TILES, T], F32R) for n in ("cq_hi", "cq_lo"))
        kv_hi, kv_lo = (s.sb(n, [P, C_TILES, KEYS], F32R) for n in ("kv_hi", "kv_lo"))
        kr_hi, kr_lo = (s.sb(n, [P, KEYS], F32R) for n in ("kr_hi", "kr_lo"))
        cos, sin = (s.sb(n, [P, T]) for n in ("cos", "sin"))
        turn = s.sb("turn", [P, P])
        latents(nc, a, d, cols, ident, out, cq_hi, cq_lo, kv_hi, kv_lo, kr_hi, kr_lo, cos, sin, turn)
        UNITS = [("qr", None)] + [(x, e) for e in range(2) for x in ("q", "k", "v")]
        U = len(UNITS)
        w_raw = s.sb("w_raw", [P, U, C_TILES, P])
        w_hi, w_lo = (s.sb(n, [P, 2, C_TILES, P], F32R) for n in ("w_hi", "w_lo"))
        q_hi, q_lo, qr_hi, qr_lo = (s.sb(n, [P, T], F32R) for n in ("q_hi", "q_lo", "qr_hi", "qr_lo"))
        k_hi, k_lo = (s.sb(n, [P, KEYS], F32R) for n in ("k_hi", "k_lo"))
        qr = s.sb("qr", [P, T])
        vT = s.sb("vT", [P, KEYS])
        v_tok = s.sb("v_tok", [P, len(KEY_TILES), P])
        probs, pT = (s.sb(n, [P, 2, SEQ]) for n in ("probs", "pT"))
        o_tok = s.sb("o_tok", [P, 2, P])
        gate = s.sb("gate", [P, 2, T])
        mix = s.sb("mix", [P, T])
        mix_hi, mix_lo = (s.sb(n, [P, T], F32R) for n in ("mix_hi", "mix_lo"))
        mx, nm, total, inv = (s.sb(n, [P, 2]) for n in ("mx", "nm", "total", "inv"))
        scores = [s.ps(f"scores{u}", [P, 1024]) for u in range(2)]
        ptp = [s.ps(f"ptp{g}", [P, 512]) for g in range(2)]
        o_ps, oT_ps = s.ps("o", [P, 512]), s.ps("oT", [P, 512])
        chunk_bank = lambda c: scores[c // 2][:, 512 * (c % 2):512 * (c % 2) + 512]
        NT = TOKEN_TILES
        ORDER = [x for pair in zip(range(PROMPT_TILES - 1, 0, -1), range(PROMPT_TILES // 2)) for x in pair]
        TILE = [(P * t, P, list(range(t + 1))) for t in ORDER] + [(SEQ, DEC, list(range(PROMPT_TILES, len(KEY_TILES))))]

        def groups(t):
            at, parts = 0, []
            for b in TILE[t][2]:
                parts.append((b, at, KEY_TILES[b][1]))
                at += KEY_TILES[b][1]
            return [parts[i:i + 4] for i in range(0, len(parts), 4)], at

        def nchunks(x):
            return NCHUNK if x in ("qr", "q") else KCH

        names = {"pe": [], "act": [], "dve": []}

        def unit_names(w):
            x, e = UNITS[w]
            for n in ("act", "dve"):
                names[n] += [f"w{w + 1}"] if w + 1 < U else []
            names["pe"] += [f"u{w}_{c}" for c in range(nchunks(x))]
            if x == "qr":
                names["act"] += [f"raw{w}_{c}" for c in range(NCHUNK)] + ["qr_hi"]
                names["pe"].append("turn")
                names["dve"] += ["sin", "cos", "qr", "qr_lo"]
            elif x == "v":
                names["act"] += [f"raw{w}_{c}" for c in range(KCH)]
                names["pe"] += [f"vt{w}_{g}" for g in range(3)]
                names["dve"] += [f"vt{w}_{g}" for g in range(3)]
            else:
                names["act"] += [f"hi{w}_{c}" for c in range(nchunks(x))]
                names["dve"] += [f"lo{w}_{c}" for c in range(nchunks(x))]

        def attention_names(e):
            for st in range(NT + 3):
                if st < NT:
                    names["pe"].append(f"S{e}_{st}")
                    names["dve"] += ([f"mask{e}_{st}"] if st < PROMPT_TILES else []) + [f"mx{e}_{st}", f"nm{e}_{st}"]
                    names["act"].append(f"E{e}_{st}")
                if 0 <= st - 1 < NT:
                    gs = range(len(groups(st - 1)[0]))
                    names["pe"] += [f"T{e}_{st - 1}_{g}" for g in gs]
                    names["dve"] += [f"T{e}_{st - 1}_0", f"inv{e}_{st - 1}"]
                    if len(gs) > 1:
                        names["act"].append(f"T{e}_{st - 1}_1")
                if 0 <= st - 2 < NT:
                    names["pe"].append(f"O{e}_{st - 2}")
                    names["act"].append(f"O{e}_{st - 2}")
                if 0 <= st - 3 < NT:
                    names["pe"].append(f"OT{e}_{st - 3}")
                    names["dve"].append(f"mix{e}_{st - 3}")
            names["act"].append(f"mix_hi{e}")
            names["dve"].append(f"mix_lo{e}")

        def each_step(unit, attention):
            unit(0)
            for e in range(2):
                for w in range(3 * e + 1, 3 * e + 4):
                    unit(w)
                attention(e)

        each_step(unit_names, attention_names)
        PE, ACTS, DVE = (Steps(s.sem(f"{n}_step"), names[n]) for n in ("pe", "act", "dve"))
        ACT_FIRST, DVE_FIRST = (Steps(s.sem(f"{n}_first"), ["w0"]) for n in ("act", "dve"))
        w_loaded = [s.sem(f"w_loaded{w}") for w in range(U)]
        gate_in, mix_out = [s.sem(f"gate_in{e}") for e in range(2)], s.sem("mix_out")
        passed, free_seen = s.sem("passed"), s.sem("free_seen")
        block = ctx.enter_context(nc.Block())
        q_up = a["w_q_up"][0].rearrange("(k p) h n -> p k h n", p=P)
        uk, uv = (a[n][0].rearrange("(k p) h n -> p k h n", p=P) for n in ("w_uk", "w_uv"))
        TURNS = HEADS // 2

        @block.sync
        def _(sp):
            with sp.Fori(0, TURNS) as i:
                for w, (x, e) in enumerate(UNITS):
                    head = sp.snap(2 * i + (e or 0))
                    both = [sp.snap(2 * i + h) for h in range(2)]
                    split_by = DVE if w else DVE_FIRST
                    sp.wait_ge(split_by.sem, split_by.at(i, f"w{w}", before=1))
                    sp.sem_inc(free_seen, 1)
                    if x == "qr":
                        for h in range(2):
                            sp.dma_start(w_raw[:, w, :, ROPE * h:ROPE * h + ROPE],
                                         q_up[:, :, bass.ds(both[h], 1), P:].rearrange("p k h n -> p k (h n)")).then_inc(w_loaded[w], 16)
                        continue
                    src = {"q": q_up, "k": uk, "v": uv}[x]
                    sp.dma_start(w_raw[:, w], src[:, :, bass.ds(head, 1), 0:P].rearrange("p k h n -> p k (h n)")).then_inc(w_loaded[w], 16)
                for e in range(2):
                    row = sp.snap(4 * i + (2 * e + 1))
                    sp.wait_ge(DVE.sem, DVE.at(i, f"mix{e}_{NT - 1}", before=1))
                    sp.sem_inc(free_seen, 1)
                    sp.dma_start(gate[:, e], d["gate"][bass.ds(row, 1)].rearrange("j p n -> p (j n)")).then_inc(gate_in[e], 16)

        @block.scalar
        def _(act):
            ACTS.begin(act)
            act.sem_inc(mix_out, 32)
            ACT_FIRST.begin(act)

            def split_first(i):
                act.wait_ge(w_loaded[0], 32 * i + 32)
                act.wait_ge(PE.sem, PE.at(i, f"u{U - 1}_{KCH - 1}", before=1))
                ACT_FIRST.done(act.copy(w_hi[:, 0], w_raw[:, 0]), "w0")

            def turn(i, last_turn):
                pe = lambda name, before=0: act.wait_ge(PE.sem, PE.at(i, name, before))
                dve = lambda name, before=0: act.wait_ge(DVE.sem, DVE.at(i, name, before))

                def split(w):
                    act.wait_ge(w_loaded[w], 16 * i + 16)
                    before = w - 2 if w >= 2 else U - 1 - w
                    pe(f"u{before}_{nchunks(UNITS[before][0]) - 1}", 0 if w >= 2 else 1)
                    ACTS.done(act.copy(w_hi[:, w % 2], w_raw[:, w]), f"w{w}")

                def unit(w):
                    x, e = UNITS[w]
                    if w + 1 < U:
                        split(w + 1)
                    for c in range(nchunks(x)):
                        pe(f"u{w}_{c}")
                        n = NW if x in ("qr", "q") else KW
                        cut = slice(n * c, n * c + n)
                        dst = {"qr": qr, "q": q_hi, "k": k_hi, "v": vT}[x]
                        ACTS.done(act.copy(dst[:, cut], chunk_bank(c)[:, 0:n]), f"{'raw' if x in ('qr', 'v') else 'hi'}{w}_{c}")
                    if x == "qr":
                        dve("qr")
                        ACTS.done(act.copy(qr_hi[:], qr[:]), "qr_hi")

                def attention(e):
                    for st in range(NT + 3):
                        if e == 1 and st == 3 and not last_turn:
                            split_first(i + 1)
                        if st < NT:
                            t, n = st, TILE[st][1]
                            width = groups(t)[1]
                            dve(f"nm{e}_{t}")
                            ACTS.done(act.activation(probs[0:n, t % 2, 0:width], scores[t % 2][0:n, 0:width], ACT.Exp,
                                                     bias=nm[0:n, t % 2:t % 2 + 1], scale=SCALE,
                                                     accum_out=total[0:n, t % 2:t % 2 + 1]), f"E{e}_{t}")
                        t = st - 1
                        if 0 <= t < NT and len(groups(t)[0]) > 1:
                            pe(f"T{e}_{t}_1")
                            k = sum(x[2] for x in groups(t)[0][1])
                            ACTS.done(act.copy(pT[:, t % 2, 512:512 + k], ptp[1][:, 0:k]), f"T{e}_{t}_1")
                        t = st - 2
                        if 0 <= t < NT:
                            n = TILE[t][1]
                            pe(f"O{e}_{t}")
                            dve(f"inv{e}_{t}")
                            ACTS.done(act.activation(o_tok[0:n, t % 2], o_ps[0:n, 0:P], ACT.Copy, scale=inv[0:n, t % 2:t % 2 + 1]), f"O{e}_{t}")
                    row = 2 * i + (HEADS + e)
                    row = row if last_turn else act.snap(row)
                    dve(f"mix{e}_{NT - 1}")
                    act.wait_ge(mix_out, 64 * i + (32 * e + 32))
                    ACTS.done(act.copy(mix_hi[:], mix[:]), f"mix_hi{e}")
                    dve(f"mix_lo{e}")
                    for w, part in enumerate((mix_hi, mix_lo)):
                        act.dma_start(d["mix"][w, bass.ds(row, 1)].rearrange("j p n -> p (j n)"), part[:].bitcast(F32)).then_inc(mix_out, 16)

                each_step(unit, attention)

            split_first(0)
            with act.Fori(0, TURNS - 1) as i:
                turn(i, False)
            turn(TURNS - 1, True)
            act.wait_ge(mix_out, 64 * TURNS + 32)

        @block.vector
        def _(dve):
            DVE.begin(dve)
            DVE_FIRST.begin(dve)

            def split_first(i):
                dve.wait_ge(ACT_FIRST.sem, ACT_FIRST.at(i, "w0"))
                DVE_FIRST.done(dve.tensor_tensor(w_lo[:, 0], w_raw[:, 0], w_hi[:, 0].bitcast(F32), ALU.subtract), "w0")

            def turn(i, last_turn):
                pe = lambda name, before=0: dve.wait_ge(PE.sem, PE.at(i, name, before))
                act = lambda name, before=0: dve.wait_ge(ACTS.sem, ACTS.at(i, name, before))
                own = lambda name, before=0: dve.wait_ge(DVE.sem, DVE.at(i, name, before))

                def split(w):
                    act(f"w{w}")
                    DVE.done(dve.tensor_tensor(w_lo[:, w % 2], w_raw[:, w], w_hi[:, w % 2].bitcast(F32), ALU.subtract), f"w{w}")

                def unit(w):
                    x, e = UNITS[w]
                    if w + 1 < U:
                        split(w + 1)
                    if x == "qr":
                        pe("turn")
                        for c in range(NCHUNK):
                            cut = slice(NW * c, NW * c + NW)
                            bank = (ptp[0], ptp[1], o_ps)[c]
                            last = dve.tensor_tensor(vT[:, cut], bank[:, 0:NW], sin[:, cut], ALU.mult)
                        DVE.done(last, "sin")
                        DVE.done(dve.tensor_tensor(qr[:], qr[:], cos[:], ALU.mult), "cos")
                        own("cos")
                        DVE.done(dve.tensor_tensor(qr[:], qr[:], vT[:, 0:T], ALU.add), "qr")
                        act("qr_hi")
                        DVE.done(dve.tensor_tensor(qr_lo[:], qr[:], qr_hi[:].bitcast(F32), ALU.subtract), "qr_lo")
                    elif x == "v":
                        for g in range(3):
                            pe(f"vt{w}_{g}")
                            tiles = list(range(len(KEY_TILES)))[4 * g:4 * g + 4]
                            b = ptp[g % 2][:, 0:P * len(tiles)].rearrange("p (t n) -> p t n", n=P)
                            if PROMPT_TILES in tiles:
                                dve.tensor_copy(v_tok[0:DEC, tiles[0]], b[0:DEC, 0])
                                DVE.done(dve.tensor_copy(v_tok[:, tiles[1]:tiles[-1] + 1], b[:, 1:]), f"vt{w}_{g}")
                            else:
                                DVE.done(dve.tensor_copy(v_tok[:, tiles[0]:tiles[-1] + 1], b), f"vt{w}_{g}")
                    else:
                        n = NW if x == "q" else KW
                        for c in range(nchunks(x)):
                            cut = slice(n * c, n * c + n)
                            hi, lo = (q_hi, q_lo) if x == "q" else (k_hi, k_lo)
                            act(f"hi{w}_{c}")
                            DVE.done(dve.tensor_tensor(lo[:, cut], chunk_bank(c)[:, 0:n], hi[:, cut].bitcast(F32), ALU.subtract), f"lo{w}_{c}")

                def attention(e):
                    for st in range(NT + 3):
                        if e == 1 and st == 3 and not last_turn:
                            split_first(i + 1)
                        if st < NT:
                            t, n = st, TILE[st][1]
                            width = groups(t)[1]
                            pe(f"S{e}_{t}")
                            if t < PROMPT_TILES:
                                DVE.done(dve.memset(scores[t % 2][0:CHUNK, width - CHUNK:width], HIDDEN), f"mask{e}_{t}")
                                own(f"mask{e}_{t}")
                            DVE.done(dve.tensor_reduce(mx[0:n, t % 2:t % 2 + 1], scores[t % 2][0:n, 0:width], AX.X, ALU.max), f"mx{e}_{t}")
                            own(f"mx{e}_{t}")
                            DVE.done(dve.tensor_scalar(nm[0:n, t % 2:t % 2 + 1], mx[0:n, t % 2:t % 2 + 1], -SCALE, None, ALU.mult), f"nm{e}_{t}")
                        t = st - 1
                        if 0 <= t < NT:
                            n = TILE[t][1]
                            pe(f"T{e}_{t}_0")
                            if t < PROMPT_TILES:
                                k = P * len(groups(t)[0][0])
                                last = dve.tensor_copy(pT[:, t % 2, 0:k], ptp[0][:, 0:k])
                            else:
                                dve.tensor_copy(pT[0:DEC, t % 2, 0:DEC], ptp[0][0:DEC, 0:DEC])
                                last = dve.tensor_copy(pT[:, t % 2, P:3 * P].rearrange("p (b n) -> p b n", n=P)[:, :, 0:DEC],
                                                       ptp[0][:, P:3 * P].rearrange("p (b n) -> p b n", n=P)[:, :, 0:DEC])
                            DVE.done(last, f"T{e}_{t}_0")
                            act(f"E{e}_{t}")
                            if t >= 2:
                                act(f"O{e}_{t - 2}")
                            DVE.done(dve.reciprocal(inv[0:n, t % 2:t % 2 + 1], total[0:n, t % 2:t % 2 + 1]), f"inv{e}_{t}")
                        t = st - 3
                        if 0 <= t < NT:
                            first, n, _ = TILE[t]
                            pe(f"OT{e}_{t}")
                            if t == 0:
                                dve.wait_ge(gate_in[e], 16 * i + 16)
                            DVE.done(dve.tensor_tensor(mix[:, first:first + n], oT_ps[:, 0:n], gate[:, e, first:first + n], ALU.mult), f"mix{e}_{t}")

                    act(f"mix_hi{e}")
                    DVE.done(dve.tensor_tensor(mix_lo[:], mix[:], mix_hi[:].bitcast(F32), ALU.subtract), f"mix_lo{e}")

                each_step(unit, attention)

            split_first(0)
            with dve.Fori(0, TURNS - 1) as i:
                turn(i, False)
            turn(TURNS - 1, True)

        @block.tensor
        def _(pe):
            PE.begin(pe)
            with pe.Fori(0, TURNS) as i:
                dve = lambda name, before=0: pe.wait_ge(DVE.sem, DVE.at(i, name, before))
                act = lambda name, before=0: pe.wait_ge(ACTS.sem, ACTS.at(i, name, before))
                THREE = ((0, 0), (0, 1), (1, 0))

                def chunk_free(w, c):
                    if w == 0:
                        act(f"E1_{NT - 1}", 1)
                        return
                    if w == 4:
                        act(f"E0_{NT - 1}")
                        return
                    x = UNITS[w - 1][0]
                    if c < nchunks(x):
                        if x in ("qr", "v"):
                            act(f"raw{w - 1}_{c}")
                        else:
                            dve(f"lo{w - 1}_{c}")

                def hold(t):
                    if t == PROMPT_TILES:
                        pe.sem_inc(passed, 1)

                def unit(w):
                    x, e = UNITS[w]
                    if w == 0:
                        pe.wait_ge(DVE_FIRST.sem, DVE_FIRST.at(i, "w0"))
                    else:
                        dve(f"w{w}")
                    n = NW if x in ("qr", "q") else KW
                    hi, lo = (cq_hi, cq_lo) if x in ("qr", "q") else (kv_hi, kv_lo)
                    for c in range(nchunks(x)):
                        chunk_free(w, c)
                        for k in range(C_TILES):
                            for j, (ww, xx) in enumerate(THREE):
                                last = pe.matmul(chunk_bank(c)[:, 0:n], (w_hi, w_lo)[ww][:, w % 2, k], (hi, lo)[xx][:, k, n * c:n * c + n],
                                                 start=(k == 0 and j == 0), stop=(k == C_TILES - 1 and j == 2))
                        PE.done(last, f"u{w}_{c}")
                    if x == "qr":
                        act(f"raw{w}_{NCHUNK - 1}")
                        for c in range(NCHUNK):
                            bank = (ptp[0], ptp[1], o_ps)[c]
                            last = pe.matmul(bank[:, 0:NW], turn[:], qr[:, NW * c:NW * c + NW], start=True, stop=True)
                        PE.done(last, "turn")
                    elif x == "v":
                        act(f"raw{w}_{KCH - 1}")
                        for g in range(3):
                            if g == 2:
                                dve(f"vt{w}_0")
                            if g == 0 and w < 4:
                                dve("sin")
                            if g == 2:
                                hold(PROMPT_TILES)
                            for j, b in enumerate(range(len(KEY_TILES))[4 * g:4 * g + 4]):
                                at, m = KEY_TILES[b]
                                last = pe.transpose(ptp[g % 2][0:m, P * j:P * j + P], vT[:, at:at + m], ident[:])
                            PE.done(last, f"vt{w}_{g}")

                def attention(e):
                    for st in range(NT + 3):
                        if st < NT:
                            t = st
                            first, n, tiles = TILE[t]
                            key0, width = KEY_TILES[tiles[0]][0], groups(t)[1]
                            if t < 2:
                                act(f"raw{3 * e + 3}_{KCH - 1}")
                                if t == 0:
                                    dve(f"vt{3 * e + 3}_2")
                            else:
                                act(f"E{e}_{t - 2}")
                            rope = slice(ROPE * e, ROPE * e + ROPE)
                            hold(t)
                            for c0 in range(0, width, 512):
                                c1 = min(c0 + 512, width)
                                for j, (ww, xx) in enumerate(THREE):
                                    pe.matmul(scores[t % 2][0:n, c0:c1], (q_hi, q_lo)[ww][:, first:first + n],
                                              (k_hi, k_lo)[xx][:, key0 + c0:key0 + c1], start=(j == 0), stop=False)
                                for j, (ww, xx) in enumerate(THREE):
                                    last = pe.matmul(scores[t % 2][0:n, c0:c1], (qr_hi, qr_lo)[ww][rope, first:first + n],
                                                     (kr_hi, kr_lo)[xx][rope, key0 + c0:key0 + c1], start=False, stop=(j == 2))
                            PE.done(last, f"S{e}_{t}")
                        t = st - 1
                        if 0 <= t < NT:
                            n = TILE[t][1]
                            act(f"E{e}_{t}")
                            for g, parts in enumerate(groups(t)[0]):
                                if t > 0:
                                    if g == 0:
                                        dve(f"T{e}_{t - 1}_0")
                                    elif len(groups(t - 1)[0]) > 1:
                                        act(f"T{e}_{t - 1}_1")
                                hold(t)
                                for j, (b, at, m) in enumerate(parts):
                                    last = pe.transpose(ptp[g][0:m, P * j:P * j + n], probs[0:n, t % 2, at:at + m], ident[0:n, 0:n])
                                PE.done(last, f"T{e}_{t}_{g}")
                        t = st - 2
                        if 0 <= t < NT:
                            n = TILE[t][1]
                            dve(f"T{e}_{t}_0")
                            if t > 0:
                                act(f"O{e}_{t - 1}")
                            elif len(groups(t)[0]) > 1:
                                act(f"T{e}_{t}_1")
                            hold(t)
                            parts = [x for g in groups(t)[0] for x in g]
                            for j, (b, at, m) in enumerate(parts):
                                last = pe.matmul(o_ps[0:n, 0:P], pT[0:m, t % 2, P * j:P * j + n], v_tok[0:m, b], start=(j == 0), stop=(j == len(parts) - 1))
                            PE.done(last, f"O{e}_{t}")
                        t = st - 3
                        if 0 <= t < NT:
                            n = TILE[t][1]
                            act(f"O{e}_{t}")
                            if t > 0:
                                dve(f"mix{e}_{t - 1}")
                            hold(t)
                            PE.done(pe.transpose(oT_ps[:, 0:n], o_tok[0:n, t % 2], ident[0:n, 0:n]), f"OT{e}_{t}")

                each_step(unit, attention)


def rotation():
    import numpy as np
    inv = (10000.0 ** (-np.arange(0, ROPE, 2) / ROPE)).astype(np.float32)
    pos = np.concatenate([np.arange(SEQ), PAST + np.arange(DEC)]).astype(np.float32)
    ang = (pos[:, None] * inv[None, :]).astype(np.float32)
    rows = np.tile(ang.T, (4, 1))
    turn = np.zeros((P, P), np.float32)
    for h in range(2):
        for r in range(ROPE // 2):
            turn[ROPE * h + r + ROPE // 2, ROPE * h + r] = -1.0
            turn[ROPE * h + r, ROPE * h + r + ROPE // 2] = 1.0
    return {"cos": np.cos(rows).astype(np.float32), "sin": np.sin(rows).astype(np.float32), "turn": turn}


def project_out(nc, a, d, ident, ssq, w_hi, w_lo, w_raw):
    MT = D_MODEL // P
    with ExitStack() as ctx:
        s = Space(nc, ctx, "mixo")
        m_hi, m_lo = (s.sb(n, [P, KT, T], F32R) for n in ("m_hi", "m_lo"))
        yT = s.sb("yT", [P, T])
        xb, yb = (s.sb(n, [P, 2, TOKEN_TILES, P]) for n in ("xb", "yb"))
        sq = s.sb("sq", [P, TOKEN_TILES, P])
        acc = [[s.ps(f"acc{u}{c}", [P, 512]) for c in range(NCHUNK)] for u in range(2)]
        back = [s.ps(f"back{u}", [P, 512]) for u in range(2)]
        w_loaded, hi_ready, lo_ready, chunk_done, yT_ready, turned, added, squared, summed, sq_zero = (
            s.sem(n) for n in ("w_loaded", "hi_ready", "lo_ready", "chunk_done", "yT_ready", "turned", "added", "squared", "summed", "sq_zero"))
        free_seen = s.sem("free_seen")
        mix_in = [s.sem(f"mix_in{k}") for k in range(NCHUNK)]
        x_in, y_out = ([s.sem(f"{n}{u}") for u in range(2)] for n in ("x_in", "y_out"))
        xs_in, ys_out = ([s.sem(f"{n}{u}") for u in range(2)] for n in ("xs_in", "ys_out"))
        block = ctx.enter_context(nc.Block())
        w_v = a["w_out"][0].rearrange("(k p) n -> p k n", p=P)
        x_v = a["x_prompt"][0].rearrange("(t p) n -> p t n", p=P)
        y_v = d["y"][0:SEQ].rearrange("(t p) n -> p t n", p=P)
        GROUPS = [(0, 4), (4, 8), (8, 9)]
        LASTT = TOKEN_TILES - 1

        @block.sync
        def _(sp):
            sp.wait_ge(lo_ready, 1)
            sp.dma_start(w_raw[:], w_v[:, :, 0:P]).then_inc(w_loaded, 16)
            for c in range(NCHUNK):
                cut = slice(NW * c, NW * c + NW)
                for w, part in enumerate((m_hi, m_lo)):
                    sp.dma_start(part[:, :, cut].bitcast(F32), d["mix"][w, :, :, cut].rearrange("k p n -> p k n")).then_inc(mix_in[c], 16)

            def tile(m, u, i):
                col = sp.snap(m * P) if not isinstance(m, int) else m * P
                if not (isinstance(m, int) and m == MT - 1):
                    after = sp.snap(m * P + P) if not isinstance(m, int) else m * P + P
                    sp.wait_ge(lo_ready, m + 2)
                    sp.sem_inc(free_seen, 1)
                    sp.dma_start(w_raw[:], w_v[:, :, bass.ds(after, P)]).then_inc(w_loaded, 16)
                sp.wait_ge(added, 3 * m + 3)
                sp.sem_inc(free_seen, 1)
                sp.dma_start(xb[:, u, 0:PROMPT_TILES], x_v[:, :, bass.ds(col, P)]).then_inc(x_in[u], 16)
                sp.dma_start(xb[0:DEC, u, LASTT], a["x_sample"][0, :, bass.ds(col, P)]).then_inc(xs_in[u], 16)

            with sp.Fori(0, MT // 2 - 1) as i:
                for u in range(2):
                    tile(sp.snap(2 * i + u), u, i)
            for u in range(2):
                tile(MT - 2 + u, u, MT // 2 - 1)

        @block.scalar
        def _(act):
            act.sem_inc(squared, 1)
            for u in range(2):
                act.sem_inc(y_out[u], 16)
                act.sem_inc(ys_out[u], 16)
            act.sem_inc(yT_ready, 6)

            def split(m, u):
                act.wait_ge(w_loaded, 16 * m + 16)
                act.wait_ge(chunk_done, NCHUNK * m + NCHUNK)
                act.copy(w_hi[:, u], w_raw[:]).then_inc(hi_ready, 1)

            def copies(m, u):
                for c in range(NCHUNK):
                    act.wait_ge(chunk_done, NCHUNK * m + (2 * NCHUNK + c + 1))
                    if c == 0:
                        act.wait_ge(turned, 3 * m + 3)
                    act.copy(yT[:, NW * c:NW * c + NW], acc[u][c][:, 0:NW]).then_inc(yT_ready, 1)

            def send(m, u):
                col = act.snap(m * P) if not isinstance(m, int) else m * P
                act.wait_ge(added, 3 * m + 9)
                act.wait_ge(summed, 2 * m + 2)
                act.activation(sq[:, 0:PROMPT_TILES], yb[:, u, 0:PROMPT_TILES], ACT.Square)
                act.activation(sq[0:DEC, LASTT], yb[0:DEC, u, LASTT], ACT.Square).then_inc(squared, 1)
                act.dma_start(y_v[:, :, bass.ds(col, P)], yb[:, u, 0:PROMPT_TILES]).then_inc(y_out[u], 16)
                act.dma_start(d["y"][SEQ:T, bass.ds(col, P)], yb[0:DEC, u, LASTT]).then_inc(ys_out[u], 16)

            split(0, 0)
            split(1, 1)
            copies(0, 0)
            with act.Fori(0, MT // 2 - 1) as i:
                for u in range(2):
                    m = act.snap(2 * i + (u + 1))
                    split(m + 1, u)
                    copies(m, 1 - u)
                    send(act.snap(m - 1), u)
            copies(MT - 1, 1)
            send(MT - 2, 0)
            send(MT - 1, 1)
            for u in range(2):
                act.wait_ge(y_out[u], 16 + 8 * MT)
                act.wait_ge(ys_out[u], 16 + 8 * MT)

        @block.vector
        def _(dve):
            dve.sem_inc(lo_ready, 1)
            dve.sem_inc(added, 6)
            dve.sem_inc(summed, 2)

            def split(m, u):
                dve.wait_ge(hi_ready, m + 1)
                dve.tensor_tensor(w_lo[:, u], w_raw[:], w_hi[:, u].bitcast(F32), ALU.subtract).then_inc(lo_ready, 1)

            def add(m, u, i):
                dve.wait_ge(x_in[u], 16 * i + 16)
                dve.wait_ge(xs_in[u], 16 * i + 16)
                dve.wait_ge(y_out[u], 16 * i + 16)
                dve.wait_ge(ys_out[u], 16 * i + 16)
                for g, (t0, t1) in enumerate(GROUPS):
                    dve.wait_ge(turned, 3 * m + (g + 4))
                    rows = DEC if g == 2 else P
                    dve.tensor_tensor(yb[0:rows, u, t0:t1], back[g % 2][0:rows, 0:P * (t1 - t0)].rearrange("p (t n) -> p t n", n=P),
                                      xb[0:rows, u, t0:t1], ALU.add).then_inc(added, 1)
                dve.wait_ge(squared, m + 2)
                mm = bass.ds(m, 1)
                dve.tensor_reduce(ssq[:, 0:PROMPT_TILES, mm].rearrange("p t m -> p (t m)"), sq[:, 0:PROMPT_TILES], AX.X, ALU.add).then_inc(summed, 1)
                dve.tensor_reduce(ssq[0:DEC, LASTT, mm], sq[0:DEC, LASTT], AX.X, ALU.add).then_inc(summed, 1)

            split(0, 0)
            split(1, 1)
            with dve.Fori(0, MT // 2 - 1) as i:
                for u in range(2):
                    m = dve.snap(2 * i + u)
                    split(m + 2, u)
                    add(m, u, i)
            add(MT - 2, 0, MT // 2 - 1)
            add(MT - 1, 1, MT // 2 - 1)

        @block.tensor
        def _(pe):
            pe.sem_inc(chunk_done, 2 * NCHUNK)
            pe.sem_inc(turned, 3)

            def turn_back(m):
                for g, (t0, t1) in enumerate(GROUPS):
                    if g == 0:
                        pe.wait_ge(yT_ready, NCHUNK * m + (6 + NCHUNK))
                    pe.wait_ge(added, 3 * m + (6 if g < 2 else 7))
                    for j, t in enumerate(range(t0, t1)):
                        n = DEC if t == LASTT else P
                        last = pe.transpose(back[g % 2][0:n, P * j:P * j + P], yT[:, P * t:P * t + n], ident[:])
                    last.then_inc(turned, 1)

            def products(m, u, i):
                pe.wait_ge(lo_ready, m + 2)
                pe.wait_ge(yT_ready, NCHUNK * m + NCHUNK)
                for c in range(NCHUNK):
                    cut = slice(NW * c, NW * c + NW)
                    for k in range(KT):
                        if isinstance(m, int) and m == 0 and k == 0:
                            pe.wait_ge(mix_in[c], 32)
                        for x, (w, h) in enumerate(((w_hi, m_hi), (w_hi, m_lo), (w_lo, m_hi))):
                            last = pe.matmul(acc[u][c][:, 0:NW], w[:, u, k], h[:, k, cut],
                                             start=(k == 0 and x == 0), stop=(k == KT - 1 and x == 2))
                    last.then_inc(chunk_done, 1)

            products(0, 0, 0)
            with pe.Fori(0, MT // 2 - 1) as i:
                for u in range(2):
                    products(2 * i + (u + 1), 1 - u, i)
                    turn_back(2 * i + u)
            products(MT - 1, 1, 0)
            turn_back(MT - 2)
            turn_back(MT - 1)


def finish(nc, a, d, ssq, out):
    with ExitStack() as ctx:
        s = Space(nc, ctx, "fin")
        y = s.sb("y", [P, TOKEN_TILES, D_MODEL])
        gain = s.sb("gain", [P, D_MODEL])
        mean, rstd, mhalf = (s.sb(n, [P, TOKEN_TILES]) for n in ("mean", "rstd", "mhalf"))
        y_in = [s.sem(f"y_in{t}") for t in range(TOKEN_TILES)]
        gain_in, ready, pooled, normed, stored = (s.sem(n) for n in ("gain_in", "ready", "pooled", "normed", "stored"))
        block = ctx.enter_context(nc.Block())
        rows = [P] * PROMPT_TILES + [DEC]

        @block.sync
        def _(sp):
            for t, n in enumerate(rows):
                sp.dma_start(y[0:n, t], d["y"][P * t:P * t + n]).then_inc(y_in[t], 16)

        @block.scalar
        def _(act):
            act.dma_start(gain[:], a["ln_final_w"].rearrange("(o n) -> o n", o=1).to_broadcast([P, D_MODEL])).then_inc(gain_in, 16)
            for t, n in enumerate(rows):
                act.wait_ge(normed, t + 1)
                dst = out["y_prompt"][0, P * t:P * t + P] if t < PROMPT_TILES else out["y_sample"][0]
                act.dma_start(dst, y[0:n, t]).then_inc(stored, 16)
            act.wait_ge(stored, 16 * TOKEN_TILES)

        @block.gpsimd
        def _(pool):
            pool.memset(mhalf[:], -0.5).then_inc(pooled, 1)
            pool.wait_ge(pooled, 1)
            pool.wait_ge(ready, 4)
            pool.tensor_tensor(rstd[:], mean[:], mhalf[:], ALU.pow).then_inc(pooled, 1)

        @block.vector
        def _(dve):
            dve.memset(mean[:], 1.0).then_inc(ready, 1)
            dve.wait_ge(ready, 1)
            dve.tensor_reduce(mean[:, 0:PROMPT_TILES], ssq[:, 0:PROMPT_TILES], AX.X, ALU.add).then_inc(ready, 1)
            dve.tensor_reduce(mean[0:DEC, PROMPT_TILES:], ssq[0:DEC, PROMPT_TILES:], AX.X, ALU.add).then_inc(ready, 1)
            dve.wait_ge(ready, 3)
            dve.tensor_scalar(mean[:], mean[:], 1.0 / D_MODEL, EPS, ALU.mult, ALU.add).then_inc(ready, 1)
            dve.wait_ge(pooled, 2)
            dve.wait_ge(gain_in, 16)
            for t, n in enumerate(rows):
                dve.wait_ge(y_in[t], 16)
                dve.scalar_tensor_tensor(y[0:n, t], y[0:n, t], rstd[0:n, t:t + 1], gain[0:n], ALU.mult, ALU.mult).then_inc(normed, 1)


def mix_and_finish(nc, a, d, ident, out):
    with ExitStack() as ctx:
        s = Space(nc, ctx, "outp")
        ssq = s.sb("ssq", [P, TOKEN_TILES, D_MODEL // P])
        with ExitStack() as inner:
            w = Space(nc, inner, "outw")
            w_raw = w.sb("w_raw", [P, KT, P])
            w_hi, w_lo = (w.sb(n, [P, 2, KT, P], F32R) for n in ("w_hi", "w_lo"))
            project_out(nc, a, d, ident, ssq, w_hi, w_lo, w_raw)
        finish(nc, a, d, ssq, out)


def streaming_step(nc, a, out):
    d = {"qkv": nc.dram_tensor("scratch_qkv", (QKV_TILES, P, CONV), F32).ap(),
         "gate": nc.dram_tensor("scratch_gate", (2 * HEADS, P, T), F32).ap(),
         "latent": nc.dram_tensor("scratch_latent", (2 * C_TILES, P, T), F32).ap(),
         "bakr": nc.dram_tensor("scratch_bakr", (BAKR, T), F32).ap(),
         "mix": nc.dram_tensor("scratch_mix", (2, 2 * HEADS, P, T), F32).ap(),
         "y": nc.dram_tensor("scratch_y", (T, D_MODEL), F32).ap()}
    with ExitStack() as ctx:
        s = Space(nc, ctx, "all")
        cols = s.sb("cols", [P, 2, P])
        ident = s.sb("ident", [P, P])
        with ExitStack() as inner:
            h = Space(nc, inner, "h")
            hn_hi, hn_lo = (h.sb(n, [P, KT, T], F32R) for n in ("hn_hi", "hn_lo"))
            normalise_inputs(nc, a, hn_hi, hn_lo, cols, ident)
            project(nc, a, d, hn_hi, hn_lo, cols, ident, out)
        delta_rule(nc, a, d, cols, ident, out)
        attend(nc, a, d, cols, ident, out)
        mix_and_finish(nc, a, d, ident, out)


INPUTS = ["x_prompt", "x_sample", "cache_mla_latent", "cache_mla_krope", "state_gdn_conv", "state_gdn_ssm", "ln_in_w", "w_in",
          "w_conv", "a_log", "dt_bias", "gdn_norm_w", "q_norm_w", "w_q_up", "kv_norm_w", "w_uk", "w_uv", "w_out", "ln_final_w"]
OUTPUTS = [("y_prompt", (1, SEQ, D_MODEL)), ("y_sample", (1, DEC, D_MODEL)),
           ("new_conv_prompt", (1, 1, PRE, QKV)), ("new_ssm_prompt", (1, 1, HEADS, P, P)),
           ("new_latent_prompt", (1, 1, SEQ, LORA)), ("new_krope_prompt", (1, 1, SEQ, ROPE)),
           ("new_conv_sample", (1, 1, PRE, QKV)), ("new_ssm_sample", (1, 1, HEADS, P, P)),
           ("new_latent_sample", (1, 1, DEC, LORA)), ("new_krope_sample", (1, 1, DEC, ROPE))]


def kernel(**inputs):
    import numpy as np
    import concourse.bacc as bacc
    from concourse.bass_utils import run_bass_kernel_spmd

    nc = bacc.Bacc("TRN2", target_bir_lowering=False, num_devices=1)
    arrays = {f"in_{n}": np.ascontiguousarray(inputs[n]) for n in INPUTS}
    arrays.update({f"in_{n}": v for n, v in (masks() | rotation()).items()})
    a = {n[3:]: nc.dram_tensor(n, v.shape, F32, kind="ExternalInput").ap() for n, v in arrays.items()}
    out = {n: nc.dram_tensor(f"out_{n}", shape, F32, kind="ExternalOutput").ap() for n, shape in OUTPUTS}
    streaming_step(nc, a, out)
    r = run_bass_kernel_spmd(nc, [arrays], core_ids=[0])
    return tuple(r.results[0][f"out_{n}"] for n, _ in OUTPUTS)
```
